# Optimizing a Trainium2 kernel written in Bass

```python
import math
import jax, jax.numpy as jnp
from jax import lax
import numpy as np

D_MODEL = 1024
BATCH = 1
SEQ = 256
DEPTH = 2

HEAD_DIM = 64
N_HEADS = D_MODEL // HEAD_DIM
SB_HEADS = N_HEADS // 4
DIL_HEADS = N_HEADS - SB_HEADS
DIL_PATTERNS = ((128, 1), (512, 4), (2048, 16))
DIL_GROUP_HEADS = DIL_HEADS // len(DIL_PATTERNS)
OUT_WIDTH = (SB_HEADS + DIL_GROUP_HEADS) * HEAD_DIM
BLOCK = 128
N_BUCKETS = 32
MAX_DISTANCE = 2048
D_FF = 2816
RWKV_HEAD = 64
RWKV_HEADS = D_MODEL // RWKV_HEAD
D_DECAY_LORA = 64
D_AAA_LORA = 64
D_GATE_LORA = 160
NORM_EPS = 1e-6
GN_EPS = 64e-5
NEG_INF = -1e30
N_EVEN = (DEPTH + 1) // 2
N_ODD = DEPTH // 2


def rms_norm(x, g, eps=NORM_EPS):
    x32 = x.astype(jnp.float32)
    y = x32 * lax.rsqrt(jnp.mean(x32 * x32, axis=-1, keepdims=True) + eps)
    return (y * g.astype(jnp.float32)).astype(x.dtype)

def swiglu(h, w_gate, w_up, w_down):
    return (jax.nn.silu(h @ w_gate) * (h @ w_up)) @ w_down

def t5_bucket(dist):
    max_exact = N_BUCKETS // 2
    d = jnp.maximum(dist, 1).astype(jnp.float32)
    large = max_exact + (jnp.log(d / max_exact) / math.log(MAX_DISTANCE / max_exact)
                         * (N_BUCKETS - max_exact)).astype(jnp.int32)
    large = jnp.minimum(large, N_BUCKETS - 1)
    return jnp.where(dist < max_exact, dist, large)

def stick_breaking_attention(q, k, v):
    B, S, H, Dh = q.shape
    nb = S // BLOCK
    scale = Dh ** -0.5
    qb = q.reshape(B, nb, BLOCK, H, Dh).transpose(1, 0, 3, 2, 4)
    kpos = jnp.arange(S)

    def one_block(args):
        qi, n = args
        z = jnp.einsum('bhqd,bshd->bhqs', qi, k).astype(jnp.float32) * scale
        qpos = n * BLOCK + jnp.arange(BLOCK)
        strict = kpos[None, :] < qpos[:, None]
        log_keep = jnp.where(strict, jax.nn.log_sigmoid(-z), 0.0)
        after = lax.cumsum(log_keep, axis=3, reverse=True) - log_keep
        weight = jnp.where(strict, jnp.exp(jax.nn.log_sigmoid(z) + after), 0.0)
        return jnp.einsum('bhqs,bshd->bqhd', weight.astype(v.dtype), v)

    out = lax.map(one_block, (qb, jnp.arange(nb)))
    return out.transpose(1, 0, 2, 3, 4).reshape(B, S, H, Dh)

def dilated_window_attention(q, k, v, bias_table, window, dilation):
    B, S, G, Dh = q.shape
    r = dilation
    L = S // r
    span = window // r
    nb = -(-L // BLOCK)
    Lp = nb * BLOCK

    def to_sub(t):
        t = t.reshape(B, L, r, G, Dh).transpose(0, 2, 1, 3, 4)
        t = jnp.pad(t, ((0, 0), (0, 0), (0, Lp - L), (0, 0), (0, 0)))
        return t.reshape(B, r, nb, BLOCK, G, Dh)

    def with_prev(t):
        prev = jnp.pad(t, ((0, 0), (0, 0), (1, 0), (0, 0), (0, 0), (0, 0)))[:, :, :-1]
        return jnp.concatenate([prev, t], axis=3)

    qs = to_sub(q)
    kw, vw = with_prev(to_sub(k)), with_prev(to_sub(v))
    logits = jnp.einsum('brnqgd,brnkgd->brngqk', qs, kw).astype(jnp.float32) * (Dh ** -0.5)
    qi = jnp.arange(BLOCK)[:, None]
    kj = jnp.arange(2 * BLOCK)[None, :] - BLOCK
    dist = qi - kj
    in_window = (dist >= 0) & (dist <= span)
    has_key = (jnp.arange(nb)[:, None, None] > 0) | (kj[None] >= 0)
    mask = (in_window[None] & has_key)[:, None]
    bias = bias_table[t5_bucket(jnp.maximum(dist, 0) * r)].astype(jnp.float32).transpose(2, 0, 1)
    logits = jnp.where(mask, logits + bias, NEG_INF)
    m = jnp.max(logits, axis=-1, keepdims=True)
    p = jnp.exp(logits - m)
    den = jnp.sum(p, axis=-1, keepdims=True)
    o = jnp.einsum('brngqk,brnkgd->brnqgd', (p / den).astype(v.dtype), vw)
    lse = (m + jnp.log(den))[..., 0].transpose(0, 1, 2, 4, 3)

    def from_sub(t):
        t = t.reshape((B, r, Lp) + t.shape[4:])[:, :, :L]
        return jnp.swapaxes(t, 1, 2).reshape((B, S) + t.shape[3:])

    return from_sub(o), from_sub(lse)

def parallel_attention_mixer(h, w_in, q_norm, k_norm, w_out, rel_bias):
    B, S, _ = h.shape
    proj = h @ w_in
    a_cols = 3 * SB_HEADS * HEAD_DIM
    sb = proj[..., :a_cols].reshape(B, S, 3, SB_HEADS, HEAD_DIM)
    dl = proj[..., a_cols:].reshape(B, S, 3, DIL_HEADS, HEAD_DIM)
    out_a = stick_breaking_attention(sb[:, :, 0], sb[:, :, 1], sb[:, :, 2])
    q = rms_norm(dl[:, :, 0], q_norm)
    k = rms_norm(dl[:, :, 1], k_norm)
    v = dl[:, :, 2]
    outs, lses = [], []
    for g, (window, dilation) in enumerate(DIL_PATTERNS):
        sl = slice(g * DIL_GROUP_HEADS, (g + 1) * DIL_GROUP_HEADS)
        o, l = dilated_window_attention(q[:, :, sl], k[:, :, sl], v[:, :, sl],
                                        rel_bias[:, sl], window, dilation)
        outs.append(o)
        lses.append(l)
    alpha = jax.nn.softmax(jnp.stack(lses, axis=0), axis=0)
    out_b = jnp.sum(alpha[..., None].astype(v.dtype) * jnp.stack(outs, axis=0), axis=0)
    merged = jnp.concatenate([out_a.reshape(B, S, -1), out_b.reshape(B, S, -1)], axis=-1)
    return merged @ w_out

def rwkv7_step(state, inp):
    r_t, w_t, k_t, v_t, a_t, b_t = inp
    sa = jnp.einsum('bhvk,bhk->bhv', state, a_t)
    state = (state * w_t[:, :, None, :] + sa[..., None] * b_t[:, :, None, :]
             + v_t[..., None] * k_t[:, :, None, :])
    return state, jnp.einsum('bhvk,bhk->bhv', state, r_t)

def rwkv7_time_mix(h, mix, w0, w1, w2, a0, a1, a2, g1, g2, k_k, k_a, r_k,
                   w_r, w_k, w_v, w_o, lnx_g, lnx_b):
    B, S, D = h.shape
    H, N = RWKV_HEADS, RWKV_HEAD
    f32 = jnp.float32
    xx = jnp.pad(h, ((0, 0), (1, 0), (0, 0)))[:, :-1] - h
    xr, xw, xk, xv, xa, xg = [h + xx * mix[i] for i in range(6)]
    r = (xr @ w_r).astype(f32)
    k = (xk @ w_k).astype(f32)
    v = (xv @ w_v).astype(f32)
    w_log = -jax.nn.softplus(-(w0 + jnp.tanh(xw @ w1) @ w2).astype(f32)) - 0.5
    decay = jnp.exp(-jnp.exp(w_log))
    a = jax.nn.sigmoid((a0 + (xa @ a1) @ a2).astype(f32))
    g = jax.nn.sigmoid(xg @ g1) @ g2
    heads = lambda t: t.reshape(B, S, H, N)
    kk = heads(k * k_k.astype(f32))
    kk = kk / jnp.maximum(jnp.sqrt(jnp.sum(kk * kk, axis=-1, keepdims=True)), 1e-12)
    k = k * (1.0 + (a - 1.0) * k_a.astype(f32))
    r_h, k_h, v_h, a_h, w_h = heads(r), heads(k), heads(v), heads(a), heads(decay)
    tm = lambda t: jnp.swapaxes(t, 0, 1)
    seqs = (tm(r_h), tm(w_h), tm(k_h), tm(v_h), tm(-kk), tm(kk * a_h))
    _, y = lax.scan(rwkv7_step, jnp.zeros((B, H, N, N), f32), seqs)
    y = jnp.swapaxes(y, 0, 1)
    mu = jnp.mean(y, axis=-1, keepdims=True)
    var = jnp.mean(jnp.square(y - mu), axis=-1, keepdims=True)
    y = ((y - mu) * lax.rsqrt(var + GN_EPS)).reshape(B, S, D)
    y = y * lnx_g.astype(f32) + lnx_b.astype(f32)
    y = y + (jnp.sum(r_h * k_h * r_k.astype(f32), axis=-1, keepdims=True) * v_h).reshape(B, S, D)
    return (y.astype(h.dtype) * g) @ w_o

def first_inputs(seed: int = 0) -> dict:
    key = jax.random.key(seed)
    ks = iter(jax.random.split(key, 48))
    D = D_MODEL
    nrm = lambda shape, scale: jax.random.normal(next(ks), shape, jnp.float32) * scale
    uni = lambda shape, lo, hi: jax.random.uniform(next(ks), shape, jnp.float32, lo, hi)
    return {
        "x": nrm((BATCH, SEQ, D), 1.0),
        "ffn_norm": 1.0 + nrm((DEPTH, 2, D), 0.05),
        "ffn_w_gate": nrm((DEPTH, 2, D, D_FF), D ** -0.5),
        "ffn_w_up": nrm((DEPTH, 2, D, D_FF), D ** -0.5),
        "ffn_w_down": nrm((DEPTH, 2, D_FF, D), D_FF ** -0.5),
        "mix_norm": 1.0 + nrm((DEPTH, D), 0.05),
        "rel_bias": nrm((N_BUCKETS, DIL_HEADS), 0.3),
        "attn_w_in": nrm((N_EVEN, D, 3 * N_HEADS * HEAD_DIM), D ** -0.5),
        "attn_q_norm": 1.0 + nrm((N_EVEN, HEAD_DIM), 0.05),
        "attn_k_norm": 1.0 + nrm((N_EVEN, HEAD_DIM), 0.05),
        "attn_w_out": nrm((N_EVEN, OUT_WIDTH, D), OUT_WIDTH ** -0.5),
        "rw_mix": uni((N_ODD, 6, D), 0.0, 1.0),
        "rw_w0": uni((N_ODD, D), -4.0, 0.0),
        "rw_w1": nrm((N_ODD, D, D_DECAY_LORA), D ** -0.5),
        "rw_w2": nrm((N_ODD, D_DECAY_LORA, D), 0.1 * D_DECAY_LORA ** -0.5),
        "rw_a0": nrm((N_ODD, D), 0.1),
        "rw_a1": nrm((N_ODD, D, D_AAA_LORA), D ** -0.5),
        "rw_a2": nrm((N_ODD, D_AAA_LORA, D), 0.1 * D_AAA_LORA ** -0.5),
        "rw_g1": nrm((N_ODD, D, D_GATE_LORA), D ** -0.5),
        "rw_g2": nrm((N_ODD, D_GATE_LORA, D), D_GATE_LORA ** -0.5),
        "rw_kk": 0.85 + nrm((N_ODD, D), 0.05),
        "rw_ka": 1.0 + nrm((N_ODD, D), 0.05),
        "rw_rk": nrm((N_ODD, RWKV_HEADS, RWKV_HEAD), 0.1),
        "rw_wr": nrm((N_ODD, D, D), D ** -0.5),
        "rw_wk": nrm((N_ODD, D, D), D ** -0.5),
        "rw_wv": nrm((N_ODD, D, D), D ** -0.5),
        "rw_wo": nrm((N_ODD, D, D), D ** -0.5),
        "rw_lnx_g": 1.0 + nrm((N_ODD, D), 0.05),
        "rw_lnx_b": nrm((N_ODD, D), 0.01),
    }

def first_block(x, ffn_norm, ffn_w_gate, ffn_w_up, ffn_w_down, mix_norm, rel_bias,
              attn_w_in, attn_q_norm, attn_k_norm, attn_w_out,
              rw_mix, rw_w0, rw_w1, rw_w2, rw_a0, rw_a1, rw_a2, rw_g1, rw_g2,
              rw_kk, rw_ka, rw_rk, rw_wr, rw_wk, rw_wv, rw_wo, rw_lnx_g, rw_lnx_b):
    for layer in range(DEPTH):
        x = x + 0.5 * swiglu(rms_norm(x, ffn_norm[layer, 0]), ffn_w_gate[layer, 0],
                             ffn_w_up[layer, 0], ffn_w_down[layer, 0])
        h = rms_norm(x, mix_norm[layer])
        if layer % 2 == 0:
            e = layer // 2
            x = x + parallel_attention_mixer(h, attn_w_in[e], attn_q_norm[e], attn_k_norm[e],
                                             attn_w_out[e], rel_bias)
        else:
            o = layer // 2
            x = x + rwkv7_time_mix(h, rw_mix[o], rw_w0[o], rw_w1[o], rw_w2[o], rw_a0[o],
                                   rw_a1[o], rw_a2[o], rw_g1[o], rw_g2[o], rw_kk[o], rw_ka[o],
                                   rw_rk[o], rw_wr[o], rw_wk[o], rw_wv[o], rw_wo[o],
                                   rw_lnx_g[o], rw_lnx_b[o])
        x = x + 0.5 * swiglu(rms_norm(x, ffn_norm[layer, 1]), ffn_w_gate[layer, 1],
                             ffn_w_up[layer, 1], ffn_w_down[layer, 1])
    return x


D_PLE = 256
D_POOL = 512
D_CONV = D_MODEL - D_POOL
POOL_WINDOWS = (2, 4, 8, 16)
N_POOL_GROUPS = len(POOL_WINDOWS)
POOL_GROUP_DIM = D_POOL // N_POOL_GROUPS
CONV_WIDTH = 31
D_IN_PROJ = D_POOL + 2 * D_CONV
D_FF_DENSE = 2816
N_EXPERTS = 8
TOP_K = 2
D_FF_EXPERT = 3584
N_DENSE = (DEPTH + 1) // 2
N_MOE = DEPTH // 2
DEEPNORM_ALPHA = (2.0 * DEPTH) ** 0.25
DEEPNORM_BETA = (8.0 * DEPTH) ** -0.25
LN_EPS = 1e-5


def layer_norm(x, g, b):
    xf = x.astype(jnp.float32)
    mu = jnp.mean(xf, axis=-1, keepdims=True)
    var = jnp.mean(jnp.square(xf - mu), axis=-1, keepdims=True)
    y = (xf - mu) * lax.rsqrt(var + LN_EPS)
    return (y * g.astype(jnp.float32) + b.astype(jnp.float32)).astype(x.dtype)

def causal_multiscale_pool(u):
    B, S, _ = u.shape
    uf = u.astype(jnp.float32).reshape(B, S, N_POOL_GROUPS, POOL_GROUP_DIM)
    cs = jnp.cumsum(uf, axis=1)
    pos = jnp.arange(S, dtype=jnp.float32)[None, :, None]
    outs = []
    for gi, w in enumerate(POOL_WINDOWS):
        c = cs[:, :, gi]
        prev = jnp.pad(c, ((0, 0), (w, 0), (0, 0)))[:, :S]
        count = jnp.minimum(pos + 1.0, float(w))
        outs.append((c - prev) / count - uf[:, :, gi])
    return jnp.stack(outs, axis=2).astype(u.dtype)

def pool_mixer(u, w_grp, scale):
    d = causal_multiscale_pool(u)
    y = jnp.einsum('bsgc,gcd->bsgd', d, w_grp)
    return y.reshape(u.shape) * scale

def conformer_conv(a, gate, w_dw, b_dw, g_ln, b_ln, w_pw):
    v = a * jax.nn.sigmoid(gate)
    vp = jnp.pad(v, ((0, 0), (CONV_WIDTH - 1, 0), (0, 0)))
    y = lax.conv_general_dilated(
        vp, w_dw[:, None, :].astype(v.dtype), window_strides=(1,), padding='VALID',
        dimension_numbers=('NWC', 'WIO', 'NWC'), feature_group_count=D_CONV) + b_dw
    y = jax.nn.silu(layer_norm(y, g_ln, b_ln))
    return y @ w_pw

def swiglu_2(h, w1, w3, w2):
    return (jax.nn.silu(h @ w1) * (h @ w3)) @ w2

def moe_swiglu(h, w_router, w1, w3, w2):
    B, S, D = h.shape
    t = h.reshape(B * S, D)
    logits = (t @ w_router).astype(jnp.float32)
    top_vals, top_idx = lax.top_k(logits, TOP_K)
    top_w = jax.nn.softmax(top_vals, axis=-1)
    gates = jnp.sum(jax.nn.one_hot(top_idx, N_EXPERTS, dtype=jnp.float32) * top_w[..., None],
                    axis=1).astype(h.dtype)
    out = jnp.zeros_like(t)
    for e in range(N_EXPERTS):
        out = out + gates[:, e:e + 1] * swiglu_2(t, w1[e], w3[e], w2[e])
    return out.reshape(B, S, D)

def second_inputs(seed: int = 0) -> dict:
    key = jax.random.key(seed)
    ks = iter(jax.random.split(key, 32))
    f32 = jnp.float32

    def nrm(shape, scale):
        return jax.random.normal(next(ks), shape, f32) * scale

    def gain(shape):
        return 1.0 + nrm(shape, 0.02)

    L = DEPTH
    return {
        "x": nrm((BATCH, SEQ, D_MODEL), 1.0),
        "p": nrm((DEPTH, BATCH, SEQ, D_PLE), 1.0),
        "w_in": nrm((L, D_MODEL, D_IN_PROJ), D_MODEL ** -0.5),
        "pool_w": nrm((L, N_POOL_GROUPS, POOL_GROUP_DIM, POOL_GROUP_DIM), POOL_GROUP_DIM ** -0.5),
        "pool_scale": gain((L, D_POOL)),
        "conv_w": nrm((L, CONV_WIDTH, D_CONV), CONV_WIDTH ** -0.5),
        "conv_b": nrm((L, D_CONV), 0.02),
        "conv_ln_g": gain((L, D_CONV)),
        "conv_ln_b": nrm((L, D_CONV), 0.02),
        "conv_pw": nrm((L, D_CONV, D_CONV), D_CONV ** -0.5),
        "w_out": nrm((L, D_MODEL, D_MODEL), DEEPNORM_BETA * D_MODEL ** -0.5),
        "ln1_g": gain((L, D_MODEL)),
        "ln1_b": nrm((L, D_MODEL), 0.02),
        "dense_w1": nrm((N_DENSE, D_MODEL, D_FF_DENSE), D_MODEL ** -0.5),
        "dense_w3": nrm((N_DENSE, D_MODEL, D_FF_DENSE), D_MODEL ** -0.5),
        "dense_w2": nrm((N_DENSE, D_FF_DENSE, D_MODEL), DEEPNORM_BETA * D_FF_DENSE ** -0.5),
        "router_w": nrm((N_MOE, D_MODEL, N_EXPERTS), D_MODEL ** -0.5),
        "exp_w1": nrm((N_MOE, N_EXPERTS, D_MODEL, D_FF_EXPERT), D_MODEL ** -0.5),
        "exp_w3": nrm((N_MOE, N_EXPERTS, D_MODEL, D_FF_EXPERT), D_MODEL ** -0.5),
        "exp_w2": nrm((N_MOE, N_EXPERTS, D_FF_EXPERT, D_MODEL), DEEPNORM_BETA * D_FF_EXPERT ** -0.5),
        "ln2_g": gain((L, D_MODEL)),
        "ln2_b": nrm((L, D_MODEL), 0.02),
        "ple_gate_w": nrm((L, D_MODEL, D_MODEL), D_MODEL ** -0.5),
        "ple_w": nrm((L, D_PLE, D_MODEL), DEEPNORM_BETA * D_PLE ** -0.5),
    }

def second_block(x, p, w_in, pool_w, pool_scale, conv_w, conv_b, conv_ln_g, conv_ln_b, conv_pw,
              w_out, ln1_g, ln1_b, dense_w1, dense_w3, dense_w2, router_w, exp_w1, exp_w3,
              exp_w2, ln2_g, ln2_b, ple_gate_w, ple_w):
    for i in range(DEPTH):
        u = x @ w_in[i]
        u_pool = u[..., :D_POOL]
        u_val = u[..., D_POOL:D_POOL + D_CONV]
        u_gate = u[..., D_POOL + D_CONV:]
        y_pool = pool_mixer(u_pool, pool_w[i], pool_scale[i])
        y_conv = conformer_conv(u_val, u_gate, conv_w[i], conv_b[i],
                                conv_ln_g[i], conv_ln_b[i], conv_pw[i])
        mix = jnp.concatenate([y_pool, y_conv], axis=-1) @ w_out[i]
        x = layer_norm(DEEPNORM_ALPHA * x + mix, ln1_g[i], ln1_b[i])
        j = i // 2
        if i % 2 == 0:
            f = swiglu_2(x, dense_w1[j], dense_w3[j], dense_w2[j])
        else:
            f = moe_swiglu(x, router_w[j], exp_w1[j], exp_w3[j], exp_w2[j])
        x = layer_norm(DEEPNORM_ALPHA * x + f, ln2_g[i], ln2_b[i])
        x = x + jax.nn.sigmoid(x @ ple_gate_w[i]) * (p[i] @ ple_w[i])
    return x


def setup_inputs(seed=0):
    out = dict(first_inputs(seed))
    for name, value in second_inputs(seed + 1).items():
        if name != "x":
            out[name + "_2"] = value
    return out


def reference(
    x, ffn_norm, ffn_w_gate, ffn_w_up, ffn_w_down, mix_norm, rel_bias, attn_w_in, attn_q_norm,
    attn_k_norm, attn_w_out, rw_mix, rw_w0, rw_w1, rw_w2, rw_a0, rw_a1, rw_a2, rw_g1, rw_g2,
    rw_kk, rw_ka, rw_rk, rw_wr, rw_wk, rw_wv, rw_wo, rw_lnx_g, rw_lnx_b, p_2, w_in_2, pool_w_2,
    pool_scale_2, conv_w_2, conv_b_2, conv_ln_g_2, conv_ln_b_2, conv_pw_2, w_out_2, ln1_g_2,
    ln1_b_2, dense_w1_2, dense_w3_2, dense_w2_2, router_w_2, exp_w1_2, exp_w3_2, exp_w2_2,
    ln2_g_2, ln2_b_2, ple_gate_w_2, ple_w_2,
):
    x = first_block(
        x, ffn_norm, ffn_w_gate, ffn_w_up, ffn_w_down, mix_norm, rel_bias, attn_w_in,
        attn_q_norm, attn_k_norm, attn_w_out, rw_mix, rw_w0, rw_w1, rw_w2, rw_a0, rw_a1, rw_a2,
        rw_g1, rw_g2, rw_kk, rw_ka, rw_rk, rw_wr, rw_wk, rw_wv, rw_wo, rw_lnx_g, rw_lnx_b,
    )
    return second_block(
        x, p_2, w_in_2, pool_w_2, pool_scale_2, conv_w_2, conv_b_2, conv_ln_g_2, conv_ln_b_2,
        conv_pw_2, w_out_2, ln1_g_2, ln1_b_2, dense_w1_2, dense_w3_2, dense_w2_2, router_w_2,
        exp_w1_2, exp_w3_2, exp_w2_2, ln2_g_2, ln2_b_2, ple_gate_w_2, ple_w_2,
    )


_drawn_inputs = setup_inputs


def setup_inputs(seed=0):
    import zlib

    import numpy as np

    out = dict(_drawn_inputs(seed))
    spreads = {}
    factors = {'attn_q_norm': 7.901,
     'attn_k_norm': 7.716,
     'rw_w1': 8.0,
     'rw_w2': 8.0,
     'rw_a2': 2.903,
     'rw_kk': 80.579,
     'rw_lnx_b': 8.0,
     'pool_scale_2': 23.347,
     'conv_b_2': 6.582,
     'conv_ln_g_2': 27.573,
     'conv_ln_b_2': 29.994}
    for name, (base, spread) in spreads.items():
        noise = np.random.default_rng([zlib.crc32(name.encode()), seed]).standard_normal(out[name].shape)
        drawn = base * np.exp(spread * noise) if base else spread * noise
        out[name] = __import__('jax').numpy.asarray(drawn.astype(out[name].dtype))
    for name, factor in factors.items():
        out[name] = (out[name] * factor).astype(out[name].dtype)
    return out
```

```python
from contextlib import ExitStack

import numpy as np

import concourse.bass as bass
from concourse import mybir

F32 = mybir.dt.float32
ALU = mybir.AluOpType
ACT = mybir.ActivationFunctionType
AX_X = mybir.AxisListType.X

P = 128
D = 1024
T = 256
KT = D // P
TT = T // P
D_FF = 2816
D_FF_EXPERT = 3584
N_EXPERTS = 8
CHUNK = 256
UNIT = KT * CHUNK
HEAD = 64
SB_HEADS = 4
DIL_HEADS = 12
DIL_PATTERNS = ((128, 1), (512, 4), (2048, 16))
N_GROUPS = len(DIL_PATTERNS)
GROUP_HEADS = DIL_HEADS // N_GROUPS
N_BUCKETS = 32
MAX_DISTANCE = 2048
NEG_INF = -1e30
SCALE = HEAD ** -0.5
RW_CHUNK = 64
DECAY_SCALE = -float(np.exp(-0.5))
CONV_WIDTH = 31
PAD_CONV = CONV_WIDTH - 1
POOL_WINDOWS = (2, 4, 8, 16)
PAD_POOL = 16
ALPHA = 4.0 ** 0.25
RING = 8
LEVELS = (2, 4, 8, 16, 32)

PARAMS = [
    ("ffn_norm", 4 * KT), ("mix_norm", 2 * KT), ("rw_mix", 6 * KT), ("rw_w0", KT), ("rw_a0", KT),
    ("rw_kk", KT), ("rw_ka", KT), ("rw_rk", KT), ("rw_lnx_g", KT), ("rw_lnx_b", KT),
    ("attn_q_norm", 1), ("attn_k_norm", 1), ("pool_scale_2", 8), ("conv_w_2", 2 * CONV_WIDTH * 4),
    ("conv_b_2", 8), ("conv_ln_g_2", 8), ("conv_ln_b_2", 8), ("ln1_g_2", 16), ("ln1_b_2", 16),
    ("ln2_g_2", 16), ("ln2_b_2", 16), ("router_w_2", KT * N_EXPERTS),
]
PARAM_AT = {}
N_PARAM = 0
for _name, _n in PARAMS:
    PARAM_AT[_name] = N_PARAM
    N_PARAM += _n

CONSTS = [
    ("ident", P), ("ones", P), ("head_ones", P), ("later", P), ("eps_rms", 1), ("eps_gn", 1),
    ("eps_ln", 1), ("one", 1), ("iota", N_EXPERTS), ("restart", T),
]
CONST_AT = {}
N_CONST = 0
for _name, _n in CONSTS:
    CONST_AT[_name] = N_CONST
    N_CONST += _n
N_LOGIT = P + 2 * P


def constant_arrays():
    row, col = np.arange(P)[:, None], np.arange(P)[None, :]
    c = np.zeros((P, N_CONST), np.float32)

    def put(name, value):
        at = CONST_AT[name]
        n = dict(CONSTS)[name]
        c[:, at:at + n] = value

    put("ident", row == col)
    put("ones", 1.0)
    put("head_ones", row // HEAD == col // HEAD)
    put("later", row > col)
    put("eps_rms", 1e-6)
    put("eps_gn", 64e-5)
    put("eps_ln", 1e-5)
    put("one", 1.0)
    put("iota", np.arange(N_EXPERTS)[None, :])
    put("restart", (np.arange(T)[None, :] % RW_CHUNK) != 0)

    before = (row < col).astype(np.float32)
    stick = np.concatenate([before, np.ones((P, P), np.float32), before], axis=1)

    dil = []
    for tile in range(TT):
        keys = np.arange(P * (tile + 1))[None, :]
        dist = tile * P + row - keys
        for window, r in DIL_PATTERNS:
            ok = (dist >= 0) & (dist <= window) & (dist % r == 0)
            dil.append(np.where(ok, 0.0, NEG_INF).astype(np.float32))
    dil = np.concatenate(dil, axis=1)

    same = row // RW_CHUNK == col // RW_CHUNK
    strict = (same & (row < col)).astype(np.float32)
    upto = (same & (row <= col)).astype(np.float32)
    rw = [strict, upto, strict, upto]
    for b in (1,) + LEVELS:
        rw.append(((row // (2 * b) == col // (2 * b)) & (row % (2 * b) < b) & (col % (2 * b) >= b)).astype(np.float32))
    rw.append(rw[4].T)
    rw = np.concatenate(rw, axis=1)

    t = np.arange(T)
    count = np.stack([1.0 / np.minimum(t + 1.0, w) for w in POOL_WINDOWS]).astype(np.float32)
    count = np.broadcast_to(count.reshape(1, -1), (P, 4 * T))
    pick = np.zeros((N_EXPERTS, N_EXPERTS, P), np.float32)
    pick[np.arange(N_EXPERTS), np.arange(N_EXPERTS), :] = 1.0
    return {"consts": c, "stick_mask": stick, "dilated_mask": dil, "rwkv_masks": rw,
            "inverse_count": np.ascontiguousarray(count), "expert_rows": pick.reshape(N_EXPERTS, -1)}


def bucket_of_distance():
    d = np.arange(T)
    large = 16 + (np.log(np.maximum(d, 1) / 16.0) / np.log(MAX_DISTANCE / 16.0) * 16).astype(np.int64)
    return np.where(d < 16, d, np.minimum(large, N_BUCKETS - 1))


class Engine:

    def __init__(self, handle, semaphore):
        self.handle, self.semaphore, self.count, self.waited = handle, semaphore, 0, {}

    def wait(self, *tokens):
        for token in tokens:
            if token is None:
                continue
            semaphore, value = token
            if self.waited.get(id(semaphore), 0) < value:
                self.waited[id(semaphore)] = value
                self.handle.wait_ge(semaphore, value)

    def counts(self, instruction):
        instruction.then_inc(self.semaphore, 1)
        self.count += 1
        return self.semaphore, self.count

    def now(self):
        return (self.semaphore, self.count) if self.count else None


def bass_macaron_attention_rwkv_conv_moe_kernel(nc, dram, out):
    with ExitStack() as ctx:
        def sb(name, cols):
            return ctx.enter_context(nc.sbuf_tensor(name, [P, cols], F32))

        def sem(name):
            return ctx.enter_context(nc.semaphore(name))

        ring = sb("weight_ring", RING * UNIT)
        x = sb("x_T", KT * T)
        xn = sb("normed_T", KT * T)
        sq = sb("squares", KT * T)
        arena = sb("arena", 12 * KT * T)
        param = sb("params", N_PARAM)
        const = sb("consts", N_CONST)
        h_buf = sb("hidden", 4 * T)
        act_buf = sb("activated", 4 * T)
        std = sb("std", T)
        rstd = sb("rstd", T)
        mean = sb("mean", T)
        bank = [ctx.enter_context(nc.psum_tensor(f"bank{i}", [P, 512], F32)) for i in range(8)]

        pe = Engine(nc.tensor, sem("pe_done"))
        dve = Engine(nc.vector, sem("dve_done"))
        act = Engine(nc.scalar, sem("act_done"))
        pool = Engine(nc.gpsimd, sem("pool_done"))
        sp = Engine(nc.sync, sem("sp_done"))
        slot_landed = [sem(f"slot_landed{i}") for i in range(RING)]
        small_landed = sem("small_landed")
        out_written = sem("out_written")
        small_count = [0]

        def load_small(engine, dst, src):
            engine.handle.dma_start(dst, src).then_inc(small_landed, 16)
            small_count[0] += 16
            return small_landed, small_count[0]

        units = []

        def take(name, i=0, rows=P, cols=UNIT):
            n = len(units)
            units.append([dram[name][i, 0:rows, 0:cols], rows, cols, None])
            pe.wait((slot_landed[n % RING], 16 * (n // RING + 1)))
            at = (n % RING) * UNIT
            return n, ring[0:rows, at:at + cols]

        def give_back(n, token):
            units[n][3] = token

        def col(name, i=0, rows=P):
            return param[0:rows, PARAM_AT[name] + i:PARAM_AT[name] + i + 1]

        def con(name):
            at = CONST_AT[name]
            return const[:, at:at + dict(CONSTS)[name]]

        ident, ones, head_ones, later = con("ident"), con("ones"), con("head_ones"), con("later")

        def blk(tile, k, w=T):
            return tile[:, k * w:(k + 1) * w]

        free = [None] * 8
        turn = [0]

        def next_bank():
            turn[0] += 1
            i = 4 + turn[0] % 4
            pe.wait(free[i])
            return i

        def mm(dst, lhsT, rhs, start, stop, shared=False):
            return nc.tensor.matmul(dst, lhsT, rhs, start=start, stop=stop, skip_group_check=shared)

        params_in = load_small(act, param[:, :], dram["params"])
        consts_in = load_small(act, const[:, :], dram["consts"])
        x_in = load_small(act, x[:, :], dram["x"])
        small_in = x_in
        for e in (pe, dve, act, pool):
            e.wait(small_in)

        state = {"xn_read": None, "sq_read": None}

        def feature_mean(source_tokens, source, n_k, matrix, square):
            b = next_bank()
            for k in range(n_k):
                if square:
                    act.wait(source_tokens[k], state["sq_read"])
                    token = act.counts(nc.scalar.activation(blk(sq, k), blk(source, k), ACT.Square))
                    pe.wait(token)
                    piece = blk(sq, k)
                else:
                    pe.wait(source_tokens[k])
                    piece = blk(source, k)
                ins = mm(bank[b][:, 0:T], matrix, piece, k == 0, k == n_k - 1)
            done = pe.counts(ins)
            if square:
                state["sq_read"] = done
            return b, done

        def reciprocal_std(b, done, n, eps):
            act.wait(done, dve.now())
            t = act.counts(nc.scalar.activation(std[:, :], bank[b][:, 0:T], ACT.Sqrt, bias=con(eps), scale=1.0 / n))
            free[b] = t
            dve.wait(t)
            return dve.counts(nc.vector.reciprocal(rstd[:, :], std[:, :]))

        def rms_norm(x_tokens, gain, first):
            b, done = feature_mean(x_tokens, x, KT, ones, True)
            r = reciprocal_std(b, done, D, "eps_rms")
            dve.wait(r, state["xn_read"])
            return [dve.counts(nc.vector.scalar_tensor_tensor(
                blk(xn, k), blk(x, k), col(gain, first + k), rstd[:, :], ALU.mult, ALU.mult))
                for k in range(KT)]

        def layer_norm(z, z_tokens, n_k, write):
            b, done = feature_mean(z_tokens, z, n_k, ones, False)
            act.wait(done, dve.now())
            t = act.counts(nc.scalar.mul(mean[:, :], bank[b][:, 0:T], 1.0 / (n_k * P)))
            free[b] = t
            dve.wait(t)
            centred = [dve.counts(nc.vector.tensor_tensor(blk(z, k), blk(z, k), mean[:, :], ALU.subtract))
                       for k in range(n_k)]
            b, done = feature_mean(centred, z, n_k, ones, True)
            r = reciprocal_std(b, done, n_k * P, "eps_ln")
            dve.wait(r)
            return [write(k) for k in range(n_k)]

        def down(n, w, i_h, h_tokens, c_first, c_last):
            done = [None] * 4
            for c in range(KT):
                for b in range(2):
                    pe.wait(h_tokens[b])
                    if c_first and b == 0 and c % 2 == 0:
                        pe.wait(free[c // 2])
                    start = c_first and b == 0 and c % 2 == 0
                    ins = mm(bank[c // 2][:, (c % 2) * T:(c % 2 + 1) * T],
                             w[:, b * D + c * P:b * D + (c + 1) * P], blk(h_buf, 2 * i_h + b),
                             start, c_last and b == 1, True)
                if c == KT - 1 or (c_last and c % 2):
                    done[c // 2] = pe.counts(ins)
            give_back(n, done[3])
            return done

        h_read = [None, None]

        def gated_ffn(src, src_tokens, names, first_unit, n_chunks, scale=None, begin=True, end=True):
            gate_name, up_name, down_name = names
            waiting = None
            done = None
            for i in range(n_chunks):
                half = i % 2
                bs = [4 + 2 * half, 5 + 2 * half]
                for part, name in ((0, gate_name), (1, up_name)):
                    n, w = take(name, first_unit + i)
                    for b in range(2):
                        if part == 0:
                            pe.wait(free[bs[b]])
                        for k in range(KT):
                            pe.wait(src_tokens[k])
                            ins = mm(bank[bs[b]][:, part * T:(part + 1) * T],
                                     w[:, k * CHUNK + b * P:k * CHUNK + (b + 1) * P], blk(src, k),
                                     k == 0, k == KT - 1)
                        if part == 1:
                            token = pe.counts(ins)
                            if b == 0:
                                first_done = token
                            else:
                                both_done = (first_done, token)
                    give_back(n, None)
                    last_n = n
                    if part == 0:
                        gate_n = n
                give_back(gate_n, both_done[1])
                give_back(last_n, both_done[1])
                h_tokens = []
                for b in range(2):
                    j = 2 * half + b
                    act.wait(both_done[b], dve_read_act[j])
                    t = act.counts(nc.scalar.activation(blk(act_buf, j), bank[bs[b]][:, 0:T], ACT.Silu))
                    dve.wait(t, h_read[half])
                    t = dve.counts(nc.vector.tensor_tensor(blk(h_buf, j), blk(act_buf, j),
                                                           bank[bs[b]][:, T:2 * T], ALU.mult))
                    dve_read_act[j] = t
                    free[bs[b]] = t
                    if scale is not None:
                        dve.wait(t)
                        t = dve.counts(nc.vector.tensor_tensor(blk(h_buf, j), blk(h_buf, j), scale, ALU.mult))
                    h_tokens.append(t)
                if waiting is not None:
                    n, w = take(down_name, first_unit + i - 1)
                    done = down(n, w, (i - 1) % 2, waiting, begin and i == 1, False)
                    h_read[(i - 1) % 2] = done[3]
                waiting = h_tokens
            n, w = take(down_name, first_unit + n_chunks - 1)
            done = down(n, w, (n_chunks - 1) % 2, waiting, begin and n_chunks == 1, end)
            h_read[(n_chunks - 1) % 2] = done[3]
            return done

        dve_read_act = [None] * 4

        def add_residual(done, scale, base=None, dst=None):
            tokens = []
            for c in range(KT):
                dve.wait(done[c // 2])
                t = dve.counts(nc.vector.scalar_tensor_tensor(
                    blk(x, c), bank[c // 2][:, (c % 2) * T:(c % 2 + 1) * T], scale, blk(x, c),
                    ALU.mult, ALU.add))
                free[c // 2] = t
                tokens.append(t)
            return tokens

        def project_T(name, i, src, src_tokens, n_blocks=2):
            n, w = take(name, i)
            b = next_bank()
            for j in range(n_blocks):
                for k in range(KT):
                    pe.wait(src_tokens[k])
                    ins = mm(bank[b][:, j * T:(j + 1) * T], w[:, k * CHUNK + j * P:k * CHUNK + (j + 1) * P],
                             blk(src, k), k == 0, k == KT - 1)
            done = pe.counts(ins)
            give_back(n, done)
            return b, done

        def attention(src_tokens, x_tokens):
            A = KT * T
            Q, K, V = arena[:, 0:A], arena[:, A:2 * A], arena[:, 2 * A:3 * A]
            bias = arena[:, 3 * A:3 * A + GROUP_HEADS * N_GROUPS * N_LOGIT]
            at = 3 * A + GROUP_HEADS * N_GROUPS * N_LOGIT
            dmask = arena[:, at:at + N_GROUPS * N_LOGIT]
            at += N_GROUPS * N_LOGIT
            smask = arena[:, at:at + N_LOGIT]
            at += N_LOGIT
            merged = arena[:, at:at + 4 * T]
            at += 4 * T
            work = arena[:, at:12 * A]
            act.wait(pe.now(), dve.now(), pool.now())
            bias_in = load_small(act, bias, dram["rel_bias"])
            dmask_in = load_small(act, dmask, dram["dilated_mask"])
            smask_in = load_small(act, smask, dram["stick_mask"])
            pool.wait(smask_in)
            for j in range(GROUP_HEADS):
                w3 = N_GROUPS * N_LOGIT
                bias_ready = pool.counts(nc.gpsimd.tensor_tensor(
                    bias[:, j * w3:(j + 1) * w3], bias[:, j * w3:(j + 1) * w3], dmask, ALU.add))
            ready = {}

            def to_sbuf(tile, block, b, done):
                act.wait(done)
                t = act.counts(nc.scalar.copy(tile[:, block * T:(block + 2) * T], bank[b][:, :]))
                free[b] = t
                return t

            def v_unit(i, block):
                n, w = take("attn_w_in", i)
                b = next_bank()
                for tt in range(TT):
                    for k in range(KT):
                        pe.wait(src_tokens[k])
                        ins = mm(bank[b][:, tt * T:(tt + 1) * T], xn[:, k * T + tt * P:k * T + (tt + 1) * P],
                                 w[:, k * CHUNK:(k + 1) * CHUNK], k == 0, k == KT - 1)
                done = pe.counts(ins)
                give_back(n, done)
                act.wait(done)
                for tt in range(TT):
                    t = act.counts(nc.scalar.copy(V[:, tt * D + block * T:tt * D + (block + 1) * T],
                                                  bank[b][:, tt * T:(tt + 1) * T]))
                free[b] = t
                state["xn_read"] = done
                return t

            norm_at = [0]

            def head_norm(tile, block, token, gain):
                i = norm_at[0] % 2
                norm_at[0] += 1
                s_b, s_s = work[:, i * T:(i + 1) * T], work[:, (2 + i) * T:(3 + i) * T]
                s_r = work[:, (4 + i) * T:(5 + i) * T]
                dve.wait(token, norm_read[i])
                piece = blk(tile, block)
                t = dve.counts(nc.vector.tensor_tensor(s_b, piece, piece, ALU.mult))
                b = next_bank()
                pe.wait(t)
                done = pe.counts(mm(bank[b][:, 0:T], head_ones, s_b, True, True))
                norm_read[i] = done
                act.wait(done, dve.now())
                t = act.counts(nc.scalar.activation(s_s, bank[b][:, 0:T], ACT.Sqrt, bias=con("eps_rms"),
                                                    scale=1.0 / HEAD))
                free[b] = t
                dve.wait(t)
                t = dve.counts(nc.vector.reciprocal(s_r, s_s))
                dve.wait(t)
                return dve.counts(nc.vector.scalar_tensor_tensor(piece, piece, col(gain), s_r,
                                                                 ALU.mult, ALU.mult))

            norm_read = [None, None]
            b, done = project_T("attn_w_in", 0, xn, src_tokens)
            sq_ready = to_sbuf(Q, 0, b, done)
            b, done = project_T("attn_w_in", 1, xn, src_tokens)
            sk_ready = to_sbuf(K, 0, b, done)
            sv_ready = v_unit(2, 0)
            raw = {}
            for i in range(3):
                b, done = project_T("attn_w_in", 3 + i, xn, src_tokens)
                raw["q", i] = to_sbuf(Q, 2 + 2 * i, b, done)
            for i in range(3):
                b, done = project_T("attn_w_in", 6 + i, xn, src_tokens)
                raw["k", i] = to_sbuf(K, 2 + 2 * i, b, done)
                for j in range(2):
                    ready["q", 2 * i + j] = head_norm(Q, 2 + 2 * i + j, raw["q", i], "attn_q_norm")
            for i in range(3):
                dv_ready = v_unit(9 + i, 1 + i)
                for j in range(2):
                    ready["k", 2 * i + j] = head_norm(K, 2 + 2 * i + j, raw["k", i], "attn_k_norm")

            LW = N_LOGIT
            sw = [work[:, 6 * T + i * 4 * LW:6 * T + (i + 1) * 4 * LW] for i in range(2)]
            sw_read = [None, None]
            merged_tokens = []
            for h in range(SB_HEADS):
                rows = slice(HEAD * (h % 2), HEAD * (h % 2) + HEAD)
                block = h // 2
                w4 = sw[h % 2]
                absz, soft, lead, wt = (w4[:, i * LW:(i + 1) * LW] for i in range(4))
                q_all = Q[rows, block * T:(block + 1) * T]
                b = next_bank()
                pe.wait(sq_ready, sk_ready)
                mm(bank[b][:, 0:T], K[rows, block * T:block * T + P], q_all, True, True)
                done = pe.counts(mm(bank[b][:, T:LW], K[rows, block * T + P:(block + 1) * T],
                                    Q[rows, block * T + P:(block + 1) * T], True, True))
                act.wait(done, sw_read[h % 2])
                z = bank[b][:, 0:LW]
                t = act.counts(nc.scalar.activation(absz, z, ACT.Abs, scale=SCALE))
                act.wait(t)
                t = act.counts(nc.scalar.activation(absz, absz, ACT.Exp, scale=-1.0))
                act.wait(t)
                t = act.counts(nc.scalar.activation(absz, absz, ACT.Ln, bias=con("one"), scale=1.0))
                dve.wait(t, smask_in)
                t1 = dve.counts(nc.vector.tensor_scalar(soft, z, SCALE, 0.0, ALU.mult, ALU.max))
                t2 = dve.counts(nc.vector.tensor_scalar(lead, z, SCALE, 0.0, ALU.mult, ALU.min))
                free[b] = t2
                dve.wait(t2)
                t1 = dve.counts(nc.vector.tensor_tensor(soft, soft, absz, ALU.add))
                t2 = dve.counts(nc.vector.tensor_tensor(lead, lead, absz, ALU.subtract))
                dve.wait(t1)
                t = dve.counts(nc.vector.tensor_tensor(soft, soft, smask, ALU.mult))
                b = next_bank()
                pe.wait(t)
                mm(bank[b][:, 0:T], later, soft[:, 0:T], True, True, True)
                mm(bank[b][:, P:T], ones, soft[:, T:LW], False, True, True)
                done = pe.counts(mm(bank[b][:, T:LW], later, soft[:, T:LW], False, True, True))
                dve.wait(done, t2)
                t = dve.counts(nc.vector.tensor_tensor(lead, lead, bank[b][:, 0:LW], ALU.subtract))
                free[b] = t
                act.wait(t)
                t = act.counts(nc.scalar.activation(wt, lead, ACT.Exp))
                dve.wait(t)
                t = dve.counts(nc.vector.tensor_tensor(wt, wt, smask, ALU.mult))
                b = next_bank()
                pe.wait(t, sv_ready)
                o = bank[b][rows, 0:T]
                mm(o, V[:, h * HEAD:(h + 1) * HEAD], wt[:, 0:T], True, False, True)
                done = pe.counts(mm(bank[b][rows, P:T], V[:, D + h * HEAD:D + (h + 1) * HEAD], wt[:, T:LW],
                                    False, True, True))
                sw_read[h % 2] = done
                act.wait(done)
                t = act.counts(nc.scalar.copy(merged[rows, block * T:(block + 1) * T], o))
                free[b] = t
                merged_tokens.append(t)

            base = 6 * T + 8 * LW
            W3 = N_GROUPS * T
            for j in range(GROUP_HEADS):
                rows = slice(HEAD * (j % 2), HEAD * (j % 2) + HEAD)
                ob = (0, 1)[j % 2]
                o_bank = bank[ob]
                for tt in range(TT):
                    s = (2 * j + tt) % 2
                    lw = work[:, base + s * W3:base + (s + 1) * W3]
                    pt = work[:, base + (2 + s) * W3:base + (3 + s) * W3]
                    small = work[:, base + 4 * W3 + 4 * s:base + 4 * W3 + 4 * (s + 1)]
                    n_keys = P * (tt + 1)
                    width = N_GROUPS * n_keys
                    where, banks = [], []
                    for g in range(N_GROUPS):
                        if g == 0 or (tt == 1 and g == 2):
                            banks.append(next_bank())
                            at0 = 0
                        where.append((banks[-1], at0))
                        at0 += n_keys
                    done = []
                    for g in range(N_GROUPS):
                        blk_i = 2 + (GROUP_HEADS * g + j) // 2
                        pe.wait(ready["q", blk_i - 2], ready["k", blk_i - 2])
                        b, a0 = where[g]
                        ins = mm(bank[b][:, a0:a0 + n_keys], Q[rows, blk_i * T + tt * P:blk_i * T + (tt + 1) * P],
                                 K[rows, blk_i * T:blk_i * T + n_keys], True, True)
                    done = pe.counts(ins)
                    dve.wait(done, bias_ready, dil_read[s])
                    off = (j * N_GROUPS * N_LOGIT) + (0 if tt == 0 else N_GROUPS * P)
                    if tt == 0:
                        parts = [(banks[0], 0, width)]
                    else:
                        parts = [(banks[0], 0, 2 * n_keys), (banks[1], 2 * n_keys, n_keys)]
                    for b, a0, n_c in parts:
                        t = dve.counts(nc.vector.scalar_tensor_tensor(
                            lw[:, a0:a0 + n_c], bank[b][:, 0:n_c], SCALE, bias[:, off + a0:off + a0 + n_c],
                            ALU.mult, ALU.add))
                        free[b] = t
                    dve.wait(t)
                    t = dve.counts(nc.vector.tensor_reduce(small[:, 0:1], lw[:, 0:width], AX_X, ALU.max))
                    dve.wait(t)
                    t = dve.counts(nc.vector.tensor_scalar(small[:, 1:2], small[:, 0:1], -1.0, None, ALU.mult))
                    act.wait(t)
                    t = act.counts(nc.scalar.activation(lw[:, 0:width], lw[:, 0:width], ACT.Exp,
                                                        bias=small[:, 1:2], scale=1.0, accum_out=small[:, 2:3]))
                    dve.wait(t)
                    t = dve.counts(nc.vector.reciprocal(small[:, 3:4], small[:, 2:3]))
                    dve.wait(t)
                    t = dve.counts(nc.vector.tensor_scalar(lw[:, 0:width], lw[:, 0:width], small[:, 3:4], None,
                                                           ALU.mult))
                    pe.wait(t)
                    n_piece = N_GROUPS * (tt + 1)
                    for p0 in range(0, n_piece, 4):
                        b = next_bank()
                        m = min(4, n_piece - p0)
                        for i in range(m):
                            ins = nc.tensor.transpose(bank[b][:, i * P:(i + 1) * P],
                                                      lw[:, (p0 + i) * P:(p0 + i + 1) * P], ident)
                        done = pe.counts(ins)
                        act.wait(done)
                        t = act.counts(nc.scalar.copy(pt[:, p0 * P:(p0 + m) * P], bank[b][:, 0:m * P]))
                        free[b] = t
                    pe.wait(t, dv_ready)
                    if tt == 0:
                        pe.wait(free[ob])
                    for i in range(n_piece):
                        g, s_tile = i // (tt + 1), i % (tt + 1)
                        head = SB_HEADS + GROUP_HEADS * g + j
                        ins = mm(o_bank[rows, tt * P:(tt + 1) * P],
                                 V[:, s_tile * D + head * HEAD:s_tile * D + (head + 1) * HEAD],
                                 pt[:, i * P:(i + 1) * P], i == 0, i == n_piece - 1)
                    done = pe.counts(ins)
                    dil_read[s] = done
                block = 2 + j // 2
                act.wait(done)
                t = act.counts(nc.scalar.copy(merged[rows, block * T:(block + 1) * T], o_bank[rows, 0:T]))
                free[ob] = t
                merged_tokens.append(t)

            for u in range(2):
                n, w = take("attn_w_out", u)
                pe.wait(*merged_tokens[4 * u:4 * u + 4])
                pe.wait(*free[0:4])
                for c in range(KT):
                    for i in range(2):
                        start = u == 0 and i == 0 and c % 2 == 0
                        ins = mm(bank[c // 2][:, (c % 2) * T:(c % 2 + 1) * T],
                                 w[:, i * D + c * P:i * D + (c + 1) * P], blk(merged, 2 * u + i),
                                 start, u == 1 and i == 1, True)
                done = pe.counts(ins)
                give_back(n, done)
            return add_residual([done] * 4, 1.0)

        dil_read = [None, None]

        def rwkv(h_tokens):
            A = KT * T
            r, kx, v, ld, a, g = (arena[:, i * A:(i + 1) * A] for i in range(6))
            xx = arena[:, 6 * A:7 * A]
            xm = [arena[:, 7 * A:8 * A], arena[:, 8 * A:9 * A]]
            lora = arena[:, 9 * A:9 * A + 4 * T]
            masks = arena[:, 12 * A - 11 * P:12 * A]
            act.wait(pe.now(), dve.now(), pool.now())
            masks_in = load_small(act, masks, dram["rwkv_masks"])

            h3 = xn[:, :].rearrange("p (k t) -> p k t", k=KT)
            xx3 = xx.rearrange("p (k t) -> p k t", k=KT)
            dve.wait(*h_tokens)
            dve.wait(pe.now(), act.now())
            t1 = dve.counts(nc.vector.tensor_tensor(xx3[:, :, 1:T], h3[:, :, 0:T - 1], h3[:, :, 1:T], ALU.subtract))
            t2 = dve.counts(nc.vector.tensor_scalar(xx3[:, :, 0:1], h3[:, :, 0:1], -1.0, None, ALU.mult))
            dve.wait(t1, t2)
            xm_read = [None, None]

            def mixed(which, i):
                dve.wait(xm_read[i])
                return [dve.counts(nc.vector.scalar_tensor_tensor(
                    blk(xm[i], k), blk(xx, k), col("rw_mix", which * KT + k), blk(xn, k), ALU.mult, ALU.add))
                    for k in range(KT)]

            def full(name, i, tokens, dst):
                for u in range(4):
                    b, done = project_T(name, u, xm[i], tokens)
                    act.wait(done)
                    t = act.counts(nc.scalar.copy(dst[:, 2 * u * T:(2 * u + 2) * T], bank[b][:, :]))
                    free[b] = t
                xm_read[i] = done
                return t

            tok = mixed(0, 0)
            tok_k = mixed(2, 1)
            r_ready = full("rw_wr", 0, tok, r)
            tok = mixed(3, 0)
            k_ready = full("rw_wk", 1, tok_k, kx)
            tok_w = mixed(1, 1)
            v_ready = full("rw_wv", 0, tok, v)
            tok_a = mixed(4, 0)
            n_in, w_in = take("lora_in", 0, P, 2 * KT * HEAD)
            n_out, w_out = take("lora_out", 0, HEAD, 2 * D)
            lt = {}
            for i, (tokens, src, func) in enumerate(((tok_w, xm[1], ACT.Tanh), (tok_a, xm[0], ACT.Copy))):
                b = next_bank()
                for k in range(KT):
                    pe.wait(tokens[k])
                    ins = mm(bank[b][0:HEAD, 0:T], w_in[:, (i * KT + k) * HEAD:(i * KT + k + 1) * HEAD],
                             blk(src, k), k == 0, k == KT - 1)
                done = pe.counts(ins)
                xm_read[1 - i] = done
                act.wait(done)
                t = act.counts(nc.scalar.activation(lora[0:HEAD, i * T:(i + 1) * T], bank[b][0:HEAD, 0:T], func))
                free[b] = t
                lt[i] = t
            give_back(n_in, done)
            tok_g = mixed(5, 1)
            for i, (dst, offset) in enumerate(((ld, "rw_w0"), (a, "rw_a0"))):
                pe.wait(lt[i])
                for c in range(0, KT, 2):
                    b = next_bank()
                    for j in range(2):
                        ins = mm(bank[b][:, j * T:(j + 1) * T],
                                 w_out[:, i * D + (c + j) * P:i * D + (c + j + 1) * P],
                                 lora[0:HEAD, i * T:(i + 1) * T], True, True)
                    done = pe.counts(ins)
                    act.wait(done)
                    for j in range(2):
                        t = act.counts(nc.scalar.activation(blk(dst, c + j), bank[b][:, j * T:(j + 1) * T],
                                                            ACT.Sigmoid, bias=col(offset, c + j), scale=1.0))
                    free[b] = t
            give_back(n_out, done)
            da_ready = t
            b, done = project_T("gate_in", 0, xm[1], tok_g)
            act.wait(done)
            t = act.counts(nc.scalar.activation(lora[:, 2 * T:4 * T], bank[b][:, :], ACT.Sigmoid))
            free[b] = t
            n, w = take("gate_out", 0)
            pe.wait(t)
            for c in range(0, KT, 2):
                b = next_bank()
                for j in range(2):
                    for i in range(2):
                        ins = mm(bank[b][:, j * T:(j + 1) * T],
                                 w[:, i * D + (c + j) * P:i * D + (c + j + 1) * P],
                                 lora[:, (2 + i) * T:(3 + i) * T], i == 0, i == 1)
                done = pe.counts(ins)
                act.wait(done)
                t = act.counts(nc.scalar.copy(g[:, c * T:(c + 2) * T], bank[b][:, :]))
                free[b] = t
            give_back(n, done)
            g_ready = t
            state["xn_read"] = pe.now()

            for e in (pe, dve, act, pool):
                e.wait(pe.now(), dve.now(), act.now(), pool.now(), masks_in)
            y_out = r
            slot_cols = (12 * A - 11 * P - 6 * A) // 2
            elsewhere = {"Ti": (xn, 0), "TiT": (xn, T), "X": (xn, 2 * T), "BH": (xn, 3 * T), "sc": (sq, 0)}
            names = [("kk", T), ("tmp", T), ("bonus", T), ("cum", T), ("grow", T), ("ar", 2 * T), ("bt", T),
                     ("kt", T), ("hat", T), ("BH", T), ("KH", T), ("VN", T), ("sc", 4 * T), ("lev", 5 * T),
                     ("Ti", T), ("TiT", T), ("X", T), ("Xs", P), ("U", P), ("S", P), ("WC", 4)]
            assert sum(n for name, n in names if name not in elsewhere) <= slot_cols
            final = [None] * KT

            def pair(kt, slot):
                at = 6 * A + slot * slot_cols
                buf = {}
                for name, n in names:
                    if name in elsewhere:
                        home, offset = elsewhere[name]
                        offset += slot * 4 * T
                        buf[name] = home[:, offset:offset + n]
                        continue
                    buf[name] = arena[:, at:at + n]
                    at += n
                b0, b1, b2, b3 = (4 * slot + i for i in range(4))
                rT, kT, vT, dT, aT = (blk(z, kt) for z in (r, kx, v, ld, a))
                kk, tmp, bonus, cum, grow = (buf[z] for z in ("kk", "tmp", "bonus", "cum", "grow"))
                ar = buf["ar"].rearrange("p (s w t) -> p s w t", s=TT, w=2)
                bt, kt_, hat = buf["bt"], buf["kt"], buf["hat"]

                def V(ins):
                    t = dve.counts(ins)
                    dve.wait(t)
                    return t

                def halves(z):
                    return z.rearrange("p (s t) -> p s t", s=TT)

                V(nc.vector.tensor_scalar(kk, kT, col("rw_kk", kt), None, ALU.mult))
                t = V(nc.vector.tensor_tensor(tmp, kk, kk, ALU.mult))
                pe.wait(t, free[b0])
                done = pe.counts(mm(bank[b0][:, 0:T], head_ones, tmp, True, True))
                yield
                act.wait(done)
                t = act.counts(nc.scalar.activation(hat, bank[b0][:, 0:T], ACT.Sqrt))
                free[b0] = t
                V(nc.vector.tensor_scalar(dT, dT, DECAY_SCALE, None, ALU.mult))
                t_cum = V(nc.vector.tensor_tensor_scan(cum, con("restart"), dT, 0.0, ALU.mult, ALU.add))
                V(nc.vector.tensor_tensor(dT, cum, dT, ALU.subtract))
                dve.wait(t)
                V(nc.vector.tensor_scalar(hat, hat, 1e-12, None, ALU.max))
                V(nc.vector.reciprocal(hat, hat))
                t_kk = V(nc.vector.tensor_tensor(kk, kk, hat, ALU.mult))
                act.wait(dve.now())
                t_grow = act.counts(nc.scalar.activation(grow, cum, ACT.Exp))
                t_prev = act.counts(nc.scalar.activation(dT, dT, ACT.Exp))
                t_shrink = act.counts(nc.scalar.activation(cum, cum, ACT.Exp, scale=-1.0))
                yield
                V(nc.vector.tensor_scalar(tmp, aT, -1.0, col("rw_ka", kt), ALU.add, ALU.mult))
                V(nc.vector.scalar_tensor_tensor(kT, tmp, 1.0, kT, ALU.add, ALU.mult))
                V(nc.vector.tensor_tensor(aT, kk, aT, ALU.mult))
                V(nc.vector.scalar_tensor_tensor(tmp, rT, col("rw_rk", kt), kT, ALU.mult, ALU.mult))
                pe.wait(dve.now(), free[b1])
                done = pe.counts(mm(bank[b1][:, 0:T], head_ones, tmp, True, True))
                pe.wait(free[b2])
                for s in range(TT):
                    ins = nc.tensor.transpose(bank[b2][:, s * P:(s + 1) * P], vT[:, s * P:(s + 1) * P], ident)
                v_done = pe.counts(ins)
                yield
                dve.wait(done)
                t = V(nc.vector.tensor_tensor(bonus, bank[b1][:, 0:T], vT, ALU.mult))
                free[b1] = t
                act.wait(v_done)
                t_vn = act.counts(nc.scalar.copy(buf["VN"], bank[b2][:, 0:T]))
                free[b2] = t_vn
                dve.wait(t_grow, t_prev, t_shrink)
                dve.counts(nc.vector.scalar_tensor_tensor(ar[:, :, 0, :], halves(kk), -1.0, halves(dT),
                                                          ALU.mult, ALU.mult))
                dve.counts(nc.vector.tensor_tensor(ar[:, :, 1, :], halves(rT), halves(grow), ALU.mult))
                dve.counts(nc.vector.tensor_tensor(bt, aT, cum, ALU.mult))
                t = V(nc.vector.tensor_tensor(kt_, kT, cum, ALU.mult))
                t_ops = t
                WC = buf["WC"]
                V(nc.vector.tensor_copy(WC, grow[:, RW_CHUNK - 1:T:RW_CHUNK]))
                wc_b = WC.rearrange("p (c o) -> p c o", o=1).to_broadcast([P, T // RW_CHUNK, RW_CHUNK])
                for src, dst in ((bt, "BH"), (kt_, "KH")):
                    t = V(nc.vector.tensor_tensor(hat.rearrange("p (c t) -> p c t", t=RW_CHUNK),
                                                  src.rearrange("p (c t) -> p c t", t=RW_CHUNK), wc_b, ALU.mult))
                    pe.wait(t, free[b2])
                    for s in range(TT):
                        ins = nc.tensor.transpose(bank[b2][:, s * P:(s + 1) * P], hat[:, s * P:(s + 1) * P], ident)
                    done = pe.counts(ins)
                    yield
                    act.wait(done)
                    t_nat = act.counts(nc.scalar.copy(buf[dst], bank[b2][:, 0:T]))
                    free[b2] = t_nat
                    dve.wait(done)
                S = buf["S"]
                t_S = V(nc.vector.memset(S, 0.0))
                yv = tmp
                sc = buf["sc"]
                for s in range(TT):
                    cols = slice(s * P, (s + 1) * P)
                    for p in range(2):
                        rows = slice(p * HEAD, (p + 1) * HEAD)
                        pe.wait(t_ops, free[(b0, b1)[p]])
                        arr = ar[rows, s, :, :].rearrange("p w t -> p (w t)")
                        mm(bank[(b0, b1)[p]][:, 0:T], bt[rows, cols], arr, True, True)
                        done = pe.counts(mm(bank[(b0, b1)[p]][:, T:2 * T], kt_[rows, cols], arr, True, True))
                        yield
                        dve.wait(done, pe_tile_read[slot])
                        t = dve.counts(nc.vector.tensor_tensor(sc[:, p * 512:(p + 1) * 512],
                                                               bank[(b0, b1)[p]][:, :], masks[:, 0:512], ALU.mult))
                        free[(b0, b1)[p]] = t
                    dve.wait(t)
                    sc4 = sc.rearrange("p (h w t) -> p h w t", h=2, w=4)
                    MabT, MrbT = (sc4[:, :, i, :] for i in (0, 1))
                    Ti = buf["Ti"].rearrange("p (h t) -> p h t", h=2)
                    TiT = buf["TiT"].rearrange("p (h t) -> p h t", h=2)
                    X = buf["X"].rearrange("p (h t) -> p h t", h=2)
                    lev = buf["lev"].rearrange("p (l h t) -> p l h t", l=5, h=2)
                    pool.wait(t, pe_tile_read[slot])
                    lev_ready = []
                    for li in range(5):
                        m_b = masks[:, (5 + li) * P:(6 + li) * P].rearrange("p (o t) -> p o t", o=1)\
                            .to_broadcast([P, 2, P])
                        lev_ready.append(pool.counts(nc.gpsimd.tensor_tensor(lev[:, li, :, :], MabT, m_b, ALU.mult)))
                    pe.wait(t, free[b2])
                    for h in range(2):
                        ins = nc.tensor.transpose(bank[b2][:, h * P:(h + 1) * P], MabT[:, h, :], ident)
                    done = pe.counts(ins)
                    m1T = masks[:, 4 * P:5 * P].rearrange("p (o t) -> p o t", o=1).to_broadcast([P, 2, P])
                    m1 = masks[:, 10 * P:11 * P].rearrange("p (o t) -> p o t", o=1).to_broadcast([P, 2, P])
                    id_b = ident.rearrange("p (o t) -> p o t", o=1).to_broadcast([P, 2, P])
                    V(nc.vector.tensor_tensor(TiT, MabT, m1T, ALU.mult))
                    t_tt = V(nc.vector.tensor_tensor(TiT, TiT, id_b, ALU.add))
                    yield
                    dve.wait(done)
                    t = V(nc.vector.tensor_tensor(Ti, bank[b2][:, 0:T].rearrange("p (h t) -> p h t", h=2), m1,
                                                  ALU.mult))
                    free[b2] = t
                    t_t = V(nc.vector.tensor_tensor(Ti, Ti, id_b, ALU.add))
                    for li in range(5):
                        pe.wait(t_t, t_tt, lev_ready[li], free[b2])
                        for h in range(2):
                            ins = mm(bank[b2][:, h * P:(h + 1) * P], lev[:, li, h, :], Ti[:, h, :], True, True)
                        done = pe.counts(ins)
                        yield
                        act.wait(done)
                        t_x = act.counts(nc.scalar.copy(buf["X"], bank[b2][:, 0:T]))
                        free[b2] = t_x
                        pe.wait(t_x)
                        pe.wait(free[b1])
                        for h in range(2):
                            ins = mm(bank[b1][:, h * P:(h + 1) * P], X[:, h, :], TiT[:, h, :], True, True)
                        done_tt = pe.counts(ins)
                        if li < 4:
                            pe.wait(free[b0])
                            for h in range(2):
                                ins = mm(bank[b0][:, h * P:(h + 1) * P], TiT[:, h, :], X[:, h, :], True, True)
                            done_t = pe.counts(ins)
                        else:
                            done_t = done_tt
                        yield
                        dve.wait(done_t, done_tt)
                        t_tt = dve.counts(nc.vector.tensor_tensor(buf["TiT"], buf["TiT"], bank[b1][:, 0:T], ALU.add))
                        free[b1] = t_tt
                        if li < 4:
                            t_t = dve.counts(nc.vector.tensor_tensor(buf["Ti"], buf["Ti"], bank[b0][:, 0:T],
                                                                     ALU.add))
                            free[b0] = t_t
                        dve.wait(t_tt, t_t)
                    VN = buf["VN"][:, cols]
                    Xs, U = buf["Xs"], buf["U"]
                    pe.wait(t_vn, free[b2])
                    for h in range(2):
                        ins = mm(bank[b2][:, h * HEAD:(h + 1) * HEAD], sc4[:, h, 2, :],
                                 VN[:, h * HEAD:(h + 1) * HEAD], True, True)
                    done = pe.counts(ins)
                    yield
                    act.wait(done)
                    t_xs = act.counts(nc.scalar.copy(Xs, bank[b2][:, 0:P]))
                    free[b2] = t_xs
                    pe.wait(free[b3])
                    for c in range(2):
                        rc = slice(c * RW_CHUNK, (c + 1) * RW_CHUNK)
                        pe.wait(t_S, free[b2])
                        mm(bank[b3][:, rc], S, ar[:, s, 1, rc], c == 0, True, True)
                        done = pe.counts(mm(bank[b2][:, 0:P], ar[:, s, 0, :], S, True, True))
                        yield
                        dve.wait(done, t_xs)
                        t = dve.counts(nc.vector.tensor_tensor(Xs[rc, :], bank[b2][rc, 0:P], Xs[rc, :], ALU.add))
                        free[b2] = t
                        pe.wait(t, t_tt, free[b1])
                        for h in range(2):
                            ins = mm(bank[b1][:, h * HEAD:(h + 1) * HEAD], TiT[:, h, :],
                                     Xs[:, h * HEAD:(h + 1) * HEAD], True, True)
                        done_u = pe.counts(ins)
                        yield
                        act.wait(done_u)
                        t_u = act.counts(nc.scalar.copy(U[rc, :], bank[b1][rc, 0:P]))
                        free[b1] = t_u
                        pe.wait(t_u, t_nat, free[b2])
                        mm(bank[b2][:, 0:P], buf["BH"][rc, cols], U[rc, :], True, False)
                        done = pe.counts(mm(bank[b2][:, 0:P], buf["KH"][rc, cols], VN[rc, :], False, True))
                        yield
                        dve.wait(done)
                        for h in range(2):
                            hs = slice(h * HEAD, (h + 1) * HEAD)
                            t_S = dve.counts(nc.vector.scalar_tensor_tensor(
                                S[hs, hs], S[hs, hs], WC[hs, 2 * s + c:2 * s + c + 1], bank[b2][hs, hs],
                                ALU.mult, ALU.add))
                        free[b2] = t_S
                        dve.wait(t_S)
                    for h in range(2):
                        hs = slice(h * HEAD, (h + 1) * HEAD)
                        mm(bank[b3][hs, 0:P], U[:, hs], sc4[:, h, 1, :], False, True, True)
                        done = mm(bank[b3][hs, 0:P], VN[:, hs], sc4[:, h, 3, :], False, True, True)
                    done = pe.counts(done)
                    pe_tile_read[slot] = done
                    yield
                    act.wait(done)
                    t_y = act.counts(nc.scalar.copy(yv[:, cols], bank[b3][:, 0:P]))
                    free[b3] = t_y
                pe.wait(t_y, free[b0])
                done = pe.counts(mm(bank[b0][:, 0:T], head_ones, yv, True, True))
                yield
                dve.wait(done, t_y)
                t = V(nc.vector.scalar_tensor_tensor(yv, bank[b0][:, 0:T], -1.0 / HEAD, yv, ALU.mult, ALU.add))
                free[b0] = t
                t = V(nc.vector.tensor_tensor(kk, yv, yv, ALU.mult))
                pe.wait(t, free[b1])
                done = pe.counts(mm(bank[b1][:, 0:T], head_ones, kk, True, True))
                yield
                act.wait(done)
                t = act.counts(nc.scalar.activation(hat, bank[b1][:, 0:T], ACT.Sqrt, bias=con("eps_gn"),
                                                    scale=1.0 / HEAD))
                free[b1] = t
                dve.wait(t)
                V(nc.vector.reciprocal(hat, hat))
                V(nc.vector.scalar_tensor_tensor(yv, yv, col("rw_lnx_g", kt), hat, ALU.mult, ALU.mult))
                V(nc.vector.scalar_tensor_tensor(yv, yv, col("rw_lnx_b", kt), bonus, ALU.add, ALU.add))
                final[kt] = V(nc.vector.tensor_tensor(blk(y_out, kt), yv, blk(g, kt), ALU.mult))

            pe_tile_read = [None, None]
            queue = list(range(KT))
            running = {}
            while queue or running:
                for slot in range(2):
                    if slot not in running and queue:
                        running[slot] = pair(queue.pop(0), slot)
                    if slot in running and next(running[slot], "end") == "end":
                        del running[slot]
            act.wait(pe.now(), dve.now(), pool.now())
            tokens = []
            for u in range(4):
                b, done = project_T("rw_wo", u, y_out, final)
                for j in range(2):
                    dve.wait(done)
                    t = dve.counts(nc.vector.tensor_tensor(blk(x, 2 * u + j), blk(x, 2 * u + j),
                                                           bank[b][:, j * T:(j + 1) * T], ALU.add))
                    tokens.append(t)
                free[b] = t
            return tokens

        def pool_conv_mixer(layer, x_tokens):
            A = KT * T
            UP = T + PAD_POOL
            VP = T + PAD_CONV
            at = [0]

            def piece(n):
                at[0] += n
                return arena[:, at[0] - n:at[0]]

            up, s_a, s_b = piece(4 * UP), piece(4 * UP), piece(4 * UP)
            vp, val = piece(4 * VP), piece(4 * T)
            y = piece(4 * T)
            cat = piece(A)
            inv = piece(4 * T)
            dd = piece(4 * T)
            z = piece(A)
            gate = piece(4 * T)
            act.wait(pe.now(), dve.now(), pool.now())
            inv_in = load_small(act, inv, dram["inverse_count"])
            up3, a3, b3 = (q.rearrange("p (g t) -> p g t", g=4) for q in (up, s_a, s_b))
            vp3 = vp.rearrange("p (g t) -> p g t", g=4)
            pool.wait(pe.now(), dve.now(), act.now())
            for q in (up3, a3, b3):
                zeroed = pool.counts(nc.gpsimd.memset(q[:, :, 0:PAD_POOL], 0.0))
            zeroed = pool.counts(nc.gpsimd.memset(vp3[:, :, 0:PAD_CONV], 0.0))
            src = x
            w_in = "w_in_2"
            for u in range(2):
                b, done = project_T(w_in, 6 * layer + 2 + u, src, x_tokens)
                act.wait(done)
                t_val = act.counts(nc.scalar.copy(val[:, 2 * u * T:(2 * u + 2) * T], bank[b][:, :]))
                free[b] = t_val
            v_tok = []
            for u in range(2):
                b, done = project_T(w_in, 6 * layer + 4 + u, src, x_tokens)
                act.wait(done)
                t = act.counts(nc.scalar.activation(gate[:, 2 * u * T:(2 * u + 2) * T], bank[b][:, :], ACT.Sigmoid))
                free[b] = t
                dve.wait(t, t_val)
                for j in range(2):
                    g = 2 * u + j
                    v_tok.append(dve.counts(nc.vector.tensor_tensor(vp3[:, g, PAD_CONV:VP], blk(val, g), blk(gate, g),
                                                                    ALU.mult)))
            for u in range(2):
                b, done = project_T(w_in, 6 * layer + u, src, x_tokens)
                act.wait(done, zeroed)
                t = act.counts(nc.scalar.copy(up3[:, 2 * u:2 * u + 2, PAD_POOL:UP],
                                              bank[b][:, :].rearrange("p (g t) -> p g t", g=2)))
                free[b] = t
            pool.wait(t)
            cur, nxt = up3, a3
            spare = {0: a3, 1: b3, 2: a3, 3: b3}
            for i, w in enumerate(POOL_WINDOWS):
                half = w // 2
                dst = spare[i]
                t = pool.counts(nc.gpsimd.tensor_tensor(dst[:, i:4, PAD_POOL:UP], cur[:, i:4, PAD_POOL:UP],
                                                        cur[:, i:4, PAD_POOL - half:UP - half], ALU.add))
                pool.wait(t)
                cur = dst
            dd3, inv3 = (q.rearrange("p (g t) -> p g t", g=4) for q in (dd, inv))
            pool.wait(inv_in)
            for i in range(4):
                t = pool.counts(nc.gpsimd.tensor_tensor(dd3[:, i, :], spare[i][:, i, PAD_POOL:UP], inv3[:, i, :],
                                                        ALU.mult))
            pool.wait(t)
            t = pool.counts(nc.gpsimd.tensor_tensor(dd3, dd3, up3[:, :, PAD_POOL:UP], ALU.subtract))
            y_tok = []
            for g in range(4):
                dve.wait(v_tok[g], zeroed)
                for j in range(CONV_WIDTH):
                    wcol = col("conv_w_2", (layer * CONV_WIDTH + j) * 4 + g)
                    tap = vp3[:, g, j:j + T]
                    if j == 0:
                        q = dve.counts(nc.vector.tensor_scalar(blk(y, g), tap, wcol, col("conv_b_2", layer * 4 + g),
                                                               ALU.mult, ALU.add))
                    else:
                        q = dve.counts(nc.vector.scalar_tensor_tensor(blk(y, g), tap, wcol, blk(y, g), ALU.mult,
                                                                      ALU.add))
                    dve.wait(q)
                y_tok.append(q)
            n, w = take("pool_w_2", layer, P, 4 * P)
            cat_tok = [None] * KT
            pe.wait(t)
            for u in range(2):
                b = next_bank()
                for j in range(2):
                    g = 2 * u + j
                    ins = mm(bank[b][:, j * T:(j + 1) * T], w[:, g * P:(g + 1) * P], blk(dd, g), True, True)
                done = pe.counts(ins)
                act.wait(done)
                for j in range(2):
                    g = 2 * u + j
                    cat_tok[g] = act.counts(nc.scalar.activation(blk(cat, g), bank[b][:, j * T:(j + 1) * T], ACT.Copy,
                                                                 scale=col("pool_scale_2", layer * 4 + g)))
                free[b] = cat_tok[g]
            give_back(n, done)

            def finish(g):
                t = dve.counts(nc.vector.scalar_tensor_tensor(blk(y, g), blk(y, g),
                                                              col("conv_ln_g_2", layer * 4 + g), rstd[:, :],
                                                              ALU.mult, ALU.mult))
                act.wait(t)
                return act.counts(nc.scalar.activation(blk(y, g), blk(y, g), ACT.Silu,
                                                       bias=col("conv_ln_b_2", layer * 4 + g), scale=1.0))

            y_tok = layer_norm(y, y_tok, 4, finish)
            n, w = take("conv_pw_2", layer)
            for u in range(2):
                b = next_bank()
                for j in range(2):
                    c = 2 * u + j
                    for k in range(4):
                        pe.wait(y_tok[k])
                        ins = mm(bank[b][:, j * T:(j + 1) * T], w[:, k * 512 + c * P:k * 512 + (c + 1) * P],
                                 blk(y, k), k == 0, k == 3)
                done = pe.counts(ins)
                act.wait(done)
                cat_tok[4 + 2 * u] = cat_tok[5 + 2 * u] = act.counts(
                    nc.scalar.copy(cat[:, (4 + 2 * u) * T:(6 + 2 * u) * T], bank[b][:, :]))
                free[b] = cat_tok[4 + 2 * u]
            give_back(n, done)
            z_tok = []
            for u in range(4):
                b, done = project_T("w_out_2", 4 * layer + u, cat, cat_tok)
                dve.wait(done)
                for j in range(2):
                    c = 2 * u + j
                    z_tok.append(dve.counts(nc.vector.scalar_tensor_tensor(
                        blk(z, c), blk(x, c), ALPHA, bank[b][:, j * T:(j + 1) * T], ALU.mult, ALU.add)))
                free[b] = z_tok[-1]
            return z, z_tok

        def norm_to_x(z, z_tok, gain, bias, layer):
            def finish(k):
                t = dve.counts(nc.vector.scalar_tensor_tensor(blk(z, k), blk(z, k), col(gain, layer * KT + k),
                                                              rstd[:, :], ALU.mult, ALU.mult))
                act.wait(t)
                return act.counts(nc.scalar.activation(blk(x, k), blk(z, k), ACT.Identity,
                                                       bias=col(bias, layer * KT + k), scale=1.0))
            return layer_norm(z, z_tok, KT, finish)

        def deep_residual(done, z):
            z_tok = []
            for c in range(KT):
                dve.wait(done[c // 2])
                z_tok.append(dve.counts(nc.vector.scalar_tensor_tensor(
                    blk(z, c), blk(x, c), ALPHA, bank[c // 2][:, (c % 2) * T:(c % 2 + 1) * T], ALU.mult, ALU.add)))
                free[c // 2] = z_tok[-1]
            return z_tok

        def router(x_tokens):
            A = KT * T
            rows = arena[0:N_EXPERTS, 0:N_EXPERTS * P]
            gT = arena[0:N_EXPERTS, 1024:1024 + T]
            wide = arena[:, 1280:1280 + N_EXPERTS * T]
            small = arena[:, 4096:4096 + 2 * 64]
            act.wait(pe.now(), dve.now(), pool.now())
            rows_in = load_small(act, rows, dram["expert_rows"])
            at = PARAM_AT["router_w_2"]
            iota = con("iota")
            b = next_bank()
            for tt in range(TT):
                for k in range(KT):
                    pe.wait(x_tokens[k])
                    ins = mm(bank[b][:, tt * N_EXPERTS:(tt + 1) * N_EXPERTS], x[:, k * T + tt * P:k * T + (tt + 1) * P],
                             param[:, at + k * N_EXPERTS:at + (k + 1) * N_EXPERTS], k == 0, k == KT - 1)
            done = pe.counts(ins)
            dve.wait(done)
            b_g = next_bank()
            for tt in range(TT):
                s = small[:, tt * 64:(tt + 1) * 64]
                lg, eq, o1, o2 = (s[:, i * 8:(i + 1) * 8] for i in range(4))
                m1, m2, i1, dif, w1, w2 = (s[:, 32 + i:33 + i] for i in range(6))

                def V(ins):
                    t = dve.counts(ins)
                    dve.wait(t)
                    return t

                V(nc.vector.tensor_copy(lg, bank[b][:, tt * 8:(tt + 1) * 8]))
                for m, hot in ((m1, o1), (m2, o2)):
                    V(nc.vector.tensor_reduce(m, lg, AX_X, ALU.max))
                    V(nc.vector.tensor_scalar(eq, lg, m, 1e9, ALU.is_lt, ALU.mult))
                    V(nc.vector.tensor_tensor(eq, eq, iota, ALU.add))
                    V(nc.vector.tensor_reduce(i1, eq, AX_X, ALU.min))
                    V(nc.vector.tensor_scalar(hot, iota, i1, None, ALU.is_equal))
                    V(nc.vector.scalar_tensor_tensor(lg, hot, -3e38, lg, ALU.mult, ALU.add))
                t = V(nc.vector.tensor_tensor(dif, m2, m1, ALU.subtract))
                act.wait(t)
                t = act.counts(nc.scalar.activation(w2, dif, ACT.Exp))
                dve.wait(t)
                V(nc.vector.tensor_scalar(w1, w2, 1.0, None, ALU.add))
                V(nc.vector.reciprocal(w1, w1))
                V(nc.vector.tensor_tensor(w2, w2, w1, ALU.mult))
                V(nc.vector.tensor_scalar(o1, o1, w1, None, ALU.mult))
                t = V(nc.vector.scalar_tensor_tensor(o1, o2, w2, o1, ALU.mult, ALU.add))
                pe.wait(t)
                done = pe.counts(nc.tensor.transpose(bank[b_g][0:N_EXPERTS, tt * P:(tt + 1) * P], o1, ident))
            free[b] = t
            act.wait(done)
            t = act.counts(nc.scalar.copy(gT, bank[b_g][0:N_EXPERTS, 0:T]))
            free[b_g] = t
            for e in range(0, N_EXPERTS, 2):
                b = next_bank()
                pe.wait(t, rows_in)
                for j in range(2):
                    ins = mm(bank[b][:, j * T:(j + 1) * T], rows[:, (e + j) * P:(e + j + 1) * P], gT, True, True)
                done = pe.counts(ins)
                act.wait(done)
                t2 = act.counts(nc.scalar.copy(wide[:, e * T:(e + 2) * T], bank[b][:, :]))
                free[b] = t2
            dve.wait(t2)
            return wide

        def per_layer_gate(layer, x_tokens):
            A = KT * T
            pT, gate, prod = arena[:, 0:2 * T], arena[:, A:2 * A], arena[:, 2 * A:3 * A]
            act.wait(pe.now(), dve.now(), pool.now())
            p_in = load_small(act, pT, dram["p_2"][layer])
            n, w = take("ple_w_2", layer)
            pe.wait(p_in)
            pe_tok = []
            pe.wait(*free[0:4])
            for c in range(KT):
                for i in range(2):
                    ins = mm(bank[c // 2][:, (c % 2) * T:(c % 2 + 1) * T], w[:, i * D + c * P:i * D + (c + 1) * P],
                             blk(pT, i), i == 0, i == 1)
            p_done = pe.counts(ins)
            give_back(n, p_done)
            prods = []
            for u in range(4):
                b, done = project_T("ple_gate_w_2", 4 * layer + u, x, x_tokens)
                act.wait(done)
                t = act.counts(nc.scalar.activation(gate[:, 2 * u * T:(2 * u + 2) * T], bank[b][:, :], ACT.Sigmoid))
                free[b] = t
                dve.wait(t, p_done)
                t = dve.counts(nc.vector.tensor_tensor(prod[:, 2 * u * T:(2 * u + 2) * T],
                                                       gate[:, 2 * u * T:(2 * u + 2) * T], bank[u][:, :], ALU.mult))
                free[u] = t
            dve.wait(t, pe.now())
            return [dve.counts(nc.vector.tensor_tensor(blk(x, k), blk(x, k), blk(prod, k), ALU.add))
                    for k in range(KT)]

        def store(x_tokens):
            nat = arena[:, 0:TT * D]
            act.wait(pe.now(), dve.now(), pool.now())
            for tt in range(TT):
                for half in range(2):
                    b = next_bank()
                    for i in range(4):
                        k = 4 * half + i
                        pe.wait(x_tokens[k])
                        ins = nc.tensor.transpose(bank[b][:, i * P:(i + 1) * P],
                                                  x[:, k * T + tt * P:k * T + (tt + 1) * P], ident)
                    done = pe.counts(ins)
                    act.wait(done)
                    t = act.counts(nc.scalar.copy(nat[:, tt * D + half * 512:tt * D + (half + 1) * 512],
                                                  bank[b][:, :]))
                    free[b] = t
            act.wait(t)
            nc.scalar.dma_start(out.rearrange("(s p) d -> p s d", p=P),
                                nat.rearrange("p (s d) -> p s d", s=TT)).then_inc(out_written, 16)
            act.wait((out_written, 16))

        names1 = ("ffn_w_gate", "ffn_w_up", "ffn_w_down")
        FFN_UNITS = D_FF // CHUNK
        EXP_UNITS = D_FF_EXPERT // CHUNK

        def half_ffn(which, tokens):
            n_tok = rms_norm(tokens, "ffn_norm", which * KT)
            done = gated_ffn(xn, n_tok, names1, which * FFN_UNITS, FFN_UNITS)
            state["xn_read"] = done[3]
            return add_residual(done, 0.5)

        def network():
            tokens = [small_in] * KT
            tokens = half_ffn(0, tokens)
            n_tok = rms_norm(tokens, "mix_norm", 0)
            tokens = attention(n_tok, tokens)
            tokens = half_ffn(1, tokens)
            tokens = half_ffn(2, tokens)
            n_tok = rms_norm(tokens, "mix_norm", KT)
            tokens = rwkv(n_tok)
            tokens = half_ffn(3, tokens)
            for layer in range(2):
                z, z_tok = pool_conv_mixer(layer, tokens)
                tokens = norm_to_x(z, z_tok, "ln1_g_2", "ln1_b_2", layer)
                z = arena[:, 8 * KT * T:9 * KT * T]
                if layer == 0:
                    done = gated_ffn(x, tokens, ("dense_w1_2", "dense_w3_2", "dense_w2_2"), 0, FFN_UNITS)
                else:
                    wide = router(tokens)
                    for e in range(N_EXPERTS):
                        done = gated_ffn(x, tokens, ("exp_w1_2", "exp_w3_2", "exp_w2_2"), e * EXP_UNITS, EXP_UNITS,
                                         blk(wide, e), e == 0, e == N_EXPERTS - 1)
                z_tok = deep_residual(done, z)
                tokens = norm_to_x(z, z_tok, "ln2_g_2", "ln2_b_2", layer)
                tokens = per_layer_gate(layer, tokens)
            return tokens

        store(network())

        for n, (src, rows, cols, _) in enumerate(units):
            if n >= RING:
                sp.wait(units[n - RING][3])
            at = (n % RING) * UNIT
            nc.sync.dma_start(ring[0:rows, at:at + cols], src).then_inc(slot_landed[n % RING], 16)


def column_units(w):
    w = np.asarray(w)
    w = w.reshape(-1, KT, P, w.shape[-1] // CHUNK, CHUNK)
    return np.ascontiguousarray(w.transpose(0, 3, 2, 1, 4)).reshape(-1, P, UNIT)


def row_units(w):
    w = np.asarray(w).reshape(-1, 2, P, D)
    return np.ascontiguousarray(w.transpose(0, 2, 1, 3)).reshape(-1, P, UNIT)


def token_T(a):
    f = a.shape[-1]
    return np.ascontiguousarray(a.reshape(T, f // P, P).transpose(2, 1, 0)).reshape(P, f // P * T)


def lay_out(inp):
    d = dict(constant_arrays())
    d["x"] = token_T(inp["x"].reshape(T, D))
    d["p_2"] = np.stack([token_T(inp["p_2"][i].reshape(T, -1)) for i in range(2)])
    cols = []
    for name, n in PARAMS:
        a = np.asarray(inp[name])
        if name in ("attn_q_norm", "attn_k_norm"):
            c = np.concatenate([a.reshape(HEAD, 1)] * 2, axis=0)
        elif name == "router_w_2":
            c = a.reshape(KT, P, N_EXPERTS).transpose(1, 0, 2).reshape(P, -1)
        else:
            c = a.reshape(n, P).T
        cols.append(c)
    d["params"] = np.ascontiguousarray(np.concatenate(cols, axis=1))
    for name in ("ffn_w_gate", "ffn_w_up", "attn_w_in", "rw_wr", "rw_wk", "rw_wv", "rw_wo", "w_in_2", "w_out_2",
                 "dense_w1_2", "dense_w3_2", "exp_w1_2", "exp_w3_2", "ple_gate_w_2"):
        d[name] = column_units(inp[name])
    for name in ("ffn_w_down", "attn_w_out", "dense_w2_2", "exp_w2_2", "ple_w_2"):
        d[name] = row_units(inp[name])
    k_tiles = lambda w: np.asarray(w).reshape(KT, P, -1).transpose(1, 0, 2).reshape(P, -1)
    d["lora_in"] = np.concatenate([k_tiles(inp["rw_w1"]), k_tiles(inp["rw_a1"])], axis=1)[None]
    d["lora_out"] = np.concatenate([inp["rw_w2"][0], inp["rw_a2"][0]], axis=1)[None]
    g1 = np.asarray(inp["rw_g1"][0])
    d["gate_in"] = column_units(np.pad(g1, ((0, 0), (0, CHUNK - g1.shape[1]))))
    g2 = np.asarray(inp["rw_g2"][0])
    d["gate_out"] = row_units(np.pad(g2, ((0, CHUNK - g2.shape[0]), (0, 0))))
    d["pool_w_2"] = np.ascontiguousarray(np.asarray(inp["pool_w_2"]).transpose(0, 2, 1, 3)).reshape(2, P, 4 * P)
    d["conv_pw_2"] = np.ascontiguousarray(
        np.asarray(inp["conv_pw_2"]).reshape(2, 4, P, 512).transpose(0, 2, 1, 3)).reshape(2, P, UNIT)
    bucket = bucket_of_distance()
    table = np.asarray(inp["rel_bias"])
    rows = []
    for j in range(GROUP_HEADS):
        for tile in range(TT):
            dist = tile * P + np.arange(P)[:, None] - np.arange(P * (tile + 1))[None, :]
            at = bucket[np.maximum(dist, 0)]
            for g in range(N_GROUPS):
                rows.append(table[:, GROUP_HEADS * g + j][at])
    d["rel_bias"] = np.concatenate(rows, axis=1)
    return {k: np.ascontiguousarray(v) for k, v in d.items()}


def kernel(**inputs):
    import concourse.bacc as bacc
    from concourse.bass_utils import run_bass_kernel_spmd

    arrays = lay_out({k: np.asarray(v) for k, v in inputs.items()})
    nc = bacc.Bacc("TRN2", target_bir_lowering=False, num_devices=1)
    dram = {name: nc.dram_tensor(f"in_{name}", a.shape, mybir.dt.from_np(a.dtype), kind="ExternalInput").ap()
            for name, a in arrays.items()}
    out = nc.dram_tensor("out", (T, D), F32, kind="ExternalOutput").ap()
    bass_macaron_attention_rwkv_conv_moe_kernel(nc, dram, out)
    result = run_bass_kernel_spmd(nc, [{f"in_{name}": a for name, a in arrays.items()}], core_ids=[0])
    return result.results[0]["out"].reshape(1, T, D)
```

```python
from contextlib import ExitStack

import numpy as np

import concourse.bass as bass
from concourse import mybir

F32 = mybir.dt.float32
F32R = mybir.dt.float32r
ALU = mybir.AluOpType
ACT = mybir.ActivationFunctionType
AX_X = mybir.AxisListType.X

P = 128
D = 1024
T = 256
KT = D // P
TT = T // P
D_FF = 2816
D_FF_EXPERT = 3584
N_EXPERTS = 8
CHUNK = 256
UNIT = KT * CHUNK
HEAD = 64
SB_HEADS = 4
DIL_HEADS = 12
DIL_PATTERNS = ((128, 1), (512, 4), (2048, 16))
N_GROUPS = len(DIL_PATTERNS)
GROUP_HEADS = DIL_HEADS // N_GROUPS
N_BUCKETS = 32
MAX_DISTANCE = 2048
NEG_INF = -1e30
SCALE = HEAD ** -0.5
RW_CHUNK = 64
DECAY_SCALE = -float(np.exp(-0.5))
CONV_WIDTH = 31
PAD_CONV = CONV_WIDTH - 1
POOL_WINDOWS = (2, 4, 8, 16)
PAD_POOL = 16
ALPHA = 4.0 ** 0.25
ARENA = 23296
RAW_SLOTS = 3
HALVES = 4
HALF = UNIT // 2
LEVELS = (2, 4, 8, 16, 32)

PARAMS = [
    ("ffn_norm", 4 * KT), ("mix_norm", 2 * KT), ("rw_mix", 6 * KT), ("rw_w0", KT), ("rw_a0", KT),
    ("rw_kk", KT), ("rw_ka", KT), ("rw_rk", KT), ("rw_lnx_g", KT), ("rw_lnx_b", KT),
    ("attn_q_norm", 1), ("attn_k_norm", 1), ("pool_scale_2", 8), ("conv_w_2", 2 * CONV_WIDTH * 4),
    ("conv_b_2", 8), ("conv_ln_g_2", 8), ("conv_ln_b_2", 8), ("ln1_g_2", 16), ("ln1_b_2", 16),
    ("ln2_g_2", 16), ("ln2_b_2", 16), ("router_w_2", KT * N_EXPERTS),
]
PARAM_AT = {}
N_PARAM = 0
for _name, _n in PARAMS:
    PARAM_AT[_name] = N_PARAM
    N_PARAM += _n

CONSTS = [
    ("ident", P), ("ones", P), ("head_ones", P), ("later", P), ("eps_rms", 1), ("eps_gn", 1),
    ("eps_ln", 1), ("one", 1), ("iota", N_EXPERTS), ("restart", T),
]
CONST_AT = {}
N_CONST = 0
for _name, _n in CONSTS:
    CONST_AT[_name] = N_CONST
    N_CONST += _n
N_LOGIT = P + 2 * P


def constant_arrays():
    row, col = np.arange(P)[:, None], np.arange(P)[None, :]
    c = np.zeros((P, N_CONST), np.float32)

    def put(name, value):
        at = CONST_AT[name]
        n = dict(CONSTS)[name]
        c[:, at:at + n] = value

    put("ident", row == col)
    put("ones", 1.0)
    put("head_ones", row // HEAD == col // HEAD)
    put("later", row > col)
    put("eps_rms", 1e-6)
    put("eps_gn", 64e-5)
    put("eps_ln", 1e-5)
    put("one", 1.0)
    put("iota", np.arange(N_EXPERTS)[None, :])
    put("restart", (np.arange(T)[None, :] % RW_CHUNK) != 0)

    before = (row < col).astype(np.float32)
    stick = np.concatenate([before, np.ones((P, P), np.float32), before], axis=1)

    dil = []
    for tile in range(TT):
        keys = np.arange(P * (tile + 1))[None, :]
        dist = tile * P + row - keys
        for window, r in DIL_PATTERNS:
            ok = (dist >= 0) & (dist <= window) & (dist % r == 0)
            dil.append(np.where(ok, 0.0, NEG_INF).astype(np.float32))
    dil = np.concatenate(dil, axis=1)

    same = row // RW_CHUNK == col // RW_CHUNK
    strict = (same & (row < col)).astype(np.float32)
    upto = (same & (row <= col)).astype(np.float32)
    rw = [strict, upto, strict, upto]
    for b in (1,) + LEVELS:
        rw.append(((row // (2 * b) == col // (2 * b)) & (row % (2 * b) < b) & (col % (2 * b) >= b)).astype(np.float32))
    rw.append(rw[4].T)
    rw = np.concatenate(rw, axis=1)

    t = np.arange(T)
    count = np.stack([1.0 / np.minimum(t + 1.0, w) for w in POOL_WINDOWS]).astype(np.float32)
    count = np.broadcast_to(count.reshape(1, -1), (P, 4 * T))
    pick = np.zeros((N_EXPERTS, N_EXPERTS, P), np.float32)
    pick[np.arange(N_EXPERTS), np.arange(N_EXPERTS), :] = 1.0
    return {"consts": c, "stick_mask": stick, "dilated_mask": dil, "rwkv_masks": rw,
            "moe_tables": np.concatenate([(row < col).astype(np.float32), np.broadcast_to(col, (P, P)).astype(np.float32)],
                                         axis=1),
            "inverse_count": np.ascontiguousarray(count), "expert_rows": pick.reshape(N_EXPERTS, -1)}


def bucket_of_distance():
    d = np.arange(T)
    large = 16 + (np.log(np.maximum(d, 1) / 16.0) / np.log(MAX_DISTANCE / 16.0) * 16).astype(np.int64)
    return np.where(d < 16, d, np.minimum(large, N_BUCKETS - 1))


def stream_order():
    order = []

    def several(name, first, n, split=True):
        order.extend((name, i, split) for i in range(first, first + n))

    def ffn(gate, up, down, first, n):
        for i in range(n + 1):
            if i < n:
                order.extend([(gate, first + i, True), (up, first + i, True)])
            if i > 0:
                order.append((down, first + i - 1, True))

    n_ffn, n_expert = D_FF // CHUNK, D_FF_EXPERT // CHUNK
    ffn("ffn_w_gate", "ffn_w_up", "ffn_w_down", 0, n_ffn)
    several("attn_w_in", 0, 12)
    several("attn_w_out", 0, 2)
    ffn("ffn_w_gate", "ffn_w_up", "ffn_w_down", n_ffn, n_ffn)
    ffn("ffn_w_gate", "ffn_w_up", "ffn_w_down", 2 * n_ffn, n_ffn)
    for name in ("rw_wr", "rw_wk", "rw_wv"):
        several(name, 0, 4, False)
    for name in ("lora_in", "lora_out", "gate_in", "gate_out"):
        several(name, 0, 1, False)
    several("rw_wo", 0, 4, False)
    ffn("ffn_w_gate", "ffn_w_up", "ffn_w_down", 3 * n_ffn, n_ffn)
    for layer in range(2):
        several("w_in_2", 6 * layer + 2, 4)
        several("w_in_2", 6 * layer, 2)
        several("pool_w_2", layer, 1, False)
        several("conv_pw_2", layer, 1)
        several("w_out_2", 4 * layer, 4)
        if layer == 0:
            ffn("dense_w1_2", "dense_w3_2", "dense_w2_2", 0, n_ffn)
        else:
            ffn("exp_w1_2", "exp_w3_2", "exp_w2_2", 0, N_EXPERTS * n_expert)
        several("ple_w_2", layer, 1)
        several("ple_gate_w_2", 4 * layer, 4)
    return order


class Engine:

    def __init__(self, handle, semaphore):
        self.handle, self.semaphore, self.count, self.waited = handle, semaphore, 0, {}

    def wait(self, *tokens):
        for token in tokens:
            if token is None:
                continue
            semaphore, value = token
            if self.waited.get(id(semaphore), 0) < value:
                self.waited[id(semaphore)] = value
                self.handle.wait_ge(semaphore, value)

    def counts(self, instruction):
        instruction.then_inc(self.semaphore, 1)
        self.count += 1
        return self.semaphore, self.count

    def count_on(self, semaphore, waited):
        self.semaphore, self.count, self.waited = semaphore, 0, dict(waited)

    def now(self):
        return (self.semaphore, self.count) if self.count else None


class Silent:

    def silent(self, *args, **kwargs):
        return self

    matmul = transpose = activation = copy = mul = tensor_tensor = tensor_scalar = silent
    scalar_tensor_tensor = tensor_copy = tensor_reduce = reciprocal = memset = wait_ge = then_inc = silent


class Issuing:

    def __init__(self, tensor, vector, scalar):
        self.tensor, self.vector, self.scalar = tensor, vector, scalar


def bass_macaron_attention_rwkv_conv_moe_kernel(nc, dram, out, tile_limit=P):
    with ExitStack() as ctx:
        def sb(name, cols, dtype=F32):
            return ctx.enter_context(nc.sbuf_tensor(name, [P, cols], dtype))

        def sem(name):
            return ctx.enter_context(nc.semaphore(name))

        raw = sb("raw_weights", RAW_SLOTS * UNIT)
        w_hi, w_lo = sb("weights_hi", HALVES * HALF, F32R), sb("weights_lo", HALVES * HALF, F32R)
        s_hi, s_lo = sb("source_hi", KT * T, F32R), sb("source_lo", KT * T, F32R)
        h_hi, h_lo = sb("hidden_hi", 4 * T, F32R), sb("hidden_lo", 4 * T, F32R)
        x = sb("x_T", KT * T)
        xn = sb("normed_T", KT * T)
        sq = sb("squares", KT * T)
        arena = sb("arena", ARENA)
        param = sb("params", N_PARAM)
        const = sb("consts", N_CONST)
        act_buf = sb("activated", 4 * T)
        std = sb("std", T)
        rstd = sb("rstd", T)
        mean = sb("mean", T)
        bank = [ctx.enter_context(nc.psum_tensor(f"bank{i}", [P, 512], F32)) for i in range(8)]

        on = Issuing(nc.tensor, nc.vector, nc.scalar)
        pe = Engine(nc.tensor, sem("pe_done"))
        dve = Engine(nc.vector, sem("dve_done"))
        act = Engine(nc.scalar, sem("act_done"))
        pool = Engine(nc.gpsimd, sem("pool_done"))
        sp = Engine(nc.sync, sem("sp_done"))
        slot_landed = [sem(f"slot_landed{i}") for i in range(RAW_SLOTS)]
        split_ready = sem("split_ready")
        split_read = sem("split_read")
        small_landed = sem("small_landed")
        out_written = sem("out_written")
        small_count = [0]

        def load_small(engine, dst, src):
            engine.handle.dma_start(dst, src).then_inc(small_landed, 16)
            small_count[0] += 16
            return small_landed, small_count[0]

        stream = stream_order()
        halves = [(n, s) for n, (_, _, split) in enumerate(stream) if split for s in range(2)]
        raw_read = [None] * len(stream)
        position = {"unit": 0, "half": 0, "split": 0, "limit": len(halves)}

        def landed(n):
            return slot_landed[n % RAW_SLOTS], 16 * (n // RAW_SLOTS + 1)

        def take(name, i=0, rows=P, cols=UNIT):
            n = position["unit"]
            position["unit"] += 1
            assert stream[n] == (name, i, False), (stream[n], name, i)
            split_ahead(position["half"] + HALVES, n)
            pe.wait(landed(n))
            at = (n % RAW_SLOTS) * UNIT
            return n, raw[0:rows, at:at + cols]

        def give_back(n, token):
            raw_read[n] = token

        def split_ahead(upto, current):
            while position["split"] < min(upto, position["limit"]):
                j = position["split"]
                n, part = halves[j]
                if n > current + RAW_SLOTS - 1:
                    break
                src = raw[:, (n % RAW_SLOTS) * UNIT + part * HALF:(n % RAW_SLOTS) * UNIT + (part + 1) * HALF]
                at = slice((j % HALVES) * HALF, (j % HALVES + 1) * HALF)
                act.wait(landed(n))
                if j >= HALVES:
                    act.wait((split_read, j - HALVES + 1))
                t = act.counts(on.scalar.copy(w_hi[:, at], src))
                dve.wait(t)
                on.vector.tensor_tensor(w_lo[:, at], src, w_hi[:, at].bitcast(F32), ALU.subtract)\
                    .then_inc(split_ready, 1)
                if part == 1:
                    raw_read[n] = (split_ready, j + 1)
                position["split"] += 1

        def take_half(name, i, part):
            j = position["half"]
            position["half"] += 1
            if part == 1:
                position["unit"] += 1
            n, p = halves[j]
            assert (stream[n], p) == ((name, i, True), part), (stream[n], p, name, i, part)
            split_ahead(j + HALVES, n)
            pe.wait((split_ready, j + 1))
            at = slice((j % HALVES) * HALF, (j % HALVES + 1) * HALF)
            return w_hi[:, at], w_lo[:, at]

        def half_read(ins):
            ins.then_inc(split_read, 1)
            return split_read, position["half"]

        def mm3(dst, w, at, src, src_at, start, stop, shared, moving_weights=False):
            for i, (a, b) in enumerate(((0, 0), (0, 1), (1, 0))):
                lhsT, rhs = (src[b][:, src_at], w[a][:, at]) if moving_weights else (w[a][:, at], src[b][:, src_at])
                ins = mm(dst, lhsT, rhs, start and i == 0, stop and i == 2, shared)
            return ins

        source = (s_hi, s_lo)
        hidden = (h_hi, h_lo)

        def split_block(pair, k, piece, token, width=T):
            act.wait(token, state["source_read"] if pair is source else None)
            t = act.counts(on.scalar.copy(blk(pair[0], k, width), piece))
            dve.wait(t)
            return dve.counts(on.vector.tensor_tensor(blk(pair[1], k, width), piece,
                                                      blk(pair[0], k, width).bitcast(F32), ALU.subtract))

        def col(name, i=0, rows=P):
            return param[0:rows, PARAM_AT[name] + i:PARAM_AT[name] + i + 1]

        def con(name):
            at = CONST_AT[name]
            return const[:, at:at + dict(CONSTS)[name]]

        ident, ones, head_ones, later = con("ident"), con("ones"), con("head_ones"), con("later")

        def blk(tile, k, w=T):
            return tile[:, k * w:(k + 1) * w]

        free = [None] * 8
        turn = [0]

        def next_bank():
            turn[0] += 1
            i = 4 + turn[0] % 4
            pe.wait(free[i])
            return i

        def mm(dst, lhsT, rhs, start, stop, shared=False):
            return on.tensor.matmul(dst, lhsT, rhs, start=start, stop=stop, skip_group_check=shared)

        params_in = load_small(act, param[:, :], dram["params"])
        consts_in = load_small(act, const[:, :], dram["consts"])
        x_in = load_small(act, x[:, :], dram["x"])
        small_in = x_in
        for e in (pe, dve, act, pool):
            e.wait(small_in)

        state = {"sq_read": None, "source_read": None}

        def feature_mean(source_tokens, source, n_k, matrix, square):
            b = next_bank()
            for k in range(n_k):
                if square:
                    act.wait(source_tokens[k], state["sq_read"])
                    token = act.counts(on.scalar.activation(blk(sq, k), blk(source, k), ACT.Square))
                    pe.wait(token)
                    piece = blk(sq, k)
                else:
                    pe.wait(source_tokens[k])
                    piece = blk(source, k)
                ins = mm(bank[b][:, 0:T], matrix, piece, k == 0, k == n_k - 1)
            done = pe.counts(ins)
            if square:
                state["sq_read"] = done
            return b, done

        def reciprocal_std(b, done, n, eps):
            act.wait(done, dve.now())
            t = act.counts(on.scalar.activation(std[:, :], bank[b][:, 0:T], ACT.Sqrt, bias=con(eps), scale=1.0 / n))
            free[b] = t
            dve.wait(t)
            return dve.counts(on.vector.reciprocal(rstd[:, :], std[:, :]))

        def rms_norm(x_tokens, gain, first, split=True):
            b, done = feature_mean(x_tokens, x, KT, ones, True)
            r = reciprocal_std(b, done, D, "eps_rms")
            dve.wait(r)
            tokens = [dve.counts(on.vector.scalar_tensor_tensor(
                blk(xn, k), blk(x, k), col(gain, first + k), rstd[:, :], ALU.mult, ALU.mult))
                for k in range(KT)]
            if split:
                tokens = [split_block(source, k, blk(xn, k), tokens[k]) for k in range(KT)]
            return tokens

        def layer_norm(z, z_tokens, n_k, write):
            b, done = feature_mean(z_tokens, z, n_k, ones, False)
            act.wait(done, dve.now())
            t = act.counts(on.scalar.mul(mean[:, :], bank[b][:, 0:T], 1.0 / (n_k * P)))
            free[b] = t
            dve.wait(t)
            centred = [dve.counts(on.vector.tensor_tensor(blk(z, k), blk(z, k), mean[:, :], ALU.subtract))
                       for k in range(n_k)]
            b, done = feature_mean(centred, z, n_k, ones, True)
            r = reciprocal_std(b, done, n_k * P, "eps_ln")
            dve.wait(r)
            return [write(k) for k in range(n_k)]

        h_read = [None, None]

        def down(name, i, h_half, h_tokens, first, last):
            done = [None] * 4
            for b in range(2):
                w = take_half(name, i, b)
                pe.wait(h_tokens[b])
                for c in range(KT):
                    start = first and b == 0 and c % 2 == 0
                    if start:
                        pe.wait(free[c // 2])
                    at = (2 * h_half + b) * T
                    ins = mm3(bank[c // 2][:, (c % 2) * T:(c % 2 + 1) * T], w, slice(c * P, (c + 1) * P),
                              hidden, slice(at, at + T), start, last and b == 1, True)
                    if last and b == 1 and c % 2 and c < KT - 1:
                        done[c // 2] = pe.counts(ins)
                done[3] = half_read(ins)
            h_read[h_half] = done[3]
            return done

        def gated_ffn(src_tokens, names, first_unit, n_chunks, scale=None, begin=True, end=True):
            gate_name, up_name, down_name = names
            waiting = None
            for i in range(n_chunks):
                side = i % 2
                bs = [4 + 2 * side, 5 + 2 * side]
                both = [None, None]
                for part, name in ((0, gate_name), (1, up_name)):
                    for s in range(2):
                        w = take_half(name, first_unit + i, s)
                        for b in range(2):
                            if part == 0 and s == 0:
                                pe.wait(free[bs[b]])
                            for k4 in range(KT // 2):
                                k = s * KT // 2 + k4
                                pe.wait(src_tokens[k])
                                ins = mm3(bank[bs[b]][:, part * T:(part + 1) * T], w,
                                          slice(k4 * CHUNK + b * P, k4 * CHUNK + (b + 1) * P),
                                          source, slice(k * T, (k + 1) * T), k == 0, k == KT - 1, False)
                            if part == 1 and s == 1 and b == 0:
                                both[0] = pe.counts(ins)
                        token = half_read(ins)
                both[1] = token
                state["source_read"] = token
                h_tokens = []
                for b in range(2):
                    j = 2 * side + b
                    piece = blk(act_buf, j)
                    act.wait(both[b], dve_read_act[j])
                    t = act.counts(on.scalar.activation(piece, bank[bs[b]][:, 0:T], ACT.Silu))
                    dve.wait(t)
                    t = dve.counts(on.vector.tensor_tensor(piece, piece, bank[bs[b]][:, T:2 * T], ALU.mult))
                    free[bs[b]] = t
                    if scale is not None:
                        dve.wait(t)
                        t = dve.counts(on.vector.tensor_tensor(piece, piece, scale(i), ALU.mult))
                    act.wait(h_read[side])
                    t = split_block(hidden, j, piece, t)
                    dve_read_act[j] = t
                    h_tokens.append(t)
                if waiting is not None:
                    done = down(down_name, first_unit + i - 1, (i - 1) % 2, waiting, begin and i == 1, False)
                waiting = h_tokens
            return down(down_name, first_unit + n_chunks - 1, (n_chunks - 1) % 2, waiting,
                        begin and n_chunks == 1, end)

        dve_read_act = [None] * 4

        def add_residual(done, scale, base=None, dst=None):
            tokens = []
            for c in range(KT):
                dve.wait(done[c // 2])
                t = dve.counts(on.vector.scalar_tensor_tensor(
                    blk(x, c), bank[c // 2][:, (c % 2) * T:(c % 2 + 1) * T], scale, blk(x, c),
                    ALU.mult, ALU.add))
                free[c // 2] = t
                tokens.append(t)
            return tokens

        def project_raw(name, i, src, src_tokens):
            n, w = take(name, i)
            b = next_bank()
            for j in range(2):
                for k in range(KT):
                    pe.wait(src_tokens[k])
                    ins = mm(bank[b][:, j * T:(j + 1) * T], w[:, k * CHUNK + j * P:k * CHUNK + (j + 1) * P],
                             blk(src, k), k == 0, k == KT - 1)
            done = pe.counts(ins)
            give_back(n, done)
            return b, done

        def project_T(name, i, src_tokens, tokens_first=False):
            b = next_bank()
            for s in range(2):
                w = take_half(name, i, s)
                for j in range(2):
                    for k4 in range(KT // 2):
                        k = s * KT // 2 + k4
                        pe.wait(src_tokens[k])
                        at = slice(k4 * CHUNK + j * P, k4 * CHUNK + (j + 1) * P)
                        src_at = slice(k * T, (k + 1) * T)
                        if tokens_first:
                            at = slice(k4 * CHUNK, (k4 + 1) * CHUNK)
                            src_at = slice(k * T + j * P, k * T + (j + 1) * P)
                        ins = mm3(bank[b][:, j * T:(j + 1) * T], w, at, source, src_at,
                                  k == 0 and j == 0, k == KT - 1, True, tokens_first)
                done = half_read(ins)
            state["source_read"] = done
            return b, done

        def row_product(name, i, pair, first_block, tokens, first, last):
            for s in range(2):
                w = take_half(name, i, s)
                pe.wait(tokens[s])
                for c in range(KT):
                    start = first and s == 0 and c % 2 == 0
                    if start:
                        pe.wait(free[c // 2])
                    at = (first_block + s) * T
                    ins = mm3(bank[c // 2][:, (c % 2) * T:(c % 2 + 1) * T], w, slice(c * P, (c + 1) * P),
                              pair, slice(at, at + T), start, last and s == 1, True)
                done = half_read(ins)
            return done

        def attention(src_tokens, x_tokens):
            A = KT * T
            Q, K, V = arena[:, 0:A], arena[:, A:2 * A], arena[:, 2 * A:3 * A]
            bias = arena[:, 3 * A:3 * A + GROUP_HEADS * N_GROUPS * N_LOGIT]
            at = 3 * A + GROUP_HEADS * N_GROUPS * N_LOGIT
            dmask = arena[:, at:at + N_GROUPS * N_LOGIT]
            at += N_GROUPS * N_LOGIT
            smask = arena[:, at:at + N_LOGIT]
            at += N_LOGIT
            merged = arena[:, at:at + 4 * T]
            at += 4 * T
            work = arena[:, at:ARENA]
            act.wait(pe.now(), dve.now(), act.now(), pool.now())
            bias_in = load_small(act, bias, dram["rel_bias"])
            dmask_in = load_small(act, dmask, dram["dilated_mask"])
            smask_in = load_small(act, smask, dram["stick_mask"])
            pool.wait(smask_in)
            for j in range(GROUP_HEADS):
                w3 = N_GROUPS * N_LOGIT
                bias_ready = pool.counts(nc.gpsimd.tensor_tensor(
                    bias[:, j * w3:(j + 1) * w3], bias[:, j * w3:(j + 1) * w3], dmask, ALU.add))
            ready = {}

            def to_sbuf(tile, block, b, done):
                act.wait(done)
                t = act.counts(on.scalar.copy(tile[:, block * T:(block + 2) * T], bank[b][:, :]))
                free[b] = t
                return t

            def v_unit(i, block):
                b, done = project_T("attn_w_in", i, src_tokens, True)
                act.wait(done)
                for tt in range(TT):
                    t = act.counts(on.scalar.copy(V[:, tt * D + block * T:tt * D + (block + 1) * T],
                                                  bank[b][:, tt * T:(tt + 1) * T]))
                free[b] = t
                return t

            norm_at = [0]

            def head_norm(tile, block, token, gain):
                i = norm_at[0] % 2
                norm_at[0] += 1
                s_b, s_s = work[:, i * T:(i + 1) * T], work[:, (2 + i) * T:(3 + i) * T]
                s_r = work[:, (4 + i) * T:(5 + i) * T]
                dve.wait(token, norm_read[i])
                piece = blk(tile, block)
                t = dve.counts(on.vector.tensor_tensor(s_b, piece, piece, ALU.mult))
                b = next_bank()
                pe.wait(t)
                done = pe.counts(mm(bank[b][:, 0:T], head_ones, s_b, True, True))
                norm_read[i] = done
                act.wait(done, dve.now())
                t = act.counts(on.scalar.activation(s_s, bank[b][:, 0:T], ACT.Sqrt, bias=con("eps_rms"),
                                                    scale=1.0 / HEAD))
                free[b] = t
                dve.wait(t)
                t = dve.counts(on.vector.reciprocal(s_r, s_s))
                dve.wait(t)
                return dve.counts(on.vector.scalar_tensor_tensor(piece, piece, col(gain), s_r,
                                                                 ALU.mult, ALU.mult))

            norm_read = [None, None]
            b, done = project_T("attn_w_in", 0, src_tokens)
            sq_ready = to_sbuf(Q, 0, b, done)
            b, done = project_T("attn_w_in", 1, src_tokens)
            sk_ready = to_sbuf(K, 0, b, done)
            sv_ready = v_unit(2, 0)
            raw = {}
            for i in range(3):
                b, done = project_T("attn_w_in", 3 + i, src_tokens)
                raw["q", i] = to_sbuf(Q, 2 + 2 * i, b, done)
            for i in range(3):
                b, done = project_T("attn_w_in", 6 + i, src_tokens)
                raw["k", i] = to_sbuf(K, 2 + 2 * i, b, done)
                for j in range(2):
                    ready["q", 2 * i + j] = head_norm(Q, 2 + 2 * i + j, raw["q", i], "attn_q_norm")
            for i in range(3):
                dv_ready = v_unit(9 + i, 1 + i)
                for j in range(2):
                    ready["k", 2 * i + j] = head_norm(K, 2 + 2 * i + j, raw["k", i], "attn_k_norm")

            LW = N_LOGIT
            sw = [work[:, 6 * T + i * 4 * LW:6 * T + (i + 1) * 4 * LW] for i in range(2)]
            sw_read = [None, None]
            merged_tokens = []
            for h in range(SB_HEADS):
                rows = slice(HEAD * (h % 2), HEAD * (h % 2) + HEAD)
                block = h // 2
                w4 = sw[h % 2]
                absz, soft, lead, wt = (w4[:, i * LW:(i + 1) * LW] for i in range(4))
                q_all = Q[rows, block * T:(block + 1) * T]
                b = next_bank()
                pe.wait(sq_ready, sk_ready)
                mm(bank[b][:, 0:T], K[rows, block * T:block * T + P], q_all, True, True)
                done = pe.counts(mm(bank[b][:, T:LW], K[rows, block * T + P:(block + 1) * T],
                                    Q[rows, block * T + P:(block + 1) * T], True, True))
                act.wait(done, sw_read[h % 2])
                z = bank[b][:, 0:LW]
                t = act.counts(on.scalar.activation(absz, z, ACT.Abs, scale=SCALE))
                act.wait(t)
                t = act.counts(on.scalar.activation(absz, absz, ACT.Exp, scale=-1.0))
                act.wait(t)
                t = act.counts(on.scalar.activation(absz, absz, ACT.Ln, bias=con("one"), scale=1.0))
                dve.wait(t, smask_in)
                t1 = dve.counts(on.vector.tensor_scalar(soft, z, SCALE, 0.0, ALU.mult, ALU.max))
                t2 = dve.counts(on.vector.tensor_scalar(lead, z, SCALE, 0.0, ALU.mult, ALU.min))
                free[b] = t2
                dve.wait(t2)
                t1 = dve.counts(on.vector.tensor_tensor(soft, soft, absz, ALU.add))
                t2 = dve.counts(on.vector.tensor_tensor(lead, lead, absz, ALU.subtract))
                dve.wait(t1)
                t = dve.counts(on.vector.tensor_tensor(soft, soft, smask, ALU.mult))
                b = next_bank()
                pe.wait(t)
                mm(bank[b][:, 0:T], later, soft[:, 0:T], True, True, True)
                mm(bank[b][:, P:T], ones, soft[:, T:LW], False, True, True)
                done = pe.counts(mm(bank[b][:, T:LW], later, soft[:, T:LW], False, True, True))
                dve.wait(done, t2)
                t = dve.counts(on.vector.tensor_tensor(lead, lead, bank[b][:, 0:LW], ALU.subtract))
                free[b] = t
                act.wait(t)
                t = act.counts(on.scalar.activation(wt, lead, ACT.Exp))
                dve.wait(t)
                t = dve.counts(on.vector.tensor_tensor(wt, wt, smask, ALU.mult))
                b = next_bank()
                pe.wait(t, sv_ready)
                o = bank[b][rows, 0:T]
                mm(o, V[:, h * HEAD:(h + 1) * HEAD], wt[:, 0:T], True, False, True)
                done = pe.counts(mm(bank[b][rows, P:T], V[:, D + h * HEAD:D + (h + 1) * HEAD], wt[:, T:LW],
                                    False, True, True))
                sw_read[h % 2] = done
                act.wait(done)
                t = act.counts(on.scalar.copy(merged[rows, block * T:(block + 1) * T], o))
                free[b] = t
                merged_tokens.append(t)

            base = 6 * T + 8 * LW
            W3 = N_GROUPS * T
            for j in range(GROUP_HEADS):
                rows = slice(HEAD * (j % 2), HEAD * (j % 2) + HEAD)
                ob = (0, 1)[j % 2]
                o_bank = bank[ob]
                for tt in range(TT):
                    s = (2 * j + tt) % 2
                    lw = work[:, base + s * W3:base + (s + 1) * W3]
                    pt = work[:, base + (2 + s) * W3:base + (3 + s) * W3]
                    small = work[:, base + 4 * W3 + 4 * s:base + 4 * W3 + 4 * (s + 1)]
                    n_keys = P * (tt + 1)
                    width = N_GROUPS * n_keys
                    where, banks = [], []
                    for g in range(N_GROUPS):
                        if g == 0 or (tt == 1 and g == 2):
                            banks.append(next_bank())
                            at0 = 0
                        where.append((banks[-1], at0))
                        at0 += n_keys
                    done = []
                    for g in range(N_GROUPS):
                        blk_i = 2 + (GROUP_HEADS * g + j) // 2
                        pe.wait(ready["q", blk_i - 2], ready["k", blk_i - 2])
                        b, a0 = where[g]
                        ins = mm(bank[b][:, a0:a0 + n_keys], Q[rows, blk_i * T + tt * P:blk_i * T + (tt + 1) * P],
                                 K[rows, blk_i * T:blk_i * T + n_keys], True, True)
                    done = pe.counts(ins)
                    dve.wait(done, bias_ready, dil_read[s])
                    off = (j * N_GROUPS * N_LOGIT) + (0 if tt == 0 else N_GROUPS * P)
                    if tt == 0:
                        parts = [(banks[0], 0, width)]
                    else:
                        parts = [(banks[0], 0, 2 * n_keys), (banks[1], 2 * n_keys, n_keys)]
                    for b, a0, n_c in parts:
                        t = dve.counts(on.vector.scalar_tensor_tensor(
                            lw[:, a0:a0 + n_c], bank[b][:, 0:n_c], SCALE, bias[:, off + a0:off + a0 + n_c],
                            ALU.mult, ALU.add))
                        free[b] = t
                    dve.wait(t)
                    t = dve.counts(on.vector.tensor_reduce(small[:, 0:1], lw[:, 0:width], AX_X, ALU.max))
                    dve.wait(t)
                    t = dve.counts(on.vector.tensor_scalar(small[:, 1:2], small[:, 0:1], -1.0, None, ALU.mult))
                    act.wait(t)
                    t = act.counts(on.scalar.activation(lw[:, 0:width], lw[:, 0:width], ACT.Exp,
                                                        bias=small[:, 1:2], scale=1.0, accum_out=small[:, 2:3]))
                    dve.wait(t)
                    t = dve.counts(on.vector.reciprocal(small[:, 3:4], small[:, 2:3]))
                    dve.wait(t)
                    t = dve.counts(on.vector.tensor_scalar(lw[:, 0:width], lw[:, 0:width], small[:, 3:4], None,
                                                           ALU.mult))
                    pe.wait(t)
                    n_piece = N_GROUPS * (tt + 1)
                    for p0 in range(0, n_piece, 4):
                        b = next_bank()
                        m = min(4, n_piece - p0)
                        for i in range(m):
                            ins = on.tensor.transpose(bank[b][:, i * P:(i + 1) * P],
                                                      lw[:, (p0 + i) * P:(p0 + i + 1) * P], ident)
                        done = pe.counts(ins)
                        act.wait(done)
                        t = act.counts(on.scalar.copy(pt[:, p0 * P:(p0 + m) * P], bank[b][:, 0:m * P]))
                        free[b] = t
                    pe.wait(t, dv_ready)
                    if tt == 0:
                        pe.wait(free[ob])
                    for i in range(n_piece):
                        g, s_tile = i // (tt + 1), i % (tt + 1)
                        head = SB_HEADS + GROUP_HEADS * g + j
                        ins = mm(o_bank[rows, tt * P:(tt + 1) * P],
                                 V[:, s_tile * D + head * HEAD:s_tile * D + (head + 1) * HEAD],
                                 pt[:, i * P:(i + 1) * P], i == 0, i == n_piece - 1)
                    done = pe.counts(ins)
                    dil_read[s] = done
                block = 2 + j // 2
                act.wait(done)
                t = act.counts(on.scalar.copy(merged[rows, block * T:(block + 1) * T], o_bank[rows, 0:T]))
                free[ob] = t
                merged_tokens.append(t)

            m_tok = [split_block(source, k, blk(merged, k), merged_tokens[2 * k + 1]) for k in range(4)]
            for u in range(2):
                done = row_product("attn_w_out", u, source, 2 * u, m_tok[2 * u:2 * u + 2], u == 0, u == 1)
            state["source_read"] = done
            return add_residual([done] * 4, 1.0)

        dil_read = [None, None]

        def rwkv(h_tokens):
            A = KT * T
            r, kx, v, ld, a, g = (arena[:, i * A:(i + 1) * A] for i in range(6))
            xx = arena[:, 6 * A:7 * A]
            xm = [arena[:, 7 * A:8 * A], arena[:, 8 * A:9 * A]]
            lora = arena[:, 9 * A:9 * A + 4 * T]
            masks = arena[:, ARENA - 11 * P:ARENA]
            act.wait(pe.now(), dve.now(), act.now(), pool.now())
            masks_in = load_small(act, masks, dram["rwkv_masks"])

            h3 = xn[:, :].rearrange("p (k t) -> p k t", k=KT)
            xx3 = xx.rearrange("p (k t) -> p k t", k=KT)
            dve.wait(*h_tokens)
            dve.wait(pe.now(), act.now())
            t1 = dve.counts(on.vector.tensor_tensor(xx3[:, :, 1:T], h3[:, :, 0:T - 1], h3[:, :, 1:T], ALU.subtract))
            t2 = dve.counts(on.vector.tensor_scalar(xx3[:, :, 0:1], h3[:, :, 0:1], -1.0, None, ALU.mult))
            dve.wait(t1, t2)
            xm_read = [None, None]

            def mixed(which, i):
                dve.wait(xm_read[i])
                return [dve.counts(on.vector.scalar_tensor_tensor(
                    blk(xm[i], k), blk(xx, k), col("rw_mix", which * KT + k), blk(xn, k), ALU.mult, ALU.add))
                    for k in range(KT)]

            def full(name, i, tokens, dst):
                for u in range(4):
                    b, done = project_raw(name, u, xm[i], tokens)
                    act.wait(done)
                    t = act.counts(on.scalar.copy(dst[:, 2 * u * T:(2 * u + 2) * T], bank[b][:, :]))
                    free[b] = t
                xm_read[i] = done
                return t

            tok = mixed(0, 0)
            tok_k = mixed(2, 1)
            r_ready = full("rw_wr", 0, tok, r)
            tok = mixed(3, 0)
            k_ready = full("rw_wk", 1, tok_k, kx)
            tok_w = mixed(1, 1)
            v_ready = full("rw_wv", 0, tok, v)
            tok_a = mixed(4, 0)
            n_in, w_in = take("lora_in", 0, P, 2 * KT * HEAD)
            n_out, w_out = take("lora_out", 0, HEAD, 2 * D)
            lt = {}
            for i, (tokens, src, func) in enumerate(((tok_w, xm[1], ACT.Tanh), (tok_a, xm[0], ACT.Copy))):
                b = next_bank()
                for k in range(KT):
                    pe.wait(tokens[k])
                    ins = mm(bank[b][0:HEAD, 0:T], w_in[:, (i * KT + k) * HEAD:(i * KT + k + 1) * HEAD],
                             blk(src, k), k == 0, k == KT - 1)
                done = pe.counts(ins)
                xm_read[1 - i] = done
                act.wait(done)
                t = act.counts(on.scalar.activation(lora[0:HEAD, i * T:(i + 1) * T], bank[b][0:HEAD, 0:T], func))
                free[b] = t
                lt[i] = t
            give_back(n_in, done)
            tok_g = mixed(5, 1)
            for i, (dst, offset) in enumerate(((ld, "rw_w0"), (a, "rw_a0"))):
                pe.wait(lt[i])
                for c in range(0, KT, 2):
                    b = next_bank()
                    for j in range(2):
                        ins = mm(bank[b][:, j * T:(j + 1) * T],
                                 w_out[:, i * D + (c + j) * P:i * D + (c + j + 1) * P],
                                 lora[0:HEAD, i * T:(i + 1) * T], True, True)
                    done = pe.counts(ins)
                    act.wait(done)
                    for j in range(2):
                        t = act.counts(on.scalar.activation(blk(dst, c + j), bank[b][:, j * T:(j + 1) * T],
                                                            ACT.Sigmoid, bias=col(offset, c + j), scale=1.0))
                    free[b] = t
            give_back(n_out, done)
            da_ready = t
            b, done = project_raw("gate_in", 0, xm[1], tok_g)
            act.wait(done)
            t = act.counts(on.scalar.activation(lora[:, 2 * T:4 * T], bank[b][:, :], ACT.Sigmoid))
            free[b] = t
            n, w = take("gate_out", 0)
            pe.wait(t)
            for c in range(0, KT, 2):
                b = next_bank()
                for j in range(2):
                    for i in range(2):
                        ins = mm(bank[b][:, j * T:(j + 1) * T],
                                 w[:, i * D + (c + j) * P:i * D + (c + j + 1) * P],
                                 lora[:, (2 + i) * T:(3 + i) * T], i == 0, i == 1)
                done = pe.counts(ins)
                act.wait(done)
                t = act.counts(on.scalar.copy(g[:, c * T:(c + 2) * T], bank[b][:, :]))
                free[b] = t
            give_back(n, done)
            g_ready = t

            for e in (pe, dve, act, pool):
                e.wait(pe.now(), dve.now(), act.now(), pool.now(), masks_in)
            y_out = r
            slot_cols = (ARENA - 11 * P - 6 * A) // 2
            elsewhere = {"Ti": (xn, 0), "TiT": (xn, T), "X": (xn, 2 * T), "BH": (xn, 3 * T), "sc": (sq, 0)}
            names = [("kk", T), ("tmp", T), ("bonus", T), ("cum", T), ("grow", T), ("ar", 2 * T), ("bt", T),
                     ("kt", T), ("hat", T), ("BH", T), ("KH", T), ("VN", T), ("sc", 4 * T), ("lev", 5 * T),
                     ("Ti", T), ("TiT", T), ("X", T), ("Xs", P), ("U", P), ("S", P), ("WC", 4)]
            assert sum(n for name, n in names if name not in elsewhere) <= slot_cols
            final = [None] * KT

            def pair(kt, slot):
                at = 6 * A + slot * slot_cols
                buf = {}
                for name, n in names:
                    if name in elsewhere:
                        home, offset = elsewhere[name]
                        offset += slot * 4 * T
                        buf[name] = home[:, offset:offset + n]
                        continue
                    buf[name] = arena[:, at:at + n]
                    at += n
                b0, b1, b2, b3 = (4 * slot + i for i in range(4))
                rT, kT, vT, dT, aT = (blk(z, kt) for z in (r, kx, v, ld, a))
                kk, tmp, bonus, cum, grow = (buf[z] for z in ("kk", "tmp", "bonus", "cum", "grow"))
                ar = buf["ar"].rearrange("p (s w t) -> p s w t", s=TT, w=2)
                bt, kt_, hat = buf["bt"], buf["kt"], buf["hat"]

                def V(ins):
                    t = dve.counts(ins)
                    dve.wait(t)
                    return t

                def halves(z):
                    return z.rearrange("p (s t) -> p s t", s=TT)

                V(on.vector.tensor_scalar(kk, kT, col("rw_kk", kt), None, ALU.mult))
                t = V(on.vector.tensor_tensor(tmp, kk, kk, ALU.mult))
                pe.wait(t, free[b0])
                done = pe.counts(mm(bank[b0][:, 0:T], head_ones, tmp, True, True))
                yield
                act.wait(done)
                t = act.counts(on.scalar.activation(hat, bank[b0][:, 0:T], ACT.Sqrt))
                free[b0] = t
                V(on.vector.tensor_scalar(dT, dT, DECAY_SCALE, None, ALU.mult))
                t_cum = V(on.vector.tensor_tensor_scan(cum, con("restart"), dT, 0.0, ALU.mult, ALU.add))
                V(on.vector.tensor_tensor(dT, cum, dT, ALU.subtract))
                dve.wait(t)
                V(on.vector.tensor_scalar(hat, hat, 1e-12, None, ALU.max))
                V(on.vector.reciprocal(hat, hat))
                t_kk = V(on.vector.tensor_tensor(kk, kk, hat, ALU.mult))
                act.wait(dve.now())
                t_grow = act.counts(on.scalar.activation(grow, cum, ACT.Exp))
                t_prev = act.counts(on.scalar.activation(dT, dT, ACT.Exp))
                t_shrink = act.counts(on.scalar.activation(cum, cum, ACT.Exp, scale=-1.0))
                yield
                V(on.vector.tensor_scalar(tmp, aT, -1.0, col("rw_ka", kt), ALU.add, ALU.mult))
                V(on.vector.scalar_tensor_tensor(kT, tmp, 1.0, kT, ALU.add, ALU.mult))
                V(on.vector.tensor_tensor(aT, kk, aT, ALU.mult))
                V(on.vector.scalar_tensor_tensor(tmp, rT, col("rw_rk", kt), kT, ALU.mult, ALU.mult))
                pe.wait(dve.now(), free[b1])
                done = pe.counts(mm(bank[b1][:, 0:T], head_ones, tmp, True, True))
                pe.wait(free[b2])
                for s in range(TT):
                    ins = on.tensor.transpose(bank[b2][:, s * P:(s + 1) * P], vT[:, s * P:(s + 1) * P], ident)
                v_done = pe.counts(ins)
                yield
                dve.wait(done)
                t = V(on.vector.tensor_tensor(bonus, bank[b1][:, 0:T], vT, ALU.mult))
                free[b1] = t
                act.wait(v_done)
                t_vn = act.counts(on.scalar.copy(buf["VN"], bank[b2][:, 0:T]))
                free[b2] = t_vn
                dve.wait(t_grow, t_prev, t_shrink)
                dve.counts(on.vector.scalar_tensor_tensor(ar[:, :, 0, :], halves(kk), -1.0, halves(dT),
                                                          ALU.mult, ALU.mult))
                dve.counts(on.vector.tensor_tensor(ar[:, :, 1, :], halves(rT), halves(grow), ALU.mult))
                dve.counts(on.vector.tensor_tensor(bt, aT, cum, ALU.mult))
                t = V(on.vector.tensor_tensor(kt_, kT, cum, ALU.mult))
                t_ops = t
                WC = buf["WC"]
                V(on.vector.tensor_copy(WC, grow[:, RW_CHUNK - 1:T:RW_CHUNK]))
                wc_b = WC.rearrange("p (c o) -> p c o", o=1).to_broadcast([P, T // RW_CHUNK, RW_CHUNK])
                for src, dst in ((bt, "BH"), (kt_, "KH")):
                    t = V(on.vector.tensor_tensor(hat.rearrange("p (c t) -> p c t", t=RW_CHUNK),
                                                  src.rearrange("p (c t) -> p c t", t=RW_CHUNK), wc_b, ALU.mult))
                    pe.wait(t, free[b2])
                    for s in range(TT):
                        ins = on.tensor.transpose(bank[b2][:, s * P:(s + 1) * P], hat[:, s * P:(s + 1) * P], ident)
                    done = pe.counts(ins)
                    yield
                    act.wait(done)
                    t_nat = act.counts(on.scalar.copy(buf[dst], bank[b2][:, 0:T]))
                    free[b2] = t_nat
                    dve.wait(done)
                S = buf["S"]
                t_S = V(on.vector.memset(S, 0.0))
                yv = tmp
                sc = buf["sc"]
                for s in range(TT):
                    cols = slice(s * P, (s + 1) * P)
                    for p in range(2):
                        rows = slice(p * HEAD, (p + 1) * HEAD)
                        pe.wait(t_ops, free[(b0, b1)[p]])
                        arr = ar[rows, s, :, :].rearrange("p w t -> p (w t)")
                        mm(bank[(b0, b1)[p]][:, 0:T], bt[rows, cols], arr, True, True)
                        done = pe.counts(mm(bank[(b0, b1)[p]][:, T:2 * T], kt_[rows, cols], arr, True, True))
                        yield
                        dve.wait(done, pe_tile_read[slot])
                        t = dve.counts(on.vector.tensor_tensor(sc[:, p * 512:(p + 1) * 512],
                                                               bank[(b0, b1)[p]][:, :], masks[:, 0:512], ALU.mult))
                        free[(b0, b1)[p]] = t
                    dve.wait(t)
                    sc4 = sc.rearrange("p (h w t) -> p h w t", h=2, w=4)
                    MabT, MrbT = (sc4[:, :, i, :] for i in (0, 1))
                    Ti = buf["Ti"].rearrange("p (h t) -> p h t", h=2)
                    TiT = buf["TiT"].rearrange("p (h t) -> p h t", h=2)
                    X = buf["X"].rearrange("p (h t) -> p h t", h=2)
                    lev = buf["lev"].rearrange("p (l h t) -> p l h t", l=5, h=2)
                    pool.wait(t, pe_tile_read[slot])
                    lev_ready = []
                    for li in range(5):
                        m_b = masks[:, (5 + li) * P:(6 + li) * P].rearrange("p (o t) -> p o t", o=1)\
                            .to_broadcast([P, 2, P])
                        lev_ready.append(pool.counts(nc.gpsimd.tensor_tensor(lev[:, li, :, :], MabT, m_b, ALU.mult)))
                    pe.wait(t, free[b2])
                    for h in range(2):
                        ins = on.tensor.transpose(bank[b2][:, h * P:(h + 1) * P], MabT[:, h, :], ident)
                    done = pe.counts(ins)
                    m1T = masks[:, 4 * P:5 * P].rearrange("p (o t) -> p o t", o=1).to_broadcast([P, 2, P])
                    m1 = masks[:, 10 * P:11 * P].rearrange("p (o t) -> p o t", o=1).to_broadcast([P, 2, P])
                    id_b = ident.rearrange("p (o t) -> p o t", o=1).to_broadcast([P, 2, P])
                    V(on.vector.tensor_tensor(TiT, MabT, m1T, ALU.mult))
                    t_tt = V(on.vector.tensor_tensor(TiT, TiT, id_b, ALU.add))
                    yield
                    dve.wait(done)
                    t = V(on.vector.tensor_tensor(Ti, bank[b2][:, 0:T].rearrange("p (h t) -> p h t", h=2), m1,
                                                  ALU.mult))
                    free[b2] = t
                    t_t = V(on.vector.tensor_tensor(Ti, Ti, id_b, ALU.add))
                    for li in range(5):
                        pe.wait(t_t, t_tt, lev_ready[li], free[b2])
                        for h in range(2):
                            ins = mm(bank[b2][:, h * P:(h + 1) * P], lev[:, li, h, :], Ti[:, h, :], True, True)
                        done = pe.counts(ins)
                        yield
                        act.wait(done)
                        t_x = act.counts(on.scalar.copy(buf["X"], bank[b2][:, 0:T]))
                        free[b2] = t_x
                        pe.wait(t_x)
                        pe.wait(free[b1])
                        for h in range(2):
                            ins = mm(bank[b1][:, h * P:(h + 1) * P], X[:, h, :], TiT[:, h, :], True, True)
                        done_tt = pe.counts(ins)
                        if li < 4:
                            pe.wait(free[b0])
                            for h in range(2):
                                ins = mm(bank[b0][:, h * P:(h + 1) * P], TiT[:, h, :], X[:, h, :], True, True)
                            done_t = pe.counts(ins)
                        else:
                            done_t = done_tt
                        yield
                        dve.wait(done_t, done_tt)
                        t_tt = dve.counts(on.vector.tensor_tensor(buf["TiT"], buf["TiT"], bank[b1][:, 0:T], ALU.add))
                        free[b1] = t_tt
                        if li < 4:
                            t_t = dve.counts(on.vector.tensor_tensor(buf["Ti"], buf["Ti"], bank[b0][:, 0:T],
                                                                     ALU.add))
                            free[b0] = t_t
                        dve.wait(t_tt, t_t)
                    VN = buf["VN"][:, cols]
                    Xs, U = buf["Xs"], buf["U"]
                    pe.wait(t_vn, free[b2])
                    for h in range(2):
                        ins = mm(bank[b2][:, h * HEAD:(h + 1) * HEAD], sc4[:, h, 2, :],
                                 VN[:, h * HEAD:(h + 1) * HEAD], True, True)
                    done = pe.counts(ins)
                    yield
                    act.wait(done)
                    t_xs = act.counts(on.scalar.copy(Xs, bank[b2][:, 0:P]))
                    free[b2] = t_xs
                    pe.wait(free[b3])
                    for c in range(2):
                        rc = slice(c * RW_CHUNK, (c + 1) * RW_CHUNK)
                        pe.wait(t_S, free[b2])
                        mm(bank[b3][:, rc], S, ar[:, s, 1, rc], c == 0, True, True)
                        done = pe.counts(mm(bank[b2][:, 0:P], ar[:, s, 0, :], S, True, True))
                        yield
                        dve.wait(done, t_xs)
                        t = dve.counts(on.vector.tensor_tensor(Xs[rc, :], bank[b2][rc, 0:P], Xs[rc, :], ALU.add))
                        free[b2] = t
                        pe.wait(t, t_tt, free[b1])
                        for h in range(2):
                            ins = mm(bank[b1][:, h * HEAD:(h + 1) * HEAD], TiT[:, h, :],
                                     Xs[:, h * HEAD:(h + 1) * HEAD], True, True)
                        done_u = pe.counts(ins)
                        yield
                        act.wait(done_u)
                        t_u = act.counts(on.scalar.copy(U[rc, :], bank[b1][rc, 0:P]))
                        free[b1] = t_u
                        pe.wait(t_u, t_nat, free[b2])
                        mm(bank[b2][:, 0:P], buf["BH"][rc, cols], U[rc, :], True, False)
                        done = pe.counts(mm(bank[b2][:, 0:P], buf["KH"][rc, cols], VN[rc, :], False, True))
                        yield
                        dve.wait(done)
                        for h in range(2):
                            hs = slice(h * HEAD, (h + 1) * HEAD)
                            t_S = dve.counts(on.vector.scalar_tensor_tensor(
                                S[hs, hs], S[hs, hs], WC[hs, 2 * s + c:2 * s + c + 1], bank[b2][hs, hs],
                                ALU.mult, ALU.add))
                        free[b2] = t_S
                        dve.wait(t_S)
                    for h in range(2):
                        hs = slice(h * HEAD, (h + 1) * HEAD)
                        mm(bank[b3][hs, 0:P], U[:, hs], sc4[:, h, 1, :], False, True, True)
                        done = mm(bank[b3][hs, 0:P], VN[:, hs], sc4[:, h, 3, :], False, True, True)
                    done = pe.counts(done)
                    pe_tile_read[slot] = done
                    yield
                    act.wait(done)
                    t_y = act.counts(on.scalar.copy(yv[:, cols], bank[b3][:, 0:P]))
                    free[b3] = t_y
                pe.wait(t_y, free[b0])
                done = pe.counts(mm(bank[b0][:, 0:T], head_ones, yv, True, True))
                yield
                dve.wait(done, t_y)
                t = V(on.vector.scalar_tensor_tensor(yv, bank[b0][:, 0:T], -1.0 / HEAD, yv, ALU.mult, ALU.add))
                free[b0] = t
                t = V(on.vector.tensor_tensor(kk, yv, yv, ALU.mult))
                pe.wait(t, free[b1])
                done = pe.counts(mm(bank[b1][:, 0:T], head_ones, kk, True, True))
                yield
                act.wait(done)
                t = act.counts(on.scalar.activation(hat, bank[b1][:, 0:T], ACT.Sqrt, bias=con("eps_gn"),
                                                    scale=1.0 / HEAD))
                free[b1] = t
                dve.wait(t)
                V(on.vector.reciprocal(hat, hat))
                V(on.vector.scalar_tensor_tensor(yv, yv, col("rw_lnx_g", kt), hat, ALU.mult, ALU.mult))
                V(on.vector.scalar_tensor_tensor(yv, yv, col("rw_lnx_b", kt), bonus, ALU.add, ALU.add))
                final[kt] = V(on.vector.tensor_tensor(blk(y_out, kt), yv, blk(g, kt), ALU.mult))

            pe_tile_read = [None, None]
            queue = list(range(KT))
            running = {}
            while queue or running:
                for slot in range(2):
                    if slot not in running and queue:
                        running[slot] = pair(queue.pop(0), slot)
                    if slot in running and next(running[slot], "end") == "end":
                        del running[slot]
            act.wait(pe.now(), dve.now(), act.now(), pool.now())
            tokens = []
            for u in range(4):
                b, done = project_raw("rw_wo", u, y_out, final)
                for j in range(2):
                    dve.wait(done)
                    t = dve.counts(on.vector.tensor_tensor(blk(x, 2 * u + j), blk(x, 2 * u + j),
                                                           bank[b][:, j * T:(j + 1) * T], ALU.add))
                    tokens.append(t)
                free[b] = t
            return tokens

        def pool_conv_mixer(layer, x_tokens):
            A = KT * T
            UP = T + PAD_POOL
            VP = T + PAD_CONV
            at = [0]

            def piece(n):
                at[0] += n
                return arena[:, at[0] - n:at[0]]

            up, s_a, s_b = piece(4 * UP), piece(4 * UP), piece(4 * UP)
            vp, val = piece(4 * VP), piece(4 * T)
            y = piece(4 * T)
            cat = piece(A)
            inv = piece(4 * T)
            dd = piece(4 * T)
            z = piece(A)
            gate = piece(4 * T)
            act.wait(pe.now(), dve.now(), act.now(), pool.now())
            inv_in = load_small(act, inv, dram["inverse_count"])
            up3, a3, b3 = (q.rearrange("p (g t) -> p g t", g=4) for q in (up, s_a, s_b))
            vp3 = vp.rearrange("p (g t) -> p g t", g=4)
            pool.wait(pe.now(), dve.now(), act.now())
            for q in (up3, a3, b3):
                zeroed = pool.counts(nc.gpsimd.memset(q[:, :, 0:PAD_POOL], 0.0))
            zeroed = pool.counts(nc.gpsimd.memset(vp3[:, :, 0:PAD_CONV], 0.0))
            w_in = "w_in_2"
            for u in range(2):
                b, done = project_T(w_in, 6 * layer + 2 + u, x_tokens)
                act.wait(done)
                t_val = act.counts(on.scalar.copy(val[:, 2 * u * T:(2 * u + 2) * T], bank[b][:, :]))
                free[b] = t_val
            v_tok = []
            for u in range(2):
                b, done = project_T(w_in, 6 * layer + 4 + u, x_tokens)
                act.wait(done)
                t = act.counts(on.scalar.activation(gate[:, 2 * u * T:(2 * u + 2) * T], bank[b][:, :], ACT.Sigmoid))
                free[b] = t
                dve.wait(t, t_val)
                for j in range(2):
                    g = 2 * u + j
                    v_tok.append(dve.counts(on.vector.tensor_tensor(vp3[:, g, PAD_CONV:VP], blk(val, g), blk(gate, g),
                                                                    ALU.mult)))
            for u in range(2):
                b, done = project_T(w_in, 6 * layer + u, x_tokens)
                act.wait(done, zeroed)
                t = act.counts(on.scalar.copy(up3[:, 2 * u:2 * u + 2, PAD_POOL:UP],
                                              bank[b][:, :].rearrange("p (g t) -> p g t", g=2)))
                free[b] = t
            pool.wait(t)
            cur, nxt = up3, a3
            spare = {0: a3, 1: b3, 2: a3, 3: b3}
            for i, w in enumerate(POOL_WINDOWS):
                half = w // 2
                dst = spare[i]
                t = pool.counts(nc.gpsimd.tensor_tensor(dst[:, i:4, PAD_POOL:UP], cur[:, i:4, PAD_POOL:UP],
                                                        cur[:, i:4, PAD_POOL - half:UP - half], ALU.add))
                pool.wait(t)
                cur = dst
            dd3, inv3 = (q.rearrange("p (g t) -> p g t", g=4) for q in (dd, inv))
            pool.wait(inv_in)
            for i in range(4):
                t = pool.counts(nc.gpsimd.tensor_tensor(dd3[:, i, :], spare[i][:, i, PAD_POOL:UP], inv3[:, i, :],
                                                        ALU.mult))
            pool.wait(t)
            t = pool.counts(nc.gpsimd.tensor_tensor(dd3, dd3, up3[:, :, PAD_POOL:UP], ALU.subtract))
            y_tok = []
            for g in range(4):
                dve.wait(v_tok[g], zeroed)
                for j in range(CONV_WIDTH):
                    wcol = col("conv_w_2", (layer * CONV_WIDTH + j) * 4 + g)
                    tap = vp3[:, g, j:j + T]
                    if j == 0:
                        q = dve.counts(on.vector.tensor_scalar(blk(y, g), tap, wcol, col("conv_b_2", layer * 4 + g),
                                                               ALU.mult, ALU.add))
                    else:
                        q = dve.counts(on.vector.scalar_tensor_tensor(blk(y, g), tap, wcol, blk(y, g), ALU.mult,
                                                                      ALU.add))
                    dve.wait(q)
                y_tok.append(q)
            n, w = take("pool_w_2", layer, P, 4 * P)
            cat_tok = [None] * KT
            pe.wait(t)
            for u in range(2):
                b = next_bank()
                for j in range(2):
                    g = 2 * u + j
                    ins = mm(bank[b][:, j * T:(j + 1) * T], w[:, g * P:(g + 1) * P], blk(dd, g), True, True)
                done = pe.counts(ins)
                act.wait(done)
                for j in range(2):
                    g = 2 * u + j
                    t = act.counts(on.scalar.activation(blk(cat, g), bank[b][:, j * T:(j + 1) * T], ACT.Copy,
                                                        scale=col("pool_scale_2", layer * 4 + g)))
                    cat_tok[g] = split_block(source, g, blk(cat, g), t)
                free[b] = t
            give_back(n, done)

            def finish(g):
                t = dve.counts(on.vector.scalar_tensor_tensor(blk(y, g), blk(y, g),
                                                              col("conv_ln_g_2", layer * 4 + g), rstd[:, :],
                                                              ALU.mult, ALU.mult))
                act.wait(t)
                t = act.counts(on.scalar.activation(blk(y, g), blk(y, g), ACT.Silu,
                                                    bias=col("conv_ln_b_2", layer * 4 + g), scale=1.0))
                return split_block(source, 4 + g, blk(y, g), t)

            y_tok = layer_norm(y, y_tok, 4, finish)
            bs = [next_bank(), next_bank()]
            for half in range(2):
                w = take_half("conv_pw_2", layer, half)
                for c in range(4):
                    for k2 in range(2):
                        k = 2 * half + k2
                        pe.wait(y_tok[k])
                        at = k2 * 512 + c * P
                        ins = mm3(bank[bs[c // 2]][:, (c % 2) * T:(c % 2 + 1) * T], w, slice(at, at + P), source,
                                  slice((4 + k) * T, (5 + k) * T), k == 0 and c % 2 == 0, k == 3, True)
                done = half_read(ins)
            state["source_read"] = done
            for u in range(2):
                t = split_block(source, 2 + u, bank[bs[u]][:, :], done, 2 * T)
                cat_tok[4 + 2 * u] = cat_tok[5 + 2 * u] = free[bs[u]] = t
            z_tok = []
            for u in range(4):
                b, done = project_T("w_out_2", 4 * layer + u, cat_tok)
                dve.wait(done)
                for j in range(2):
                    c = 2 * u + j
                    z_tok.append(dve.counts(on.vector.scalar_tensor_tensor(
                        blk(z, c), blk(x, c), ALPHA, bank[b][:, j * T:(j + 1) * T], ALU.mult, ALU.add)))
                free[b] = z_tok[-1]
            return z, z_tok

        def norm_to_x(z, z_tok, gain, bias, layer, split=True):
            def finish(k):
                t = dve.counts(on.vector.scalar_tensor_tensor(blk(z, k), blk(z, k), col(gain, layer * KT + k),
                                                              rstd[:, :], ALU.mult, ALU.mult))
                act.wait(t)
                return act.counts(on.scalar.activation(blk(x, k), blk(z, k), ACT.Identity,
                                                       bias=col(bias, layer * KT + k), scale=1.0))
            tokens = layer_norm(z, z_tok, KT, finish)
            return split_x(tokens) if split else tokens

        def split_x(tokens):
            return [split_block(source, k, blk(x, k), tokens[k]) for k in range(KT)]

        def deep_residual(done, z):
            z_tok = []
            for c in range(KT):
                dve.wait(done[c // 2])
                z_tok.append(dve.counts(on.vector.scalar_tensor_tensor(
                    blk(z, c), blk(x, c), ALPHA, bank[c // 2][:, (c % 2) * T:(c % 2 + 1) * T], ALU.mult, ALU.add)))
                free[c // 2] = z_tok[-1]
            return z_tok

        E = N_EXPERTS

        def moe(x_tokens, z):
            A = KT * T
            small = arena[:, 4096:4096 + 2 * 64]
            table = arena[:, 4224:4224 + 8 * 16]
            chosen, gates, place = (table[:, i * 16:(i + 1) * 16] for i in range(3))
            most = table[:, 48:49]
            earlier, ramp = arena[:, 6 * A:6 * A + P], arena[:, 6 * A + P:6 * A + 2 * P]
            act.wait(pe.now(), dve.now(), act.now(), pool.now())
            load_small(act, arena[:, 6 * A:6 * A + 2 * P], dram["moe_tables"])
            rows = arena[0:E, 0:E * P]
            rows_in = load_small(act, rows, dram["expert_rows"])
            at = PARAM_AT["router_w_2"]
            iota = con("iota")
            b = next_bank()
            for tt in range(TT):
                for k in range(KT):
                    pe.wait(x_tokens[k])
                    ins = mm(bank[b][:, tt * E:(tt + 1) * E], x[:, k * T + tt * P:k * T + (tt + 1) * P],
                             param[:, at + k * E:at + (k + 1) * E], k == 0, k == KT - 1)
            done = pe.counts(ins)
            dve.wait(done, pe.now(), act.now())
            for tt in range(TT):
                s = small[:, tt * 64:(tt + 1) * 64]
                lg, eq, o1, o2 = (s[:, i * 8:(i + 1) * 8] for i in range(4))
                m1, m2, i1, dif, w1, w2 = (s[:, 32 + i:33 + i] for i in range(6))
                here = slice(tt * E, (tt + 1) * E)

                def V(ins):
                    t = dve.counts(ins)
                    dve.wait(t)
                    return t

                V(on.vector.tensor_copy(lg, bank[b][:, here]))
                for m, hot in ((m1, o1), (m2, o2)):
                    V(on.vector.tensor_reduce(m, lg, AX_X, ALU.max))
                    V(on.vector.tensor_scalar(eq, lg, m, 1e9, ALU.is_lt, ALU.mult))
                    V(on.vector.tensor_tensor(eq, eq, iota, ALU.add))
                    V(on.vector.tensor_reduce(i1, eq, AX_X, ALU.min))
                    V(on.vector.tensor_scalar(hot, iota, i1, None, ALU.is_equal))
                    V(on.vector.scalar_tensor_tensor(lg, hot, -3e38, lg, ALU.mult, ALU.add))
                t = V(on.vector.tensor_tensor(dif, m2, m1, ALU.subtract))
                act.wait(t)
                t = act.counts(on.scalar.activation(w2, dif, ACT.Exp))
                dve.wait(t)
                V(on.vector.tensor_scalar(w1, w2, 1.0, None, ALU.add))
                V(on.vector.reciprocal(w1, w1))
                V(on.vector.tensor_tensor(w2, w2, w1, ALU.mult))
                V(on.vector.tensor_tensor(chosen[:, here], o1, o2, ALU.add))
                V(on.vector.tensor_scalar(o1, o1, w1, None, ALU.mult))
                t = V(on.vector.scalar_tensor_tensor(gates[:, here], o2, w2, o1, ALU.mult, ALU.add))
            free[b] = t
            b = next_bank()
            pe.wait(t, rows_in)
            first, second = chosen[:, 0:E], chosen[:, E:2 * E]
            mm(bank[b][:, 0:E], earlier, first, True, True)
            mm(bank[b][:, E:2 * E], ones, first, True, False)
            mm(bank[b][:, E:2 * E], earlier, second, False, True)
            mm(bank[b][:, 2 * E:3 * E], ones, first, True, False)
            done = pe.counts(mm(bank[b][:, 2 * E:3 * E], ones, second, False, True))
            dve.wait(done)
            dve.counts(on.vector.tensor_copy(place, bank[b][:, 0:2 * E]))
            t = dve.counts(on.vector.tensor_reduce(most, bank[b][:, 2 * E:3 * E], AX_X, ALU.max))
            free[b] = t
            dve.wait(t)
            t = dve.counts(on.vector.tensor_scalar(crowded[:, :], most, float(tile_limit), None, ALU.is_gt))

            def shared_state():
                return (dict(position), list(free), list(h_read), list(dve_read_act), dict(state), turn[0])

            def set_state(saved):
                position.update(saved[0])
                free[:], h_read[:], dve_read_act[:] = saved[1], saved[2], saved[3]
                state.update(saved[4])
                turn[0] = saved[5]

            before = shared_state()
            branching = (pe, dve, act)
            waited = []
            for e in branching:
                e.wait(t, rows_in)
                waited.append(dict(e.waited))
            real = (nc.tensor, nc.vector, nc.scalar)
            ends = []
            for kept in range(3):
                flag = real[kept].value_load(crowded[0:1, 0:1], min_val=0, max_val=1)
                handles = [real[i] if i == kept else Silent() for i in range(3)]
                on.tensor, on.vector, on.scalar = handles
                for way, body in enumerate((experts_on_all, experts_on_their_own)):
                    with real[kept].If(flag) if way == 0 else real[kept].Else():
                        for e, h, w, s in zip(branching, handles, waited, way_done[way]):
                            e.handle = h
                            e.count_on(s, w)
                        set_state(before)
                        body(x_tokens, z, chosen, gates, place, ramp, rows)
                        dve.wait(pe.now(), act.now(), dve.now())
                        on.vector.memset(most, 0.0).then_inc(moe_done, 1)
                        ends.append(dict(position))
            assert all(end == ends[0] for end in ends)
            on.tensor, on.vector, on.scalar = real
            for e, h in zip(branching, real):
                e.handle = h
            for e, w, s in zip(branching, waited, after_done):
                e.count_on(s, w)
            set_state((ends[0], [None] * 8, [None] * 2, [None] * 4, {"sq_read": None, "source_read": None}, 0))
            for e in branching + (pool,):
                e.wait((moe_done, 1))
            return moe_done, 1

        crowded = ctx.enter_context(nc.sbuf_tensor("crowded", [P, 1], mybir.dt.int32))
        way_done = [[sem(f"{w}_{e}") for e in ("pe", "dve", "act")] for w in ("all", "own")]
        after_done = [sem(f"after_{e}") for e in ("pe", "dve", "act")]
        moe_done = sem("moe_done")
        exp_names = ("exp_w1_2", "exp_w3_2", "exp_w2_2")
        EXP_UNITS = D_FF_EXPERT // CHUNK

        def experts_on_all(x_tokens, z, chosen, gates, place, ramp, rows):
            gT = arena[0:E, 1024:1024 + T]
            wide = arena[:, 1280:1280 + E * T]
            b = next_bank()
            for tt in range(TT):
                done = pe.counts(on.tensor.transpose(bank[b][0:E, tt * P:(tt + 1) * P], gates[:, tt * E:(tt + 1) * E],
                                                     ident))
            act.wait(done)
            t = act.counts(on.scalar.copy(gT, bank[b][0:E, 0:T]))
            free[b] = t
            for e in range(0, E, 2):
                b = next_bank()
                pe.wait(t)
                for j in range(2):
                    ins = mm(bank[b][:, j * T:(j + 1) * T], rows[:, (e + j) * P:(e + j + 1) * P], gT, True, True)
                done = pe.counts(ins)
                act.wait(done)
                t2 = act.counts(on.scalar.copy(wide[:, e * T:(e + 2) * T], bank[b][:, :]))
                free[b] = t2
            dve.wait(t2)
            tokens = split_x(x_tokens)
            done = gated_ffn(tokens, exp_names, 0, E * EXP_UNITS, lambda i: blk(wide, i // EXP_UNITS))
            deep_residual(done, z)

        def experts_on_their_own(x_tokens, z, chosen, gates, place, ramp, rows):
            A = KT * T
            x_nat = arena[:, 3 * A:4 * A]
            pick = [arena[:, 4 * A + i * T:4 * A + (i + 1) * T] for i in range(2)]
            pick_g = [arena[:, 4 * A + (2 + i) * T:4 * A + (3 + i) * T] for i in range(2)]
            back = [arena[:, 4 * A + (4 + i) * T:4 * A + (5 + i) * T] for i in range(2)]
            y_own = [arena[:, 5 * A + i * D:5 * A + (i + 1) * D] for i in range(2)]
            spare = [0]

            def spare_bank():
                spare[0] += 1
                i = 6 + spare[0] % 2
                pe.wait(free[i])
                return i

            for tt in range(TT):
                for half in range(2):
                    b = spare_bank()
                    for i in range(4):
                        k = 4 * half + i
                        ins = on.tensor.transpose(bank[b][:, i * P:(i + 1) * P],
                                                  x[:, k * T + tt * P:k * T + (tt + 1) * P], ident)
                    done = pe.counts(ins)
                    act.wait(done)
                    x_ready = act.counts(on.scalar.copy(x_nat[:, tt * D + half * 512:tt * D + (half + 1) * 512],
                                                        bank[b][:, :]))
                    free[b] = x_ready
            z_ready = dve.counts(on.vector.tensor_scalar(z, x[:, :], ALPHA, None, ALU.mult))
            gathered, back_ready = {}, {}
            own_read = [None, None]
            back_read = [None, None]
            y_read = [None, None]

            def gather(e):
                q = e % 2
                dve.wait(own_read[q], back_read[q], x_ready)
                for tt in range(TT):
                    at = slice(tt * P, (tt + 1) * P)
                    c = slice(tt * E + e, tt * E + e + 1)
                    dve.counts(on.vector.tensor_scalar(pick[q][:, at], ramp, place[:, c], chosen[:, c], ALU.is_equal,
                                                       ALU.mult))
                    t = dve.counts(on.vector.tensor_scalar(pick_g[q][:, at], ramp, place[:, c], gates[:, c],
                                                           ALU.is_equal, ALU.mult))
                pe.wait(t, x_ready)
                for half in range(2):
                    b = spare_bank()
                    for k4 in range(4):
                        for tt in range(TT):
                            k = 4 * half + k4
                            ins = mm(bank[b][:, k4 * P:(k4 + 1) * P], x_nat[:, tt * D + k * P:tt * D + (k + 1) * P],
                                     pick[q][:, tt * P:(tt + 1) * P], tt == 0, tt == 1)
                    done = pe.counts(ins)
                    act.wait(own_read[q])
                    t = split_block(source, 2 * q + half, bank[b][:, :], done, 2 * T)
                    free[b] = t
                    gathered[e, half] = t
                b = spare_bank()
                for tt in range(TT):
                    ins = on.tensor.transpose(bank[b][:, tt * P:(tt + 1) * P], pick_g[q][:, tt * P:(tt + 1) * P], ident)
                done = pe.counts(ins)
                act.wait(done)
                back_ready[e] = act.counts(on.scalar.copy(back[q], bank[b][:, 0:T]))
                free[b] = back_ready[e]

            def gate_or_up(e, i, part, name, b):
                for s in range(2):
                    w = take_half(name, e * EXP_UNITS + i, s)
                    pe.wait(gathered[e, s])
                    for k4 in range(KT // 2):
                        k = s * KT // 2 + k4
                        at = (e % 2) * KT * P + k * P
                        ins = mm3(bank[b][:, part * T:(part + 1) * T], w, slice(k4 * CHUNK, (k4 + 1) * CHUNK),
                                  source, slice(at, at + P), k == 0, k == KT - 1, False, True)
                    done = half_read(ins)
                return done

            def turn_hidden(j, t):
                pe.wait(t)
                b = spare_bank()
                for i in range(2):
                    ins = on.tensor.transpose(bank[b][:, i * P:(i + 1) * P], act_buf[:, j * T + i * P:j * T + (i + 1) * P],
                                              ident)
                done = pe.counts(ins)
                act.wait(h_read[j])
                t = split_block(hidden, j, bank[b][:, 0:T], done)
                free[b] = t
                return done, t

            def down_own(e, i, j, h_ready):
                y0 = 2 * (e % 2)
                for s in range(2):
                    w = take_half(exp_names[2], e * EXP_UNITS + i, s)
                    pe.wait(h_ready)
                    for n in range(2):
                        if i == 0 and s == 0:
                            pe.wait(free[y0 + n])
                        at = j * T + s * P
                        ins = mm3(bank[y0 + n][:, :], w, slice(n * 512, (n + 1) * 512), hidden, slice(at, at + P),
                                  i == 0 and s == 0, i == EXP_UNITS - 1 and s == 1, True, True)
                    done = half_read(ins)
                h_read[j] = done
                if i == EXP_UNITS - 1:
                    q = e % 2
                    act.wait(done, y_read[q])
                    for n in range(2):
                        t = act.counts(on.scalar.copy(y_own[q][:, n * 512:(n + 1) * 512], bank[y0 + n][:, :]))
                        free[y0 + n] = t
                    return t

            def scatter(e, y_ready):
                q = e % 2
                pe.wait(y_ready, back_ready[e])
                for u in range(4):
                    b = spare_bank()
                    for j in range(2):
                        c = 2 * u + j
                        ins = mm(bank[b][:, j * T:(j + 1) * T], y_own[q][:, c * P:(c + 1) * P], back[q], True, True)
                    done = pe.counts(ins)
                    dve.wait(done, z_ready if e == 0 else z_last[u])
                    piece = z[:, 2 * u * T:(2 * u + 2) * T]
                    z_last[u] = dve.counts(on.vector.tensor_tensor(piece, piece, bank[b][:, :], ALU.add))
                    free[b] = z_last[u]
                y_read[q] = back_read[q] = done

            z_last = [None] * 4
            gather(0)
            previous = None
            y_ready = {}
            buf_read = [None, None]
            for e in range(E):
                for i in range(EXP_UNITS):
                    n = e * EXP_UNITS + i
                    j = n % 2
                    b = 4 + j
                    pe.wait(free[b])
                    gate_or_up(e, i, 0, exp_names[0], b)
                    if previous is not None:
                        buf_read[1 - j], h_ready = turn_hidden(1 - j, previous[2])
                    done = gate_or_up(e, i, 1, exp_names[1], b)
                    own_read[e % 2] = done
                    act.wait(done, buf_read[j])
                    piece = blk(act_buf, j)
                    t = act.counts(on.scalar.activation(piece, bank[b][:, 0:T], ACT.Silu))
                    dve.wait(t)
                    t = dve.counts(on.vector.tensor_tensor(piece, piece, bank[b][:, T:2 * T], ALU.mult))
                    free[b] = t
                    if previous is not None:
                        pe_, pi, _ = previous
                        y_ready[pe_] = down_own(pe_, pi, 1 - j, h_ready)
                    previous = (e, i, t)
                    if i == 2 and e > 0:
                        scatter(e - 1, y_ready[e - 1])
                    if i == EXP_UNITS - 6 and e < E - 1:
                        gather(e + 1)
            buf_read[j], h_ready = turn_hidden(j, previous[2])
            scatter(E - 1, down_own(E - 1, EXP_UNITS - 1, j, h_ready))

        def per_layer_gate(layer, x_tokens):
            A = KT * T
            pT, gate, prod = arena[:, 0:2 * T], arena[:, A:2 * A], arena[:, 2 * A:3 * A]
            act.wait(pe.now(), dve.now(), act.now(), pool.now())
            p_in = load_small(act, pT, dram["p_2"][layer])
            act.wait(h_read[0], h_read[1])
            p_tok = [split_block(hidden, i, blk(pT, i), p_in) for i in range(2)]
            p_done = row_product("ple_w_2", layer, hidden, 0, p_tok, True, True)
            h_read[0] = p_done
            prods = []
            for u in range(4):
                b, done = project_T("ple_gate_w_2", 4 * layer + u, x_tokens)
                act.wait(done)
                t = act.counts(on.scalar.activation(gate[:, 2 * u * T:(2 * u + 2) * T], bank[b][:, :], ACT.Sigmoid))
                free[b] = t
                dve.wait(t, p_done)
                t = dve.counts(on.vector.tensor_tensor(prod[:, 2 * u * T:(2 * u + 2) * T],
                                                       gate[:, 2 * u * T:(2 * u + 2) * T], bank[u][:, :], ALU.mult))
                free[u] = t
            dve.wait(t, pe.now())
            return [dve.counts(on.vector.tensor_tensor(blk(x, k), blk(x, k), blk(prod, k), ALU.add))
                    for k in range(KT)]

        def store(x_tokens):
            nat = arena[:, 0:TT * D]
            act.wait(pe.now(), dve.now(), act.now(), pool.now())
            for tt in range(TT):
                for half in range(2):
                    b = next_bank()
                    for i in range(4):
                        k = 4 * half + i
                        pe.wait(x_tokens[k])
                        ins = on.tensor.transpose(bank[b][:, i * P:(i + 1) * P],
                                                  x[:, k * T + tt * P:k * T + (tt + 1) * P], ident)
                    done = pe.counts(ins)
                    act.wait(done)
                    t = act.counts(on.scalar.copy(nat[:, tt * D + half * 512:tt * D + (half + 1) * 512],
                                                  bank[b][:, :]))
                    free[b] = t
            act.wait(t)
            on.scalar.dma_start(out.rearrange("(s p) d -> p s d", p=P),
                                nat.rearrange("p (s d) -> p s d", s=TT)).then_inc(out_written, 16)
            act.wait((out_written, 16))

        names1 = ("ffn_w_gate", "ffn_w_up", "ffn_w_down")
        FFN_UNITS = D_FF // CHUNK

        def half_ffn(which, tokens):
            n_tok = rms_norm(tokens, "ffn_norm", which * KT)
            done = gated_ffn(n_tok, names1, which * FFN_UNITS, FFN_UNITS)
            return add_residual(done, 0.5)

        def network():
            tokens = [small_in] * KT
            tokens = half_ffn(0, tokens)
            n_tok = rms_norm(tokens, "mix_norm", 0)
            tokens = attention(n_tok, tokens)
            tokens = half_ffn(1, tokens)
            tokens = half_ffn(2, tokens)
            n_tok = rms_norm(tokens, "mix_norm", KT, False)
            tokens = rwkv(n_tok)
            tokens = split_x(half_ffn(3, tokens))
            for layer in range(2):
                z, z_tok = pool_conv_mixer(layer, tokens)
                tokens = norm_to_x(z, z_tok, "ln1_g_2", "ln1_b_2", layer, layer == 0)
                z = arena[:, 8 * KT * T:9 * KT * T]
                if layer == 0:
                    done = gated_ffn(tokens, ("dense_w1_2", "dense_w3_2", "dense_w2_2"), 0, FFN_UNITS)
                    z_tok = deep_residual(done, z)
                else:
                    z_tok = [moe(tokens, z)] * KT
                tokens = norm_to_x(z, z_tok, "ln2_g_2", "ln2_b_2", layer)
                tokens = per_layer_gate(layer, tokens)
                if layer == 0:
                    tokens = split_x(tokens)
            return tokens

        store(network())

        for n in range(max(position["unit"], halves[position["split"] - 1][0] + 1)):
            name, i, _ = stream[n]
            if n >= RAW_SLOTS:
                sp.wait(raw_read[n - RAW_SLOTS])
            src = dram[name][i]
            rows, cols = src.shape
            at = (n % RAW_SLOTS) * UNIT
            nc.sync.dma_start(raw[0:rows, at:at + cols], src).then_inc(slot_landed[n % RAW_SLOTS], 16)


def column_units(w):
    w = np.asarray(w)
    w = w.reshape(-1, KT, P, w.shape[-1] // CHUNK, CHUNK)
    return np.ascontiguousarray(w.transpose(0, 3, 2, 1, 4)).reshape(-1, P, UNIT)


def row_units(w):
    w = np.asarray(w).reshape(-1, 2, P, D)
    return np.ascontiguousarray(w.transpose(0, 2, 1, 3)).reshape(-1, P, UNIT)


def token_T(a):
    f = a.shape[-1]
    return np.ascontiguousarray(a.reshape(T, f // P, P).transpose(2, 1, 0)).reshape(P, f // P * T)


def lay_out(inp):
    d = dict(constant_arrays())
    d["x"] = token_T(inp["x"].reshape(T, D))
    d["p_2"] = np.stack([token_T(inp["p_2"][i].reshape(T, -1)) for i in range(2)])
    cols = []
    for name, n in PARAMS:
        a = np.asarray(inp[name])
        if name in ("attn_q_norm", "attn_k_norm"):
            c = np.concatenate([a.reshape(HEAD, 1)] * 2, axis=0)
        elif name == "router_w_2":
            c = a.reshape(KT, P, N_EXPERTS).transpose(1, 0, 2).reshape(P, -1)
        else:
            c = a.reshape(n, P).T
        cols.append(c)
    d["params"] = np.ascontiguousarray(np.concatenate(cols, axis=1))
    for name in ("ffn_w_gate", "ffn_w_up", "attn_w_in", "rw_wr", "rw_wk", "rw_wv", "rw_wo", "w_in_2", "w_out_2",
                 "dense_w1_2", "dense_w3_2", "exp_w1_2", "exp_w3_2", "ple_gate_w_2"):
        d[name] = column_units(inp[name])
    for name in ("ffn_w_down", "attn_w_out", "dense_w2_2", "exp_w2_2", "ple_w_2"):
        d[name] = row_units(inp[name])
    k_tiles = lambda w: np.asarray(w).reshape(KT, P, -1).transpose(1, 0, 2).reshape(P, -1)
    d["lora_in"] = np.concatenate([k_tiles(inp["rw_w1"]), k_tiles(inp["rw_a1"])], axis=1)[None]
    d["lora_out"] = np.concatenate([inp["rw_w2"][0], inp["rw_a2"][0]], axis=1)[None]
    g1 = np.asarray(inp["rw_g1"][0])
    d["gate_in"] = column_units(np.pad(g1, ((0, 0), (0, CHUNK - g1.shape[1]))))
    g2 = np.asarray(inp["rw_g2"][0])
    d["gate_out"] = row_units(np.pad(g2, ((0, CHUNK - g2.shape[0]), (0, 0))))
    d["pool_w_2"] = np.ascontiguousarray(np.asarray(inp["pool_w_2"]).transpose(0, 2, 1, 3)).reshape(2, P, 4 * P)
    d["conv_pw_2"] = np.ascontiguousarray(
        np.asarray(inp["conv_pw_2"]).reshape(2, 4, P, 512).transpose(0, 2, 1, 3)).reshape(2, P, UNIT)
    bucket = bucket_of_distance()
    table = np.asarray(inp["rel_bias"])
    rows = []
    for j in range(GROUP_HEADS):
        for tile in range(TT):
            dist = tile * P + np.arange(P)[:, None] - np.arange(P * (tile + 1))[None, :]
            at = bucket[np.maximum(dist, 0)]
            for g in range(N_GROUPS):
                rows.append(table[:, GROUP_HEADS * g + j][at])
    d["rel_bias"] = np.concatenate(rows, axis=1)
    return {k: np.ascontiguousarray(v) for k, v in d.items()}


def kernel(**inputs):
    import concourse.bacc as bacc
    from concourse.bass_utils import run_bass_kernel_spmd

    arrays = lay_out({k: np.asarray(v) for k, v in inputs.items()})
    nc = bacc.Bacc("TRN2", target_bir_lowering=False, num_devices=1)
    dram = {name: nc.dram_tensor(f"in_{name}", a.shape, mybir.dt.from_np(a.dtype), kind="ExternalInput").ap()
            for name, a in arrays.items()}
    out = nc.dram_tensor("out", (T, D), F32, kind="ExternalOutput").ap()
    bass_macaron_attention_rwkv_conv_moe_kernel(nc, dram, out)
    result = run_bass_kernel_spmd(nc, [{f"in_{name}": a for name, a in arrays.items()}], core_ids=[0])
    return result.results[0]["out"].reshape(1, T, D)
```

```python
from contextlib import ExitStack

import numpy as np

import concourse.bass as bass
from concourse import mybir

F32 = mybir.dt.float32
F32R = mybir.dt.float32r
ALU = mybir.AluOpType
ACT = mybir.ActivationFunctionType
AX_X = mybir.AxisListType.X

P = 128
D = 1024
T = 256
KT = D // P
TT = T // P
D_FF = 2816
D_FF_EXPERT = 3584
N_EXPERTS = 8
CHUNK = 256
UNIT = KT * CHUNK
HEAD = 64
SB_HEADS = 4
DIL_HEADS = 12
DIL_PATTERNS = ((128, 1), (512, 4), (2048, 16))
N_GROUPS = len(DIL_PATTERNS)
GROUP_HEADS = DIL_HEADS // N_GROUPS
N_BUCKETS = 32
MAX_DISTANCE = 2048
NEG_INF = -1e30
SCALE = HEAD ** -0.5
RW_CHUNK = 64
DECAY_SCALE = -float(np.exp(-0.5))
CONV_WIDTH = 31
PAD_CONV = CONV_WIDTH - 1
POOL_WINDOWS = (2, 4, 8, 16)
PAD_POOL = 16
ALPHA = 4.0 ** 0.25
ARENA = 23296
RAW_SLOTS = 3
HALVES = 4
HALF = UNIT // 2
LEVELS = (2, 4, 8, 16, 32)

PARAMS = [
    ("ffn_norm", 4 * KT), ("mix_norm", 2 * KT), ("rw_mix", 6 * KT), ("rw_w0", KT), ("rw_a0", KT),
    ("rw_kk", KT), ("rw_ka", KT), ("rw_rk", KT), ("rw_lnx_g", KT), ("rw_lnx_b", KT),
    ("attn_q_norm", 1), ("attn_k_norm", 1), ("pool_scale_2", 8), ("conv_w_2", 2 * CONV_WIDTH * 4),
    ("conv_b_2", 8), ("conv_ln_g_2", 8), ("conv_ln_b_2", 8), ("ln1_g_2", 16), ("ln1_b_2", 16),
    ("ln2_g_2", 16), ("ln2_b_2", 16), ("router_w_2", KT * N_EXPERTS),
]
PARAM_AT = {}
N_PARAM = 0
for _name, _n in PARAMS:
    PARAM_AT[_name] = N_PARAM
    N_PARAM += _n

CONSTS = [
    ("ident", P), ("ones", P), ("head_ones", P), ("later", P), ("eps_rms", 1), ("eps_gn", 1),
    ("eps_ln", 1), ("one", 1), ("iota", N_EXPERTS), ("restart", T),
]
CONST_AT = {}
N_CONST = 0
for _name, _n in CONSTS:
    CONST_AT[_name] = N_CONST
    N_CONST += _n
N_LOGIT = P + 2 * P


def constant_arrays():
    row, col = np.arange(P)[:, None], np.arange(P)[None, :]
    c = np.zeros((P, N_CONST), np.float32)

    def put(name, value):
        at = CONST_AT[name]
        n = dict(CONSTS)[name]
        c[:, at:at + n] = value

    put("ident", row == col)
    put("ones", 1.0)
    put("head_ones", row // HEAD == col // HEAD)
    put("later", row > col)
    put("eps_rms", 1e-6)
    put("eps_gn", 64e-5)
    put("eps_ln", 1e-5)
    put("one", 1.0)
    put("iota", np.arange(N_EXPERTS)[None, :])
    put("restart", (np.arange(T)[None, :] % RW_CHUNK) != 0)

    before = (row < col).astype(np.float32)
    stick = np.concatenate([before, np.ones((P, P), np.float32), before], axis=1)

    dil = []
    for tile in range(TT):
        keys = np.arange(P * (tile + 1))[None, :]
        dist = tile * P + row - keys
        for window, r in DIL_PATTERNS:
            ok = (dist >= 0) & (dist <= window) & (dist % r == 0)
            dil.append(np.where(ok, 0.0, NEG_INF).astype(np.float32))
    dil = np.concatenate(dil, axis=1)

    same = row // RW_CHUNK == col // RW_CHUNK
    strict = (same & (row < col)).astype(np.float32)
    upto = (same & (row <= col)).astype(np.float32)
    rw = [strict, upto, strict, upto]
    for b in (1,) + LEVELS:
        rw.append(((row // (2 * b) == col // (2 * b)) & (row % (2 * b) < b) & (col % (2 * b) >= b)).astype(np.float32))
    rw.append(rw[4].T)
    rw = np.concatenate(rw, axis=1)

    t = np.arange(T)
    count = np.stack([1.0 / np.minimum(t + 1.0, w) for w in POOL_WINDOWS]).astype(np.float32)
    count = np.broadcast_to(count.reshape(1, -1), (P, 4 * T))
    pick = np.zeros((N_EXPERTS, N_EXPERTS, P), np.float32)
    pick[np.arange(N_EXPERTS), np.arange(N_EXPERTS), :] = 1.0
    return {"consts": c, "stick_mask": stick, "dilated_mask": dil, "rwkv_masks": rw,
            "moe_tables": np.concatenate([(row < col).astype(np.float32), np.broadcast_to(col, (P, P)).astype(np.float32)],
                                         axis=1),
            "inverse_count": np.ascontiguousarray(count), "expert_rows": pick.reshape(N_EXPERTS, -1)}


def bucket_of_distance():
    d = np.arange(T)
    large = 16 + (np.log(np.maximum(d, 1) / 16.0) / np.log(MAX_DISTANCE / 16.0) * 16).astype(np.int64)
    return np.where(d < 16, d, np.minimum(large, N_BUCKETS - 1))


def stream_order():
    order = []

    def several(name, first, n, split=True):
        order.extend((name, i, split) for i in range(first, first + n))

    def ffn(gate, up, down, first, n):
        for i in range(n + 1):
            if i < n:
                order.extend([(gate, first + i, True), (up, first + i, True)])
            if i > 0:
                order.append((down, first + i - 1, True))

    n_ffn, n_expert = D_FF // CHUNK, D_FF_EXPERT // CHUNK
    ffn("ffn_w_gate", "ffn_w_up", "ffn_w_down", 0, n_ffn)
    several("attn_w_in", 0, 12)
    several("attn_w_out", 0, 2)
    ffn("ffn_w_gate", "ffn_w_up", "ffn_w_down", n_ffn, n_ffn)
    ffn("ffn_w_gate", "ffn_w_up", "ffn_w_down", 2 * n_ffn, n_ffn)
    for name in ("rw_wr", "rw_wk", "rw_wv"):
        several(name, 0, 4, False)
    for name in ("lora_in", "lora_out", "gate_in", "gate_out"):
        several(name, 0, 1, False)
    several("rw_wo", 0, 4, False)
    ffn("ffn_w_gate", "ffn_w_up", "ffn_w_down", 3 * n_ffn, n_ffn)
    for layer in range(2):
        several("w_in_2", 6 * layer + 2, 4)
        several("w_in_2", 6 * layer, 2)
        several("pool_w_2", layer, 1, False)
        several("conv_pw_2", layer, 1)
        several("w_out_2", 4 * layer, 4)
        if layer == 0:
            ffn("dense_w1_2", "dense_w3_2", "dense_w2_2", 0, n_ffn)
        else:
            ffn("exp_w1_2", "exp_w3_2", "exp_w2_2", 0, N_EXPERTS * n_expert)
        several("ple_w_2", layer, 1)
        several("ple_gate_w_2", 4 * layer, 4)
    return order


class Engine:

    def __init__(self, handle, semaphore):
        self.handle, self.semaphore, self.count, self.waited = handle, semaphore, 0, {}

    def wait(self, *tokens):
        for token in tokens:
            if token is None:
                continue
            semaphore, value = token
            if self.waited.get(id(semaphore), 0) < value:
                self.waited[id(semaphore)] = value
                self.handle.wait_ge(semaphore, value)

    def counts(self, instruction):
        instruction.then_inc(self.semaphore, 1)
        self.count += 1
        return self.semaphore, self.count

    def count_on(self, semaphore, waited):
        self.semaphore, self.count, self.waited = semaphore, 0, dict(waited)

    def now(self):
        return (self.semaphore, self.count) if self.count else None


class Silent:

    def silent(self, *args, **kwargs):
        return self

    matmul = transpose = activation = copy = mul = tensor_tensor = tensor_scalar = silent
    scalar_tensor_tensor = tensor_copy = tensor_reduce = reciprocal = memset = wait_ge = then_inc = silent


class Issuing:

    def __init__(self, tensor, vector, scalar):
        self.tensor, self.vector, self.scalar = tensor, vector, scalar


def bass_macaron_attention_rwkv_conv_moe_kernel(nc, dram, out, tile_limit=P):
    with ExitStack() as ctx:
        def sb(name, cols, dtype=F32):
            return ctx.enter_context(nc.sbuf_tensor(name, [P, cols], dtype))

        def sem(name):
            return ctx.enter_context(nc.semaphore(name))

        raw = sb("raw_weights", RAW_SLOTS * UNIT)
        w_hi, w_lo = sb("weights_hi", HALVES * HALF, F32R), sb("weights_lo", HALVES * HALF, F32R)
        s_hi, s_lo = sb("source_hi", KT * T, F32R), sb("source_lo", KT * T, F32R)
        h_hi, h_lo = sb("hidden_hi", 4 * T, F32R), sb("hidden_lo", 4 * T, F32R)
        x = sb("x_T", KT * T)
        xn = sb("normed_T", KT * T)
        sq = sb("squares", KT * T)
        arena = sb("arena", ARENA)
        param = sb("params", N_PARAM)
        const = sb("consts", N_CONST)
        act_buf = sb("activated", 4 * T)
        std = sb("std", T)
        rstd = sb("rstd", T)
        mean = sb("mean", T)
        bank = [ctx.enter_context(nc.psum_tensor(f"bank{i}", [P, 512], F32)) for i in range(8)]

        on = Issuing(nc.tensor, nc.vector, nc.scalar)
        pe = Engine(nc.tensor, sem("pe_done"))
        dve = Engine(nc.vector, sem("dve_done"))
        act = Engine(nc.scalar, sem("act_done"))
        pool = Engine(nc.gpsimd, sem("pool_done"))
        sp = Engine(nc.sync, sem("sp_done"))
        slot_landed = [sem(f"slot_landed{i}") for i in range(RAW_SLOTS)]
        split_ready = sem("split_ready")
        split_read = sem("split_read")
        x_landed = sem("x_landed")
        small_landed = sem("small_landed")
        attn_tables_landed = sem("attn_tables_landed")
        out_written = sem("out_written")
        small_count = [0]

        def load_small(engine, dst, src):
            engine.handle.dma_start(dst, src).then_inc(small_landed, 16)
            small_count[0] += 16
            return small_landed, small_count[0]

        stream = stream_order()
        halves = [(n, s) for n, (_, _, split) in enumerate(stream) if split for s in range(2)]
        raw_read = [None] * len(stream)
        position = {"unit": 0, "half": 0, "split": 0, "limit": len(halves)}

        def landed(n):
            return slot_landed[n % RAW_SLOTS], 16 * (n // RAW_SLOTS + 1)

        def take(name, i=0, rows=P, cols=UNIT):
            n = position["unit"]
            position["unit"] += 1
            assert stream[n] == (name, i, False), (stream[n], name, i)
            split_ahead(position["half"] + HALVES, n)
            pe.wait(landed(n))
            at = (n % RAW_SLOTS) * UNIT
            return n, raw[0:rows, at:at + cols]

        def give_back(n, token):
            raw_read[n] = token

        def split_ahead(upto, current):
            while position["split"] < min(upto, position["limit"]):
                j = position["split"]
                n, part = halves[j]
                if n > current + RAW_SLOTS - 1:
                    break
                src = raw[:, (n % RAW_SLOTS) * UNIT + part * HALF:(n % RAW_SLOTS) * UNIT + (part + 1) * HALF]
                at = slice((j % HALVES) * HALF, (j % HALVES + 1) * HALF)
                act.wait(landed(n))
                if j >= HALVES:
                    act.wait((split_read, j - HALVES + 1))
                t = act.counts(on.scalar.copy(w_hi[:, at], src))
                dve.wait(t)
                on.vector.tensor_tensor(w_lo[:, at], src, w_hi[:, at].bitcast(F32), ALU.subtract)\
                    .then_inc(split_ready, 1)
                if part == 1:
                    raw_read[n] = (split_ready, j + 1)
                position["split"] += 1

        def take_half(name, i, part):
            j = position["half"]
            position["half"] += 1
            if part == 1:
                position["unit"] += 1
            n, p = halves[j]
            assert (stream[n], p) == ((name, i, True), part), (stream[n], p, name, i, part)
            split_ahead(j + HALVES, n)
            pe.wait((split_ready, j + 1))
            at = slice((j % HALVES) * HALF, (j % HALVES + 1) * HALF)
            return w_hi[:, at], w_lo[:, at]

        def half_read(ins):
            ins.then_inc(split_read, 1)
            return split_read, position["half"]

        def mm3(dst, w, at, src, src_at, start, stop, shared, moving_weights=False):
            for i, (a, b) in enumerate(((0, 0), (0, 1), (1, 0))):
                lhsT, rhs = (src[b][:, src_at], w[a][:, at]) if moving_weights else (w[a][:, at], src[b][:, src_at])
                ins = mm(dst, lhsT, rhs, start and i == 0, stop and i == 2, shared)
            return ins

        source = (s_hi, s_lo)
        hidden = (h_hi, h_lo)

        def split_block(pair, k, piece, token, width=T):
            act.wait(token, state["source_read"] if pair is source else None)
            t = act.counts(on.scalar.copy(blk(pair[0], k, width), piece))
            dve.wait(t)
            return dve.counts(on.vector.tensor_tensor(blk(pair[1], k, width), piece,
                                                      blk(pair[0], k, width).bitcast(F32), ALU.subtract))

        def col(name, i=0, rows=P):
            return param[0:rows, PARAM_AT[name] + i:PARAM_AT[name] + i + 1]

        def con(name):
            at = CONST_AT[name]
            return const[:, at:at + dict(CONSTS)[name]]

        ident, ones, head_ones, later = con("ident"), con("ones"), con("head_ones"), con("later")

        def blk(tile, k, w=T):
            return tile[:, k * w:(k + 1) * w]

        free = [None] * 8
        turn = [0]

        def next_bank():
            turn[0] += 1
            i = 4 + turn[0] % 4
            pe.wait(free[i])
            return i

        def mm(dst, lhsT, rhs, start, stop, shared=False):
            return on.tensor.matmul(dst, lhsT, rhs, start=start, stop=stop, skip_group_check=shared)

        nc.scalar.dma_start(param[:, :], dram["params"]).then_inc(x_landed, 16)
        nc.scalar.dma_start(x[:, :], dram["x"]).then_inc(x_landed, 16)
        x_in = (x_landed, 2 * 16)
        act.wait(x_in)
        consts_in = load_small(act, const[:, :], dram["consts"])
        for e in (pe, dve, pool):
            e.wait(x_in)

        state = {"sq_read": None, "source_read": None}

        def feature_mean(source_tokens, source, n_k, matrix, square):
            b = next_bank()
            for k in range(n_k):
                if square:
                    act.wait(source_tokens[k], state["sq_read"])
                    token = act.counts(on.scalar.activation(blk(sq, k), blk(source, k), ACT.Square))
                    pe.wait(token)
                    piece = blk(sq, k)
                else:
                    pe.wait(source_tokens[k])
                    piece = blk(source, k)
                ins = mm(bank[b][:, 0:T], matrix, piece, k == 0, k == n_k - 1)
            done = pe.counts(ins)
            if square:
                state["sq_read"] = done
            return b, done

        def reciprocal_std(b, done, n, eps):
            act.wait(done, dve.now())
            t = act.counts(on.scalar.activation(std[:, :], bank[b][:, 0:T], ACT.Sqrt, bias=con(eps), scale=1.0 / n))
            free[b] = t
            dve.wait(t)
            return dve.counts(on.vector.reciprocal(rstd[:, :], std[:, :]))

        def rms_norm(x_tokens, gain, first, split=True):
            b, done = feature_mean(x_tokens, x, KT, ones, True)
            r = reciprocal_std(b, done, D, "eps_rms")
            dve.wait(r)
            tokens = [dve.counts(on.vector.scalar_tensor_tensor(
                blk(xn, k), blk(x, k), col(gain, first + k), rstd[:, :], ALU.mult, ALU.mult))
                for k in range(KT)]
            if split:
                tokens = [split_block(source, k, blk(xn, k), tokens[k]) for k in range(KT)]
            return tokens

        def rms_norm_late(x_tokens, gain, first):
            tokens = []
            for k in range(KT):
                act.wait(x_tokens[k], state["source_read"])
                t = act.counts(on.scalar.activation(blk(s_hi, k), blk(x, k), ACT.Copy, scale=col(gain, first + k)))
                dve.wait(t)
                tokens.append(dve.counts(on.vector.scalar_tensor_tensor(
                    blk(s_lo, k), blk(x, k), col(gain, first + k), blk(s_hi, k).bitcast(F32),
                    ALU.mult, ALU.subtract)))
            squares = []
            for k in range(KT):
                act.wait(state["sq_read"])
                squares.append(act.counts(on.scalar.activation(blk(sq, k), blk(x, k), ACT.Square)))

            def finish(b):
                for e in (pe, dve, act, pool):
                    e.wait(consts_in)
                pe.wait(free[b])
                for k in range(KT):
                    pe.wait(squares[k])
                    ins = mm(bank[b][:, 0:T], ones, blk(sq, k), k == 0, k == KT - 1)
                done = state["sq_read"] = pe.counts(ins)
                return reciprocal_std(b, done, D, "eps_rms")

            return tokens, finish

        def layer_norm(z, z_tokens, n_k, write):
            b, done = feature_mean(z_tokens, z, n_k, ones, False)
            act.wait(done, dve.now())
            t = act.counts(on.scalar.mul(mean[:, :], bank[b][:, 0:T], 1.0 / (n_k * P)))
            free[b] = t
            dve.wait(t)
            centred = [dve.counts(on.vector.tensor_tensor(blk(z, k), blk(z, k), mean[:, :], ALU.subtract))
                       for k in range(n_k)]
            b, done = feature_mean(centred, z, n_k, ones, True)
            r = reciprocal_std(b, done, n_k * P, "eps_ln")
            dve.wait(r)
            return [write(k) for k in range(n_k)]

        h_read = [None, None]

        def down(name, i, h_half, h_tokens, first, last):
            done = [None] * 4
            for b in range(2):
                w = take_half(name, i, b)
                pe.wait(h_tokens[b])
                for c in range(KT):
                    start = first and b == 0 and c % 2 == 0
                    if start:
                        pe.wait(free[c // 2])
                    at = (2 * h_half + b) * T
                    ins = mm3(bank[c // 2][:, (c % 2) * T:(c % 2 + 1) * T], w, slice(c * P, (c + 1) * P),
                              hidden, slice(at, at + T), start, last and b == 1, True)
                    if last and b == 1 and c % 2 and c < KT - 1:
                        done[c // 2] = pe.counts(ins)
                done[3] = half_read(ins)
            h_read[h_half] = done[3]
            return done

        def gated_ffn(src_tokens, names, first_unit, n_chunks, scale=None, begin=True, end=True,
                      late_norm=None):
            gate_name, up_name, down_name = names
            waiting = None
            for i in range(n_chunks):
                side = i % 2
                bs = [4 + 2 * side, 5 + 2 * side]
                both = [None, None]
                for part, name in ((0, gate_name), (1, up_name)):
                    for s in range(2):
                        w = take_half(name, first_unit + i, s)
                        for b in range(2):
                            if part == 0 and s == 0:
                                pe.wait(free[bs[b]])
                            for k4 in range(KT // 2):
                                k = s * KT // 2 + k4
                                pe.wait(src_tokens[k])
                                ins = mm3(bank[bs[b]][:, part * T:(part + 1) * T], w,
                                          slice(k4 * CHUNK + b * P, k4 * CHUNK + (b + 1) * P),
                                          source, slice(k * T, (k + 1) * T), k == 0, k == KT - 1, False)
                            if part == 1 and s == 1 and b == 0:
                                both[0] = pe.counts(ins)
                        token = half_read(ins)
                both[1] = token
                state["source_read"] = token
                if late_norm is not None and i == 0:
                    dve.wait(late_norm(7))
                h_tokens = []
                for b in range(2):
                    j = 2 * side + b
                    piece = blk(act_buf, j)
                    act.wait(both[b], dve_read_act[j])
                    if late_norm is not None:
                        dve.wait(both[b], dve_read_act[j])
                        t = dve.counts(on.vector.tensor_tensor(piece, bank[bs[b]][:, 0:T], rstd[:, :], ALU.mult))
                        act.wait(t)
                        t_gate = act.counts(on.scalar.activation(piece, piece, ACT.Silu))
                        up = blk(xn, j)
                        t_up = dve.counts(on.vector.tensor_tensor(up, bank[bs[b]][:, T:2 * T], rstd[:, :],
                                                                  ALU.mult))
                        free[bs[b]] = t_up
                        dve.wait(t_gate, t_up)
                        t = dve.counts(on.vector.tensor_tensor(piece, piece, up, ALU.mult))
                    else:
                        t = act.counts(on.scalar.activation(piece, bank[bs[b]][:, 0:T], ACT.Silu))
                        dve.wait(t)
                        t = dve.counts(on.vector.tensor_tensor(piece, piece, bank[bs[b]][:, T:2 * T], ALU.mult))
                        free[bs[b]] = t
                    if scale is not None:
                        dve.wait(t)
                        t = dve.counts(on.vector.tensor_tensor(piece, piece, scale(i), ALU.mult))
                    act.wait(h_read[side])
                    t = split_block(hidden, j, piece, t)
                    dve_read_act[j] = t
                    h_tokens.append(t)
                if waiting is not None:
                    done = down(down_name, first_unit + i - 1, (i - 1) % 2, waiting, begin and i == 1, False)
                waiting = h_tokens
            return down(down_name, first_unit + n_chunks - 1, (n_chunks - 1) % 2, waiting,
                        begin and n_chunks == 1, end)

        dve_read_act = [None] * 4

        def add_residual(done, scale, base=None, dst=None):
            tokens = []
            for c in range(KT):
                dve.wait(done[c // 2])
                t = dve.counts(on.vector.scalar_tensor_tensor(
                    blk(x, c), bank[c // 2][:, (c % 2) * T:(c % 2 + 1) * T], scale, blk(x, c),
                    ALU.mult, ALU.add))
                free[c // 2] = t
                tokens.append(t)
            return tokens

        def project_raw(name, i, src, src_tokens):
            n, w = take(name, i)
            b = next_bank()
            for j in range(2):
                for k in range(KT):
                    pe.wait(src_tokens[k])
                    ins = mm(bank[b][:, j * T:(j + 1) * T], w[:, k * CHUNK + j * P:k * CHUNK + (j + 1) * P],
                             blk(src, k), k == 0, k == KT - 1)
            done = pe.counts(ins)
            give_back(n, done)
            return b, done

        def project_T(name, i, src_tokens, tokens_first=False):
            b = next_bank()
            for s in range(2):
                w = take_half(name, i, s)
                for j in range(2):
                    for k4 in range(KT // 2):
                        k = s * KT // 2 + k4
                        pe.wait(src_tokens[k])
                        at = slice(k4 * CHUNK + j * P, k4 * CHUNK + (j + 1) * P)
                        src_at = slice(k * T, (k + 1) * T)
                        if tokens_first:
                            at = slice(k4 * CHUNK, (k4 + 1) * CHUNK)
                            src_at = slice(k * T + j * P, k * T + (j + 1) * P)
                        ins = mm3(bank[b][:, j * T:(j + 1) * T], w, at, source, src_at,
                                  k == 0 and j == 0, k == KT - 1, True, tokens_first)
                done = half_read(ins)
            state["source_read"] = done
            return b, done

        def row_product(name, i, pair, first_block, tokens, first, last):
            for s in range(2):
                w = take_half(name, i, s)
                pe.wait(tokens[s])
                for c in range(KT):
                    start = first and s == 0 and c % 2 == 0
                    if start:
                        pe.wait(free[c // 2])
                    at = (first_block + s) * T
                    ins = mm3(bank[c // 2][:, (c % 2) * T:(c % 2 + 1) * T], w, slice(c * P, (c + 1) * P),
                              pair, slice(at, at + T), start, last and s == 1, True)
                done = half_read(ins)
            return done

        def attention(src_tokens, x_tokens):
            A = KT * T
            Q, K, V = arena[:, 0:A], arena[:, A:2 * A], arena[:, 2 * A:3 * A]
            bias = arena[:, 3 * A:3 * A + GROUP_HEADS * N_GROUPS * N_LOGIT]
            at = 3 * A + GROUP_HEADS * N_GROUPS * N_LOGIT
            dmask = arena[:, at:at + N_GROUPS * N_LOGIT]
            at += N_GROUPS * N_LOGIT
            smask = arena[:, at:at + N_LOGIT]
            at += N_LOGIT
            merged = arena[:, at:at + 4 * T]
            at += 4 * T
            work = arena[:, at:ARENA]
            pool.wait((split_read, 8))
            for tile, name in ((bias, "rel_bias"), (dmask, "dilated_mask"), (smask, "stick_mask")):
                nc.gpsimd.dma_start(tile, dram[name]).then_inc(attn_tables_landed, 16)
            smask_in = (attn_tables_landed, 3 * 16)
            pool.wait(smask_in)
            for j in range(GROUP_HEADS):
                w3 = N_GROUPS * N_LOGIT
                bias_ready = pool.counts(nc.gpsimd.tensor_tensor(
                    bias[:, j * w3:(j + 1) * w3], bias[:, j * w3:(j + 1) * w3], dmask, ALU.add))
            ready = {}

            def to_sbuf(tile, block, b, done):
                act.wait(done)
                t = act.counts(on.scalar.copy(tile[:, block * T:(block + 2) * T], bank[b][:, :]))
                free[b] = t
                return t

            def v_unit(i, block):
                b, done = project_T("attn_w_in", i, src_tokens, True)
                act.wait(done)
                for tt in range(TT):
                    t = act.counts(on.scalar.copy(V[:, tt * D + block * T:tt * D + (block + 1) * T],
                                                  bank[b][:, tt * T:(tt + 1) * T]))
                free[b] = t
                return t

            norm_at = [0]
            NORM_SQUARES = 4

            def head_squares(tile, block, token):
                i = norm_at[0]
                norm_at[0] += 1
                piece = sq[:, i % NORM_SQUARES * 2 * T:(i % NORM_SQUARES + 1) * 2 * T]
                unit = tile[:, block * T:(block + 2) * T]
                pool.wait(token, squares_read.get(i - NORM_SQUARES), state["sq_read"])
                return i, piece, pool.counts(nc.gpsimd.tensor_tensor(piece, unit, unit, ALU.mult))

            def head_norm(tile, block, squares, gain):
                i, s_b, squared = squares
                s_s, s_r = (work[:, (2 * i + j) % 4 * 2 * T:((2 * i + j) % 4 + 1) * 2 * T] for j in range(2))
                unit = tile[:, block * T:(block + 2) * T]
                b = next_bank()
                pe.wait(squared)
                done = squares_read[i] = pe.counts(mm(bank[b][:, :], head_ones, s_b, True, True))
                act.wait(done, roots_read.get(i - 2))
                t = act.counts(on.scalar.activation(s_s, bank[b][:, :], ACT.Sqrt, bias=con("eps_rms"),
                                                    scale=1.0 / HEAD))
                free[b] = t
                dve.wait(t)
                t = roots_read[i] = dve.counts(on.vector.reciprocal(s_r, s_s))
                dve.wait(t)
                return dve.counts(on.vector.scalar_tensor_tensor(unit, unit, col(gain), s_r, ALU.mult, ALU.mult))

            LW = N_LOGIT
            W3 = N_GROUPS * T
            SLOT_COLS = 2 * W3 + 4
            slot_work = [work[:, 8 * T + i * SLOT_COLS:8 * T + (i + 1) * SLOT_COLS] for i in range(4)]
            work_read = [None] * 4
            merged_tokens = {}

            def stick_head(h, slot):
                rows = slice(HEAD * (h % 2), HEAD * (h % 2) + HEAD)
                block = h // 2
                w4 = slot_work[slot]
                absz, soft, lead, wt = (w4[:, i * LW:(i + 1) * LW] for i in range(4))
                q_all = Q[rows, block * T:(block + 1) * T]
                b = b2 = slot
                pe.wait(sq_ready, sk_ready, free[b])
                mm(bank[b][:, 0:T], K[rows, block * T:block * T + P], q_all, True, True)
                done = pe.counts(mm(bank[b][:, T:LW], K[rows, block * T + P:(block + 1) * T],
                                    Q[rows, block * T + P:(block + 1) * T], True, True))
                yield
                act.wait(done, work_read[slot])
                z = bank[b][:, 0:LW]
                t = act.counts(on.scalar.activation(absz, z, ACT.Abs, scale=SCALE))
                act.wait(t)
                t = act.counts(on.scalar.activation(absz, absz, ACT.Exp, scale=-1.0))
                yield
                act.wait(t)
                t = act.counts(on.scalar.activation(absz, absz, ACT.Ln, bias=con("one"), scale=1.0))
                yield
                dve.wait(t, smask_in)
                t1 = dve.counts(on.vector.tensor_scalar(soft, z, SCALE, 0.0, ALU.mult, ALU.max))
                t2 = dve.counts(on.vector.tensor_scalar(lead, z, SCALE, 0.0, ALU.mult, ALU.min))
                free[b] = t2
                dve.wait(t2)
                t1 = dve.counts(on.vector.tensor_tensor(soft, soft, absz, ALU.add))
                t2 = dve.counts(on.vector.tensor_tensor(lead, lead, absz, ALU.subtract))
                dve.wait(t1)
                t = dve.counts(on.vector.tensor_tensor(soft, soft, smask, ALU.mult))
                yield
                pe.wait(t, free[b2])
                mm(bank[b2][:, 0:T], later, soft[:, 0:T], True, True, True)
                mm(bank[b2][:, P:T], ones, soft[:, T:LW], False, True, True)
                done = pe.counts(mm(bank[b2][:, T:LW], later, soft[:, T:LW], False, True, True))
                yield
                dve.wait(done, t2)
                t = dve.counts(on.vector.tensor_tensor(lead, lead, bank[b2][:, 0:LW], ALU.subtract))
                free[b2] = t
                act.wait(t)
                t = act.counts(on.scalar.activation(wt, lead, ACT.Exp))
                yield
                dve.wait(t)
                t = dve.counts(on.vector.tensor_tensor(wt, wt, smask, ALU.mult))
                yield
                pe.wait(t, sv_ready, free[b])
                o = bank[b][rows, 0:T]
                mm(o, V[:, h * HEAD:(h + 1) * HEAD], wt[:, 0:T], True, False, True)
                done = pe.counts(mm(bank[b][rows, P:T], V[:, D + h * HEAD:D + (h + 1) * HEAD], wt[:, T:LW],
                                    False, True, True))
                work_read[slot] = done
                yield
                act.wait(done)
                t = act.counts(on.scalar.copy(merged[rows, block * T:(block + 1) * T], o))
                free[b] = t
                merged_tokens[h] = [t]

            def dilated_head(j, tt, slot):
                rows = slice(HEAD * (j % 2), HEAD * (j % 2) + HEAD)
                lw, pt, small = (slot_work[slot][:, 0:W3], slot_work[slot][:, W3:2 * W3],
                                 slot_work[slot][:, 2 * W3:2 * W3 + 4])
                two = (2 * slot, 2 * slot + 1)
                n_keys = P * (tt + 1)
                width = N_GROUPS * n_keys
                per_bank = min(N_GROUPS, 512 // n_keys)
                pe.wait(free[two[0]], free[two[1]])
                for g in range(N_GROUPS):
                    blk_i = 2 + (GROUP_HEADS * g + j) // 2
                    pe.wait(ready["q", blk_i - 2], ready["k", blk_i - 2])
                    a0 = (g % per_bank) * n_keys
                    ins = mm(bank[two[g // per_bank]][:, a0:a0 + n_keys],
                             Q[rows, blk_i * T + tt * P:blk_i * T + (tt + 1) * P],
                             K[rows, blk_i * T:blk_i * T + n_keys], True, True)
                done = pe.counts(ins)
                yield
                dve.wait(done, bias_ready, work_read[slot])
                off = (j * N_GROUPS * N_LOGIT) + (0 if tt == 0 else N_GROUPS * P)
                for i, a0 in enumerate(range(0, width, per_bank * n_keys)):
                    n_c = min(per_bank * n_keys, width - a0)
                    t = dve.counts(on.vector.scalar_tensor_tensor(
                        lw[:, a0:a0 + n_c], bank[two[i]][:, 0:n_c], SCALE, bias[:, off + a0:off + a0 + n_c],
                        ALU.mult, ALU.add))
                    free[two[i]] = t
                dve.wait(t)
                t = dve.counts(on.vector.tensor_reduce(small[:, 0:1], lw[:, 0:width], AX_X, ALU.max))
                dve.wait(t)
                t = dve.counts(on.vector.tensor_scalar(small[:, 1:2], small[:, 0:1], -1.0, None, ALU.mult))
                yield
                act.wait(t)
                t = act.counts(on.scalar.activation(lw[:, 0:width], lw[:, 0:width], ACT.Exp,
                                                    bias=small[:, 1:2], scale=1.0, accum_out=small[:, 2:3]))
                yield
                dve.wait(t)
                t = dve.counts(on.vector.reciprocal(small[:, 3:4], small[:, 2:3]))
                dve.wait(t)
                t = dve.counts(on.vector.tensor_scalar(lw[:, 0:width], lw[:, 0:width], small[:, 3:4], None,
                                                       ALU.mult))
                yield
                pe.wait(t, free[two[0]], free[two[1]])
                n_piece = N_GROUPS * (tt + 1)
                pieces_done = []
                for p0 in range(0, n_piece, 4):
                    m = min(4, n_piece - p0)
                    for i in range(m):
                        ins = on.tensor.transpose(bank[two[p0 // 4]][:, i * P:(i + 1) * P],
                                                  lw[:, (p0 + i) * P:(p0 + i + 1) * P], ident)
                    pieces_done.append((p0, m, pe.counts(ins)))
                yield
                for p0, m, done in pieces_done:
                    act.wait(done)
                    t = act.counts(on.scalar.copy(pt[:, p0 * P:(p0 + m) * P], bank[two[p0 // 4]][:, 0:m * P]))
                    free[two[p0 // 4]] = t
                yield
                pe.wait(t, dv_ready)
                o = bank[two[0]][rows, 0:P]
                for i in range(n_piece):
                    g, s_tile = i // (tt + 1), i % (tt + 1)
                    head = SB_HEADS + GROUP_HEADS * g + j
                    ins = mm(o, V[:, s_tile * D + head * HEAD:s_tile * D + (head + 1) * HEAD],
                             pt[:, i * P:(i + 1) * P], i == 0, i == n_piece - 1)
                done = pe.counts(ins)
                work_read[slot] = done
                yield
                act.wait(done)
                at = (2 + j // 2) * T + tt * P
                t = act.counts(on.scalar.copy(merged[rows, at:at + P], o))
                free[two[0]] = t
                merged_tokens.setdefault(SB_HEADS + j, []).append(t)

            def step(running, queue, slots):
                for slot in slots:
                    if slot not in running and queue:
                        head, *which = queue.pop(0)
                        running[slot] = head(*which, slot)
                    if slot in running and next(running[slot], "end") == "end":
                        del running[slot]

            squares_read, roots_read = {}, {}
            b, done = project_T("attn_w_in", 0, src_tokens)
            sq_ready = to_sbuf(Q, 0, b, done)
            b, done = project_T("attn_w_in", 1, src_tokens)
            sk_ready = to_sbuf(K, 0, b, done)
            sv_ready = v_unit(2, 0)
            running, queue = {}, [(stick_head, h) for h in range(SB_HEADS)]
            step(running, queue, range(4))
            step(running, queue, range(4))
            to_norm = []

            def norm_waiting():
                for _ in range(min(2, len(to_norm))):
                    name, tile, block, squares, gain = to_norm.pop(0)
                    t = head_norm(tile, block, squares, gain)
                    ready[name, block - 2] = ready[name, block - 1] = t

            for name, tile, first_unit, gain in (("q", Q, 3, "attn_q_norm"), ("k", K, 6, "attn_k_norm")):
                for i in range(3):
                    b, done = project_T("attn_w_in", first_unit + i, src_tokens)
                    t = to_sbuf(tile, 2 + 2 * i, b, done)
                    if running:
                        for _ in range(4):
                            step(running, queue, range(4))
                    else:
                        norm_waiting()
                    to_norm.append((name, tile, 2 + 2 * i, head_squares(tile, 2 + 2 * i, t), gain))
            for i in range(3):
                dv_ready = v_unit(9 + i, 1 + i)
                norm_waiting()
            queue += [(dilated_head, j, tt) for j in range(GROUP_HEADS) for tt in (1, 0)]
            while queue or running:
                step(running, queue, range(4))

            m_tok = []
            for k in range(4):
                for t in merged_tokens[2 * k]:
                    act.wait(t)
                    dve.wait(t)
                m_tok.append(split_block(source, k, blk(merged, k), merged_tokens[2 * k + 1][-1]))
            for u in range(2):
                done = row_product("attn_w_out", u, source, 2 * u, m_tok[2 * u:2 * u + 2], u == 0, u == 1)
            state["source_read"] = done
            return add_residual([done] * 4, 1.0)

        NARROW = 4

        def rwkv(h_tokens):
            A = KT * T
            r, kx, v, ld, a, g = (arena[:, i * A:(i + 1) * A] for i in range(6))
            xx = arena[:, 6 * A:7 * A]
            xm = [arena[:, 7 * A:8 * A], arena[:, 8 * A:9 * A]]
            lora = arena[:, 9 * A:9 * A + 4 * T]
            masks = arena[:, ARENA - 11 * P:ARENA]
            act.wait(pe.now(), dve.now(), act.now(), pool.now())
            masks_in = load_small(act, masks, dram["rwkv_masks"])

            h3 = xn[:, :].rearrange("p (k t) -> p k t", k=KT)
            xx3 = xx.rearrange("p (k t) -> p k t", k=KT)
            dve.wait(*h_tokens)
            dve.wait(pe.now(), act.now())
            t1 = dve.counts(on.vector.tensor_tensor(xx3[:, :, 1:T], h3[:, :, 0:T - 1], h3[:, :, 1:T], ALU.subtract))
            t2 = dve.counts(on.vector.tensor_scalar(xx3[:, :, 0:1], h3[:, :, 0:1], -1.0, None, ALU.mult))
            dve.wait(t1, t2)
            xm_read = [None, None]

            def mixed(which, i):
                dve.wait(xm_read[i])
                return [dve.counts(on.vector.scalar_tensor_tensor(
                    blk(xm[i], k), blk(xx, k), col("rw_mix", which * KT + k), blk(xn, k), ALU.mult, ALU.add))
                    for k in range(KT)]

            def full(name, i, tokens, dst):
                for u in range(4):
                    b, done = project_raw(name, u, xm[i], tokens)
                    act.wait(done)
                    t = act.counts(on.scalar.copy(dst[:, 2 * u * T:(2 * u + 2) * T], bank[b][:, :]))
                    free[b] = t
                xm_read[i] = done
                return t

            tok = mixed(0, 0)
            tok_k = mixed(2, 1)
            r_ready = full("rw_wr", 0, tok, r)
            tok = mixed(3, 0)
            k_ready = full("rw_wk", 1, tok_k, kx)
            tok_w = mixed(1, 1)
            v_ready = full("rw_wv", 0, tok, v)
            tok_a = mixed(4, 0)
            n_in, w_in = take("lora_in", 0, P, 2 * KT * HEAD)
            n_out, w_out = take("lora_out", 0, HEAD, 2 * D)
            lt = {}
            for i, (tokens, src, func) in enumerate(((tok_w, xm[1], ACT.Tanh), (tok_a, xm[0], ACT.Copy))):
                b = next_bank()
                for k in range(KT):
                    pe.wait(tokens[k])
                    ins = mm(bank[b][0:HEAD, 0:T], w_in[:, (i * KT + k) * HEAD:(i * KT + k + 1) * HEAD],
                             blk(src, k), k == 0, k == KT - 1)
                done = pe.counts(ins)
                xm_read[1 - i] = done
                act.wait(done)
                t = act.counts(on.scalar.activation(lora[0:HEAD, i * T:(i + 1) * T], bank[b][0:HEAD, 0:T], func))
                free[b] = t
                lt[i] = t
            give_back(n_in, done)
            tok_g = mixed(5, 1)
            for i, (dst, offset) in enumerate(((ld, "rw_w0"), (a, "rw_a0"))):
                pe.wait(lt[i])
                for c in range(0, KT, 2):
                    b = next_bank()
                    for j in range(2):
                        ins = mm(bank[b][:, j * T:(j + 1) * T],
                                 w_out[:, i * D + (c + j) * P:i * D + (c + j + 1) * P],
                                 lora[0:HEAD, i * T:(i + 1) * T], True, True)
                    done = pe.counts(ins)
                    act.wait(done)
                    for j in range(2):
                        t = act.counts(on.scalar.activation(blk(dst, c + j), bank[b][:, j * T:(j + 1) * T],
                                                            ACT.Sigmoid, bias=col(offset, c + j), scale=1.0))
                    free[b] = t
            give_back(n_out, done)
            da_ready = t
            b, done = project_raw("gate_in", 0, xm[1], tok_g)
            act.wait(done)
            t = act.counts(on.scalar.activation(lora[:, 2 * T:4 * T], bank[b][:, :], ACT.Sigmoid))
            free[b] = t
            n, w = take("gate_out", 0)
            pe.wait(t)
            for c in range(0, KT, 2):
                b = next_bank()
                for j in range(2):
                    for i in range(2):
                        ins = mm(bank[b][:, j * T:(j + 1) * T],
                                 w[:, i * D + (c + j) * P:i * D + (c + j + 1) * P],
                                 lora[:, (2 + i) * T:(3 + i) * T], i == 0, i == 1)
                done = pe.counts(ins)
                act.wait(done)
                t = act.counts(on.scalar.copy(g[:, c * T:(c + 2) * T], bank[b][:, :]))
                free[b] = t
            give_back(n, done)
            g_ready = t

            for e in (pe, dve, act, pool):
                e.wait(pe.now(), dve.now(), act.now(), pool.now(), masks_in)
            y_out = r
            N_MAT = 2 * TT
            slot_cols = (ARENA - 11 * P - 6 * A) // 2
            names = [("sc", 4 * N_MAT * P), ("ar", 2 * T), ("bt", T), ("kt", T), ("KH", T), ("VN", T), ("bonus", T),
                     ("tmp", T), ("Xs", T), ("U", P), ("S", P), ("WC", 4)]
            assert sum(n for _, n in names) <= slot_cols
            final = [None] * KT

            def pair(kt, slot):
                at = 6 * A + slot * slot_cols
                buf = {}
                for name, n in names:
                    buf[name] = arena[:, at:at + n]
                    at += n
                for name, home, offset, n in (("Ti", xn, 0, 2 * T), ("TiT", xn, 2 * T, 2 * T), ("X", sq, 0, 2 * T),
                                              ("BH", sq, 2 * T, T), ("kk", sq, 3 * T, T)):
                    buf[name] = home[:, slot * 4 * T + offset:slot * 4 * T + offset + n]
                cum, grow = (act_buf[:, (2 * slot + i) * T:(2 * slot + i + 1) * T] for i in range(2))
                b0, b1, b2, b3 = (4 * slot + i for i in range(4))
                rT, kT, vT, dT, aT = (blk(z, kt) for z in (r, kx, v, ld, a))
                kk, tmp, bonus = (buf[z] for z in ("kk", "tmp", "bonus"))
                ar = buf["ar"].rearrange("p (s w t) -> p s w t", s=TT, w=2)
                bt, kt_ = buf["bt"], buf["kt"]
                hat = (std, rstd)[slot][:, :]

                def V(ins):
                    t = dve.counts(ins)
                    dve.wait(t)
                    return t

                def halves(z):
                    return z.rearrange("p (s t) -> p s t", s=TT)

                def mats(z):
                    return z.rearrange("p (m t) -> p m t", m=N_MAT)

                V(on.vector.tensor_scalar(kk, kT, col("rw_kk", kt), None, ALU.mult))
                t = V(on.vector.tensor_tensor(tmp, kk, kk, ALU.mult))
                pe.wait(t, free[b0])
                done = pe.counts(mm(bank[b0][:, 0:T], head_ones, tmp, True, True))
                pe.wait(free[b2])
                for s in range(TT):
                    ins = on.tensor.transpose(bank[b2][:, s * P:(s + 1) * P], vT[:, s * P:(s + 1) * P], ident)
                v_done = pe.counts(ins)
                yield
                act.wait(done)
                t_norm = act.counts(on.scalar.activation(hat, bank[b0][:, 0:T], ACT.Sqrt))
                free[b0] = t_norm
                act.wait(v_done)
                t_vn = act.counts(on.scalar.copy(buf["VN"], bank[b2][:, 0:T]))
                free[b2] = t_vn
                V(on.vector.tensor_scalar(dT, dT, DECAY_SCALE, None, ALU.mult))
                V(on.vector.tensor_tensor_scan(cum, con("restart"), dT, 0.0, ALU.mult, ALU.add))
                t = V(on.vector.tensor_tensor(dT, cum, dT, ALU.subtract))
                act.wait(t)
                t_grow = act.counts(on.scalar.activation(grow, cum, ACT.Exp))
                t_prev = act.counts(on.scalar.activation(dT, dT, ACT.Exp))
                t_shrink = act.counts(on.scalar.activation(cum, cum, ACT.Exp, scale=-1.0))
                yield
                dve.wait(t_norm)
                V(on.vector.tensor_scalar(hat, hat, 1e-12, None, ALU.max))
                V(on.vector.reciprocal(hat, hat))
                V(on.vector.tensor_tensor(kk, kk, hat, ALU.mult))
                yield
                V(on.vector.tensor_scalar(tmp, aT, -1.0, col("rw_ka", kt), ALU.add, ALU.mult))
                V(on.vector.scalar_tensor_tensor(kT, tmp, 1.0, kT, ALU.add, ALU.mult))
                V(on.vector.tensor_tensor(aT, kk, aT, ALU.mult))
                t = V(on.vector.scalar_tensor_tensor(tmp, rT, col("rw_rk", kt), kT, ALU.mult, ALU.mult))
                pe.wait(t, free[b1])
                done = pe.counts(mm(bank[b1][:, 0:T], head_ones, tmp, True, True))
                yield
                dve.wait(t_grow, t_prev, t_shrink)
                dve.counts(on.vector.scalar_tensor_tensor(ar[:, :, 0, :], halves(kk), -1.0, halves(dT),
                                                          ALU.mult, ALU.mult))
                dve.counts(on.vector.tensor_tensor(ar[:, :, 1, :], halves(rT), halves(grow), ALU.mult))
                dve.counts(on.vector.tensor_tensor(bt, aT, cum, ALU.mult))
                t_ops = V(on.vector.tensor_tensor(kt_, kT, cum, ALU.mult))
                WC = buf["WC"]
                dve.counts(on.vector.tensor_copy(WC, grow[:, RW_CHUNK - 1:T:RW_CHUNK]))
                dve.wait(done)
                t = V(on.vector.tensor_tensor(bonus, bank[b1][:, 0:T], vT, ALU.mult))
                free[b1] = t
                yield
                sc = buf["sc"].rearrange("p (w m t) -> p w m t", w=4, m=N_MAT)
                for s in range(TT):
                    for p in range(2):
                        m = 2 * s + p
                        rows = slice(p * HEAD, (p + 1) * HEAD)
                        cols = slice(s * P, (s + 1) * P)
                        pe.wait(t_ops, free[(b0, b1)[p]])
                        arr = ar[rows, s, :, :].rearrange("p w t -> p (w t)")
                        mm(bank[(b0, b1)[p]][:, 0:T], bt[rows, cols], arr, True, True)
                        done = pe.counts(mm(bank[(b0, b1)[p]][:, T:2 * T], kt_[rows, cols], arr, True, True))
                        if p == 1:
                            yield
                        dve.wait(done)
                        t = dve.counts(on.vector.tensor_tensor(
                            sc[:, :, m, :], bank[(b0, b1)[p]][:, :].rearrange("p (w t) -> p w t", w=4),
                            masks[:, 0:512].rearrange("p (w t) -> p w t", w=4), ALU.mult))
                        free[(b0, b1)[p]] = t
                dve.wait(t)
                t_sc = t
                MabT, MrbT, MakT, MrkT = (sc[:, i, :, :] for i in range(4))
                Ti, TiT, X = mats(buf["Ti"]), mats(buf["TiT"]), mats(buf["X"])

                def level_mask(i, n=N_MAT):
                    return masks[:, i * P:(i + 1) * P].rearrange("p (o t) -> p o t", o=1).to_broadcast([P, n, P])

                lev_home = ((dT, aT), (kT, cum))
                lev_read = [None, None]

                def make_level(li):
                    pool.wait(t_sc, lev_read[li % 2])
                    for s in range(TT):
                        dst = lev_home[li % 2][s].rearrange("p (h t) -> p h t", h=2)
                        t = pool.counts(nc.gpsimd.tensor_tensor(dst, MabT[:, 2 * s:2 * s + 2, :],
                                                                level_mask(5 + li, 2), ALU.mult))
                    return t

                lev_ready = [make_level(0), make_level(1), None, None, None]
                pe.wait(t_sc, free[b2])
                for m in range(N_MAT):
                    ins = on.tensor.transpose(bank[b2][:, m * P:(m + 1) * P], MabT[:, m, :], ident)
                done = pe.counts(ins)
                id_b = ident.rearrange("p (o t) -> p o t", o=1).to_broadcast([P, N_MAT, P])
                V(on.vector.tensor_tensor(TiT, MabT, level_mask(4), ALU.mult))
                t_tt = V(on.vector.tensor_tensor(TiT, TiT, id_b, ALU.add))
                yield
                dve.wait(done)
                t = V(on.vector.tensor_tensor(Ti, mats(bank[b2][:, :]), level_mask(10), ALU.mult))
                free[b2] = t
                t_t = V(on.vector.tensor_tensor(Ti, Ti, id_b, ALU.add))

                def half_columns(z, size, which):
                    if size < NARROW:
                        return z
                    return z.rearrange("p (q w b) -> p q w b", w=2, b=size)[:, :, which, :]

                def dense(z, size):
                    if size < NARROW:
                        return z
                    return z.rearrange("p (q b) -> p q b", b=size)

                x_cleared = None
                for li, size in enumerate(LEVELS):
                    H = P if size < NARROW else P // 2
                    if size >= NARROW:
                        pool.wait(done_t, done_tt)
                        x_cleared = pool.counts(nc.gpsimd.memset(buf["X"], 0.0))
                    pe.wait(t_t, t_tt, lev_ready[li], free[b2])
                    for m in range(N_MAT):
                        lev = lev_home[li % 2][m // 2][:, (m % 2) * P:(m % 2 + 1) * P]
                        ins = mm(dense(bank[b2][:, m * H:(m + 1) * H], size), lev,
                                 half_columns(Ti[:, m, :], size, 0), True, True)
                    done = pe.counts(ins)
                    lev_read[li % 2] = done
                    if li + 2 < len(LEVELS):
                        lev_ready[li + 2] = make_level(li + 2)
                    yield
                    act.wait(done, x_cleared)
                    t_x = act.counts(on.scalar.copy(half_columns(buf["X"], size, 0),
                                                    dense(bank[b2][:, 0:N_MAT * H], size)))
                    free[b2] = t_x
                    pe.wait(t_x, free[b1])
                    for m in range(N_MAT):
                        ins = mm(dense(bank[b1][:, m * H:(m + 1) * H], size), X[:, m, :],
                                 half_columns(TiT[:, m, :], size, 1), True, True)
                    done_tt = pe.counts(ins)
                    last = li == len(LEVELS) - 1
                    if not last:
                        pe.wait(free[b0])
                        for m in range(N_MAT):
                            ins = mm(dense(bank[b0][:, m * H:(m + 1) * H], size), TiT[:, m, :],
                                     half_columns(X[:, m, :], size, 0), True, True)
                        done_t = pe.counts(ins)
                    else:
                        done_t = done_tt
                    yield
                    dve.wait(done_t, done_tt)
                    piece = half_columns(buf["TiT"], size, 1)
                    t_tt = dve.counts(on.vector.tensor_tensor(piece, piece, dense(bank[b1][:, 0:N_MAT * H], size),
                                                              ALU.add))
                    free[b1] = t_tt
                    if not last:
                        piece = half_columns(buf["Ti"], size, 0)
                        t_t = dve.counts(on.vector.tensor_tensor(piece, piece,
                                                                 dense(bank[b0][:, 0:N_MAT * H], size), ALU.add))
                        free[b0] = t_t
                    dve.wait(t_tt, t_t)
                VN = halves(buf["VN"])
                Xs, U, S = halves(buf["Xs"]), buf["U"], buf["S"]
                pe.wait(t_vn, free[b2])
                for m in range(N_MAT):
                    ins = mm(bank[b2][:, m * HEAD:(m + 1) * HEAD], MakT[:, m, :],
                             VN[:, m // 2, (m % 2) * HEAD:(m % 2 + 1) * HEAD], True, True)
                done = pe.counts(ins)
                wc_b = WC.rearrange("p (c o) -> p c o", o=1).to_broadcast([P, T // RW_CHUNK, RW_CHUNK])
                t_S = V(on.vector.memset(S, 0.0))
                for src, dst in ((bt, "BH"), (kt_, "KH")):
                    t = V(on.vector.tensor_tensor(hat.rearrange("p (c t) -> p c t", t=RW_CHUNK),
                                                  src.rearrange("p (c t) -> p c t", t=RW_CHUNK), wc_b, ALU.mult))
                    pe.wait(t, free[b0])
                    for s in range(TT):
                        ins = on.tensor.transpose(bank[b0][:, s * P:(s + 1) * P], hat[:, s * P:(s + 1) * P], ident)
                    done_h = pe.counts(ins)
                    yield
                    if dst == "BH":
                        act.wait(done)
                        t_xs = act.counts(on.scalar.copy(buf["Xs"], bank[b2][:, 0:T]))
                        free[b2] = t_xs
                    act.wait(done_h)
                    t_nat = act.counts(on.scalar.copy(buf[dst], bank[b0][:, 0:T]))
                    free[b0] = t_nat
                    dve.wait(done_h)
                yv = tmp
                for s in range(TT):
                    cols = slice(s * P, (s + 1) * P)
                    pe.wait(free[b3])
                    for c in range(2):
                        rc = slice(c * RW_CHUNK, (c + 1) * RW_CHUNK)
                        pe.wait(t_S, free[b2])
                        done = pe.counts(mm(bank[b2][:, 0:P], ar[:, s, 0, :], S, True, True))
                        ins = mm(bank[b3][:, rc], S, ar[:, s, 1, rc], c == 0, True, True)
                        yield
                        dve.wait(done, t_xs)
                        t = dve.counts(on.vector.tensor_tensor(Xs[rc, s, :], bank[b2][rc, 0:P], Xs[rc, s, :],
                                                               ALU.add))
                        free[b2] = t
                        pe.wait(t, t_tt, free[b1])
                        for h in range(2):
                            ins = mm(bank[b1][:, h * HEAD:(h + 1) * HEAD], TiT[:, 2 * s + h, :],
                                     Xs[:, s, h * HEAD:(h + 1) * HEAD], True, True)
                        done_u = pe.counts(ins)
                        yield
                        act.wait(done_u)
                        t_u = act.counts(on.scalar.copy(U[rc, :], bank[b1][rc, 0:P]))
                        free[b1] = t_u
                        pe.wait(t_nat, free[b2])
                        mm(bank[b2][:, 0:P], buf["KH"][rc, cols], VN[rc, s, :], True, False)
                        pe.wait(t_u)
                        done = pe.counts(mm(bank[b2][:, 0:P], buf["BH"][rc, cols], U[rc, :], False, True))
                        yield
                        dve.wait(done)
                        for h in range(2):
                            hs = slice(h * HEAD, (h + 1) * HEAD)
                            t_S = dve.counts(on.vector.scalar_tensor_tensor(
                                S[hs, hs], S[hs, hs], WC[hs, 2 * s + c:2 * s + c + 1], bank[b2][hs, hs],
                                ALU.mult, ALU.add))
                        free[b2] = t_S
                        dve.wait(t_S)
                    for h in range(2):
                        hs = slice(h * HEAD, (h + 1) * HEAD)
                        mm(bank[b3][hs, 0:P], U[:, hs], MrbT[:, 2 * s + h, :], False, True, True)
                        done = mm(bank[b3][hs, 0:P], VN[:, s, hs], MrkT[:, 2 * s + h, :], False, True, True)
                    done = pe.counts(done)
                    act.wait(done)
                    t_y = act.counts(on.scalar.copy(yv[:, cols], bank[b3][:, 0:P]))
                    free[b3] = t_y
                pe.wait(t_y, free[b0])
                done = pe.counts(mm(bank[b0][:, 0:T], head_ones, yv, True, True))
                yield
                dve.wait(done, t_y)
                t = V(on.vector.scalar_tensor_tensor(yv, bank[b0][:, 0:T], -1.0 / HEAD, yv, ALU.mult, ALU.add))
                free[b0] = t
                t = V(on.vector.tensor_tensor(kk, yv, yv, ALU.mult))
                pe.wait(t, free[b1])
                done = pe.counts(mm(bank[b1][:, 0:T], head_ones, kk, True, True))
                yield
                act.wait(done)
                t = act.counts(on.scalar.activation(hat, bank[b1][:, 0:T], ACT.Sqrt, bias=con("eps_gn"),
                                                    scale=1.0 / HEAD))
                free[b1] = t
                yield
                dve.wait(t)
                V(on.vector.reciprocal(hat, hat))
                V(on.vector.scalar_tensor_tensor(yv, yv, col("rw_lnx_g", kt), hat, ALU.mult, ALU.mult))
                V(on.vector.scalar_tensor_tensor(yv, yv, col("rw_lnx_b", kt), bonus, ALU.add, ALU.add))
                final[kt] = V(on.vector.tensor_tensor(blk(y_out, kt), yv, blk(g, kt), ALU.mult))

            queue = list(range(KT))
            running = {}
            while queue or running:
                for slot in range(2):
                    if slot not in running and queue:
                        running[slot] = pair(queue.pop(0), slot)
                    if slot in running and next(running[slot], "end") == "end":
                        del running[slot]
            act.wait(pe.now(), dve.now(), act.now(), pool.now())
            tokens = []
            for u in range(4):
                b, done = project_raw("rw_wo", u, y_out, final)
                for j in range(2):
                    dve.wait(done)
                    t = dve.counts(on.vector.tensor_tensor(blk(x, 2 * u + j), blk(x, 2 * u + j),
                                                           bank[b][:, j * T:(j + 1) * T], ALU.add))
                    tokens.append(t)
                free[b] = t
            return tokens

        TAPS = P
        TE_TAPS = 13
        taps_home = arena[:, ARENA - 4 * TE_TAPS * TAPS:ARENA]
        taps_ready = [None]

        def make_tap_matrices(layer):
            pool.wait(pe.now(), dve.now(), act.now())
            for i in range(4 * TE_TAPS):
                g, j = i // TE_TAPS, i % TE_TAPS
                taps_ready[0] = pool.counts(nc.gpsimd.tensor_scalar(
                    blk(taps_home, i, TAPS), ident, col("conv_w_2", (layer * CONV_WIDTH + j) * 4 + g), None,
                    ALU.mult))

        def pool_conv_mixer(layer, x_tokens):
            A = KT * T
            UP = T + PAD_POOL
            VP = T + PAD_CONV
            at = [0]

            def piece(n):
                at[0] += n
                return arena[:, at[0] - n:at[0]]

            up, s_a, s_b = piece(4 * UP), piece(4 * UP), piece(4 * UP)
            vp, val = piece(4 * VP), piece(4 * T)
            y = piece(4 * T)
            cat = piece(A)
            inv = piece(4 * T)
            dd = piece(4 * T)
            z = piece(A)
            gate = piece(4 * T)
            act.wait(pe.now(), dve.now(), act.now(), pool.now())
            inv_in = load_small(act, inv, dram["inverse_count"])
            up3, a3, b3 = (q.rearrange("p (g t) -> p g t", g=4) for q in (up, s_a, s_b))
            vp3 = vp.rearrange("p (g t) -> p g t", g=4)
            pool.wait(pe.now(), dve.now(), act.now())
            for q in (up3, a3, b3):
                zeroed = pool.counts(nc.gpsimd.memset(q[:, :, 0:PAD_POOL], 0.0))
            zeroed = pool.counts(nc.gpsimd.memset(vp3[:, :, 0:PAD_CONV], 0.0))
            w_in = "w_in_2"
            for u in range(2):
                b, done = project_T(w_in, 6 * layer + 2 + u, x_tokens)
                act.wait(done)
                t_val = act.counts(on.scalar.copy(val[:, 2 * u * T:(2 * u + 2) * T], bank[b][:, :]))
                free[b] = t_val
            v_tok = []
            for u in range(2):
                b, done = project_T(w_in, 6 * layer + 4 + u, x_tokens)
                act.wait(done)
                t = act.counts(on.scalar.activation(gate[:, 2 * u * T:(2 * u + 2) * T], bank[b][:, :], ACT.Sigmoid))
                free[b] = t
                dve.wait(t, t_val)
                for j in range(2):
                    g = 2 * u + j
                    v_tok.append(dve.counts(on.vector.tensor_tensor(vp3[:, g, PAD_CONV:VP], blk(val, g), blk(gate, g),
                                                                    ALU.mult)))
            for u in range(2):
                b, done = project_T(w_in, 6 * layer + u, x_tokens)
                act.wait(done, zeroed)
                t = act.counts(on.scalar.copy(up3[:, 2 * u:2 * u + 2, PAD_POOL:UP],
                                              bank[b][:, :].rearrange("p (g t) -> p g t", g=2)))
                free[b] = t
            pool.wait(t)
            cur, nxt = up3, a3
            spare = {0: a3, 1: b3, 2: a3, 3: b3}
            for i, w in enumerate(POOL_WINDOWS):
                half = w // 2
                dst = spare[i]
                t = pool.counts(nc.gpsimd.tensor_tensor(dst[:, i:4, PAD_POOL:UP], cur[:, i:4, PAD_POOL:UP],
                                                        cur[:, i:4, PAD_POOL - half:UP - half], ALU.add))
                pool.wait(t)
                cur = dst
            dd3, inv3 = (q.rearrange("p (g t) -> p g t", g=4) for q in (dd, inv))
            pool.wait(inv_in)
            for i in range(4):
                t = pool.counts(nc.gpsimd.tensor_tensor(dd3[:, i, :], spare[i][:, i, PAD_POOL:UP], inv3[:, i, :],
                                                        ALU.mult))
            pool.wait(t)
            t = pool.counts(nc.gpsimd.tensor_tensor(dd3, dd3, up3[:, :, PAD_POOL:UP], ALU.subtract))
            y_tok = []
            conv_banks = [next_bank(), next_bank()]
            pe.wait(taps_ready[0], zeroed)
            tap_done = []
            for g in range(4):
                pe.wait(v_tok[g])
                for j in range(TE_TAPS):
                    ins = mm(bank[conv_banks[g // 2]][:, (g % 2) * T:(g % 2 + 1) * T],
                             blk(taps_home, g * TE_TAPS + j, TAPS), vp3[:, g, j:j + T],
                             j == 0, j == TE_TAPS - 1)
                tap_done.append(pe.counts(ins))
            for g in range(4):
                dve.wait(v_tok[g], zeroed)
                for j in range(TE_TAPS, CONV_WIDTH):
                    wcol = col("conv_w_2", (layer * CONV_WIDTH + j) * 4 + g)
                    tap = vp3[:, g, j:j + T]
                    if j == TE_TAPS:
                        q = dve.counts(on.vector.tensor_scalar(blk(y, g), tap, wcol, col("conv_b_2", layer * 4 + g),
                                                               ALU.mult, ALU.add))
                    else:
                        q = dve.counts(on.vector.scalar_tensor_tensor(blk(y, g), tap, wcol, blk(y, g), ALU.mult,
                                                                      ALU.add))
                    dve.wait(q)
                dve.wait(tap_done[g // 2 * 2 + 1])
                q = dve.counts(on.vector.tensor_tensor(blk(y, g), blk(y, g),
                                                       bank[conv_banks[g // 2]][:, (g % 2) * T:(g % 2 + 1) * T],
                                                       ALU.add))
                free[conv_banks[g // 2]] = q
                y_tok.append(q)
            n, w = take("pool_w_2", layer, P, 4 * P)
            cat_tok = [None] * KT
            pe.wait(t)
            for u in range(2):
                b = next_bank()
                for j in range(2):
                    g = 2 * u + j
                    ins = mm(bank[b][:, j * T:(j + 1) * T], w[:, g * P:(g + 1) * P], blk(dd, g), True, True)
                done = pe.counts(ins)
                act.wait(done)
                for j in range(2):
                    g = 2 * u + j
                    t = act.counts(on.scalar.activation(blk(cat, g), bank[b][:, j * T:(j + 1) * T], ACT.Copy,
                                                        scale=col("pool_scale_2", layer * 4 + g)))
                    cat_tok[g] = split_block(source, g, blk(cat, g), t)
                free[b] = t
            give_back(n, done)

            def finish(g):
                t = dve.counts(on.vector.scalar_tensor_tensor(blk(y, g), blk(y, g),
                                                              col("conv_ln_g_2", layer * 4 + g), rstd[:, :],
                                                              ALU.mult, ALU.mult))
                act.wait(t)
                t = act.counts(on.scalar.activation(blk(y, g), blk(y, g), ACT.Silu,
                                                    bias=col("conv_ln_b_2", layer * 4 + g), scale=1.0))
                return split_block(source, 4 + g, blk(y, g), t)

            y_tok = layer_norm(y, y_tok, 4, finish)
            bs = [next_bank(), next_bank()]
            for half in range(2):
                w = take_half("conv_pw_2", layer, half)
                for c in range(4):
                    for k2 in range(2):
                        k = 2 * half + k2
                        pe.wait(y_tok[k])
                        at = k2 * 512 + c * P
                        ins = mm3(bank[bs[c // 2]][:, (c % 2) * T:(c % 2 + 1) * T], w, slice(at, at + P), source,
                                  slice((4 + k) * T, (5 + k) * T), k == 0 and c % 2 == 0, k == 3, True)
                done = half_read(ins)
            state["source_read"] = done
            for u in range(2):
                t = split_block(source, 2 + u, bank[bs[u]][:, :], done, 2 * T)
                cat_tok[4 + 2 * u] = cat_tok[5 + 2 * u] = free[bs[u]] = t
            z_tok = []
            for u in range(4):
                b, done = project_T("w_out_2", 4 * layer + u, cat_tok)
                dve.wait(done)
                for j in range(2):
                    c = 2 * u + j
                    z_tok.append(dve.counts(on.vector.scalar_tensor_tensor(
                        blk(z, c), blk(x, c), ALPHA, bank[b][:, j * T:(j + 1) * T], ALU.mult, ALU.add)))
                free[b] = z_tok[-1]
            return z, z_tok

        def norm_to_x(z, z_tok, gain, bias, layer, split=True):
            def finish(k):
                t = dve.counts(on.vector.scalar_tensor_tensor(blk(z, k), blk(z, k), col(gain, layer * KT + k),
                                                              rstd[:, :], ALU.mult, ALU.mult))
                act.wait(t)
                return act.counts(on.scalar.activation(blk(x, k), blk(z, k), ACT.Identity,
                                                       bias=col(bias, layer * KT + k), scale=1.0))
            tokens = layer_norm(z, z_tok, KT, finish)
            return split_x(tokens) if split else tokens

        def split_x(tokens):
            return [split_block(source, k, blk(x, k), tokens[k]) for k in range(KT)]

        def deep_residual(done, z):
            z_tok = []
            for c in range(KT):
                dve.wait(done[c // 2])
                z_tok.append(dve.counts(on.vector.scalar_tensor_tensor(
                    blk(z, c), blk(x, c), ALPHA, bank[c // 2][:, (c % 2) * T:(c % 2 + 1) * T], ALU.mult, ALU.add)))
                free[c // 2] = z_tok[-1]
            return z_tok

        E = N_EXPERTS

        def moe(x_tokens, z):
            A = KT * T
            small = arena[:, 4096:4096 + 2 * 64]
            table = arena[:, 4224:4224 + 8 * 16]
            chosen, gates, place = (table[:, i * 16:(i + 1) * 16] for i in range(3))
            most = table[:, 48:49]
            earlier, ramp = arena[:, 6 * A:6 * A + P], arena[:, 6 * A + P:6 * A + 2 * P]
            act.wait(pe.now(), dve.now(), act.now(), pool.now())
            load_small(act, arena[:, 6 * A:6 * A + 2 * P], dram["moe_tables"])
            rows = arena[0:E, 0:E * P]
            rows_in = load_small(act, rows, dram["expert_rows"])
            at = PARAM_AT["router_w_2"]
            iota = con("iota")
            b = next_bank()
            for tt in range(TT):
                for k in range(KT):
                    pe.wait(x_tokens[k])
                    ins = mm(bank[b][:, tt * E:(tt + 1) * E], x[:, k * T + tt * P:k * T + (tt + 1) * P],
                             param[:, at + k * E:at + (k + 1) * E], k == 0, k == KT - 1)
            done = pe.counts(ins)
            dve.wait(done, pe.now(), act.now())
            for tt in range(TT):
                s = small[:, tt * 64:(tt + 1) * 64]
                lg, eq, o1, o2 = (s[:, i * 8:(i + 1) * 8] for i in range(4))
                m1, m2, i1, dif, w1, w2 = (s[:, 32 + i:33 + i] for i in range(6))
                here = slice(tt * E, (tt + 1) * E)

                def V(ins):
                    t = dve.counts(ins)
                    dve.wait(t)
                    return t

                V(on.vector.tensor_copy(lg, bank[b][:, here]))
                for m, hot in ((m1, o1), (m2, o2)):
                    V(on.vector.tensor_reduce(m, lg, AX_X, ALU.max))
                    V(on.vector.tensor_scalar(eq, lg, m, 1e9, ALU.is_lt, ALU.mult))
                    V(on.vector.tensor_tensor(eq, eq, iota, ALU.add))
                    V(on.vector.tensor_reduce(i1, eq, AX_X, ALU.min))
                    V(on.vector.tensor_scalar(hot, iota, i1, None, ALU.is_equal))
                    V(on.vector.scalar_tensor_tensor(lg, hot, -3e38, lg, ALU.mult, ALU.add))
                t = V(on.vector.tensor_tensor(dif, m2, m1, ALU.subtract))
                act.wait(t)
                t = act.counts(on.scalar.activation(w2, dif, ACT.Exp))
                dve.wait(t)
                V(on.vector.tensor_scalar(w1, w2, 1.0, None, ALU.add))
                V(on.vector.reciprocal(w1, w1))
                V(on.vector.tensor_tensor(w2, w2, w1, ALU.mult))
                V(on.vector.tensor_tensor(chosen[:, here], o1, o2, ALU.add))
                V(on.vector.tensor_scalar(o1, o1, w1, None, ALU.mult))
                t = V(on.vector.scalar_tensor_tensor(gates[:, here], o2, w2, o1, ALU.mult, ALU.add))
            free[b] = t
            b = next_bank()
            pe.wait(t, rows_in)
            first, second = chosen[:, 0:E], chosen[:, E:2 * E]
            mm(bank[b][:, 0:E], earlier, first, True, True)
            mm(bank[b][:, E:2 * E], ones, first, True, False)
            mm(bank[b][:, E:2 * E], earlier, second, False, True)
            mm(bank[b][:, 2 * E:3 * E], ones, first, True, False)
            done = pe.counts(mm(bank[b][:, 2 * E:3 * E], ones, second, False, True))
            dve.wait(done)
            dve.counts(on.vector.tensor_copy(place, bank[b][:, 0:2 * E]))
            t = dve.counts(on.vector.tensor_reduce(most, bank[b][:, 2 * E:3 * E], AX_X, ALU.max))
            free[b] = t
            dve.wait(t)
            t = dve.counts(on.vector.tensor_scalar(crowded[:, :], most, float(tile_limit), None, ALU.is_gt))

            def shared_state():
                return (dict(position), list(free), list(h_read), list(dve_read_act), dict(state), turn[0])

            def set_state(saved):
                position.update(saved[0])
                free[:], h_read[:], dve_read_act[:] = saved[1], saved[2], saved[3]
                state.update(saved[4])
                turn[0] = saved[5]

            before = shared_state()
            branching = (pe, dve, act)
            waited = []
            for e in branching:
                e.wait(t, rows_in)
                waited.append(dict(e.waited))
            real = (nc.tensor, nc.vector, nc.scalar)
            ends = []
            for kept in range(3):
                flag = real[kept].value_load(crowded[0:1, 0:1], min_val=0, max_val=1)
                handles = [real[i] if i == kept else Silent() for i in range(3)]
                on.tensor, on.vector, on.scalar = handles
                for way, body in enumerate((experts_on_all, experts_on_their_own)):
                    with real[kept].If(flag) if way == 0 else real[kept].Else():
                        for e, h, w, s in zip(branching, handles, waited, way_done[way]):
                            e.handle = h
                            e.count_on(s, w)
                        set_state(before)
                        body(x_tokens, z, chosen, gates, place, ramp, rows)
                        dve.wait(pe.now(), act.now(), dve.now())
                        on.vector.memset(most, 0.0).then_inc(moe_done, 1)
                        ends.append(dict(position))
            assert all(end == ends[0] for end in ends)
            on.tensor, on.vector, on.scalar = real
            for e, h in zip(branching, real):
                e.handle = h
            for e, w, s in zip(branching, waited, after_done):
                e.count_on(s, w)
            set_state((ends[0], [None] * 8, [None] * 2, [None] * 4, {"sq_read": None, "source_read": None}, 0))
            for e in branching + (pool,):
                e.wait((moe_done, 1))
            return moe_done, 1

        crowded = ctx.enter_context(nc.sbuf_tensor("crowded", [P, 1], mybir.dt.int32))
        way_done = [[sem(f"{w}_{e}") for e in ("pe", "dve", "act")] for w in ("all", "own")]
        after_done = [sem(f"after_{e}") for e in ("pe", "dve", "act")]
        moe_done = sem("moe_done")
        exp_names = ("exp_w1_2", "exp_w3_2", "exp_w2_2")
        EXP_UNITS = D_FF_EXPERT // CHUNK

        def experts_on_all(x_tokens, z, chosen, gates, place, ramp, rows):
            gT = arena[0:E, 1024:1024 + T]
            wide = arena[:, 1280:1280 + E * T]
            b = next_bank()
            for tt in range(TT):
                done = pe.counts(on.tensor.transpose(bank[b][0:E, tt * P:(tt + 1) * P], gates[:, tt * E:(tt + 1) * E],
                                                     ident))
            act.wait(done)
            t = act.counts(on.scalar.copy(gT, bank[b][0:E, 0:T]))
            free[b] = t
            for e in range(0, E, 2):
                b = next_bank()
                pe.wait(t)
                for j in range(2):
                    ins = mm(bank[b][:, j * T:(j + 1) * T], rows[:, (e + j) * P:(e + j + 1) * P], gT, True, True)
                done = pe.counts(ins)
                act.wait(done)
                t2 = act.counts(on.scalar.copy(wide[:, e * T:(e + 2) * T], bank[b][:, :]))
                free[b] = t2
            dve.wait(t2)
            tokens = split_x(x_tokens)
            done = gated_ffn(tokens, exp_names, 0, E * EXP_UNITS, lambda i: blk(wide, i // EXP_UNITS))
            deep_residual(done, z)

        def experts_on_their_own(x_tokens, z, chosen, gates, place, ramp, rows):
            A = KT * T
            x_nat = arena[:, 3 * A:4 * A]
            pick = [arena[:, 4 * A + i * T:4 * A + (i + 1) * T] for i in range(2)]
            pick_g = [arena[:, 4 * A + (2 + i) * T:4 * A + (3 + i) * T] for i in range(2)]
            back = [arena[:, 4 * A + (4 + i) * T:4 * A + (5 + i) * T] for i in range(2)]
            y_own = [arena[:, 5 * A + i * D:5 * A + (i + 1) * D] for i in range(2)]
            spare = [0]

            def spare_bank():
                spare[0] += 1
                i = 6 + spare[0] % 2
                pe.wait(free[i])
                return i

            for tt in range(TT):
                for half in range(2):
                    b = spare_bank()
                    for i in range(4):
                        k = 4 * half + i
                        ins = on.tensor.transpose(bank[b][:, i * P:(i + 1) * P],
                                                  x[:, k * T + tt * P:k * T + (tt + 1) * P], ident)
                    done = pe.counts(ins)
                    act.wait(done)
                    x_ready = act.counts(on.scalar.copy(x_nat[:, tt * D + half * 512:tt * D + (half + 1) * 512],
                                                        bank[b][:, :]))
                    free[b] = x_ready
            z_ready = dve.counts(on.vector.tensor_scalar(z, x[:, :], ALPHA, None, ALU.mult))
            gathered, back_ready = {}, {}
            own_read = [None, None]
            back_read = [None, None]
            y_read = [None, None]

            def gather(e):
                q = e % 2
                dve.wait(own_read[q], back_read[q], x_ready)
                for tt in range(TT):
                    at = slice(tt * P, (tt + 1) * P)
                    c = slice(tt * E + e, tt * E + e + 1)
                    dve.counts(on.vector.tensor_scalar(pick[q][:, at], ramp, place[:, c], chosen[:, c], ALU.is_equal,
                                                       ALU.mult))
                    t = dve.counts(on.vector.tensor_scalar(pick_g[q][:, at], ramp, place[:, c], gates[:, c],
                                                           ALU.is_equal, ALU.mult))
                pe.wait(t, x_ready)
                for half in range(2):
                    b = spare_bank()
                    for k4 in range(4):
                        for tt in range(TT):
                            k = 4 * half + k4
                            ins = mm(bank[b][:, k4 * P:(k4 + 1) * P], x_nat[:, tt * D + k * P:tt * D + (k + 1) * P],
                                     pick[q][:, tt * P:(tt + 1) * P], tt == 0, tt == 1)
                    done = pe.counts(ins)
                    act.wait(own_read[q])
                    t = split_block(source, 2 * q + half, bank[b][:, :], done, 2 * T)
                    free[b] = t
                    gathered[e, half] = t
                b = spare_bank()
                for tt in range(TT):
                    ins = on.tensor.transpose(bank[b][:, tt * P:(tt + 1) * P], pick_g[q][:, tt * P:(tt + 1) * P], ident)
                done = pe.counts(ins)
                act.wait(done)
                back_ready[e] = act.counts(on.scalar.copy(back[q], bank[b][:, 0:T]))
                free[b] = back_ready[e]

            def gate_or_up(e, i, part, name, b):
                for s in range(2):
                    w = take_half(name, e * EXP_UNITS + i, s)
                    pe.wait(gathered[e, s])
                    for k4 in range(KT // 2):
                        k = s * KT // 2 + k4
                        at = (e % 2) * KT * P + k * P
                        ins = mm3(bank[b][:, part * T:(part + 1) * T], w, slice(k4 * CHUNK, (k4 + 1) * CHUNK),
                                  source, slice(at, at + P), k == 0, k == KT - 1, False, True)
                    done = half_read(ins)
                return done

            def turn_hidden(j, t):
                pe.wait(t)
                b = spare_bank()
                for i in range(2):
                    ins = on.tensor.transpose(bank[b][:, i * P:(i + 1) * P], act_buf[:, j * T + i * P:j * T + (i + 1) * P],
                                              ident)
                done = pe.counts(ins)
                act.wait(h_read[j])
                t = split_block(hidden, j, bank[b][:, 0:T], done)
                free[b] = t
                return done, t

            def down_own(e, i, j, h_ready):
                y0 = 2 * (e % 2)
                for s in range(2):
                    w = take_half(exp_names[2], e * EXP_UNITS + i, s)
                    pe.wait(h_ready)
                    for n in range(2):
                        if i == 0 and s == 0:
                            pe.wait(free[y0 + n])
                        at = j * T + s * P
                        ins = mm3(bank[y0 + n][:, :], w, slice(n * 512, (n + 1) * 512), hidden, slice(at, at + P),
                                  i == 0 and s == 0, i == EXP_UNITS - 1 and s == 1, True, True)
                    done = half_read(ins)
                h_read[j] = done
                if i == EXP_UNITS - 1:
                    q = e % 2
                    act.wait(done, y_read[q])
                    for n in range(2):
                        t = act.counts(on.scalar.copy(y_own[q][:, n * 512:(n + 1) * 512], bank[y0 + n][:, :]))
                        free[y0 + n] = t
                    return t

            def scatter(e, y_ready):
                q = e % 2
                pe.wait(y_ready, back_ready[e])
                for u in range(4):
                    b = spare_bank()
                    for j in range(2):
                        c = 2 * u + j
                        ins = mm(bank[b][:, j * T:(j + 1) * T], y_own[q][:, c * P:(c + 1) * P], back[q], True, True)
                    done = pe.counts(ins)
                    dve.wait(done, z_ready if e == 0 else z_last[u])
                    piece = z[:, 2 * u * T:(2 * u + 2) * T]
                    z_last[u] = dve.counts(on.vector.tensor_tensor(piece, piece, bank[b][:, :], ALU.add))
                    free[b] = z_last[u]
                y_read[q] = back_read[q] = done

            z_last = [None] * 4
            gather(0)
            previous = None
            y_ready = {}
            buf_read = [None, None]
            for e in range(E):
                for i in range(EXP_UNITS):
                    n = e * EXP_UNITS + i
                    j = n % 2
                    b = 4 + j
                    pe.wait(free[b])
                    gate_or_up(e, i, 0, exp_names[0], b)
                    if previous is not None:
                        buf_read[1 - j], h_ready = turn_hidden(1 - j, previous[2])
                    done = gate_or_up(e, i, 1, exp_names[1], b)
                    own_read[e % 2] = done
                    act.wait(done, buf_read[j])
                    piece = blk(act_buf, j)
                    t = act.counts(on.scalar.activation(piece, bank[b][:, 0:T], ACT.Silu))
                    dve.wait(t)
                    t = dve.counts(on.vector.tensor_tensor(piece, piece, bank[b][:, T:2 * T], ALU.mult))
                    free[b] = t
                    if previous is not None:
                        pe_, pi, _ = previous
                        y_ready[pe_] = down_own(pe_, pi, 1 - j, h_ready)
                    previous = (e, i, t)
                    if i == 2 and e > 0:
                        scatter(e - 1, y_ready[e - 1])
                    if i == EXP_UNITS - 6 and e < E - 1:
                        gather(e + 1)
            buf_read[j], h_ready = turn_hidden(j, previous[2])
            scatter(E - 1, down_own(E - 1, EXP_UNITS - 1, j, h_ready))

        def per_layer_gate(layer, x_tokens):
            A = KT * T
            pT, gate, prod = arena[:, 0:2 * T], arena[:, A:2 * A], arena[:, 2 * A:3 * A]
            act.wait(pe.now(), dve.now(), act.now(), pool.now())
            p_in = load_small(act, pT, dram["p_2"][layer])
            act.wait(h_read[0], h_read[1])
            p_tok = [split_block(hidden, i, blk(pT, i), p_in) for i in range(2)]
            p_done = row_product("ple_w_2", layer, hidden, 0, p_tok, True, True)
            h_read[0] = p_done
            prods = []
            for u in range(4):
                b, done = project_T("ple_gate_w_2", 4 * layer + u, x_tokens)
                act.wait(done)
                t = act.counts(on.scalar.activation(gate[:, 2 * u * T:(2 * u + 2) * T], bank[b][:, :], ACT.Sigmoid))
                free[b] = t
                dve.wait(t, p_done)
                t = dve.counts(on.vector.tensor_tensor(prod[:, 2 * u * T:(2 * u + 2) * T],
                                                       gate[:, 2 * u * T:(2 * u + 2) * T], bank[u][:, :], ALU.mult))
                free[u] = t
            dve.wait(t, pe.now())
            return [dve.counts(on.vector.tensor_tensor(blk(x, k), blk(x, k), blk(prod, k), ALU.add))
                    for k in range(KT)]

        def store(x_tokens):
            nat = arena[:, 0:TT * D]
            act.wait(pe.now(), dve.now(), act.now(), pool.now())
            for tt in range(TT):
                for half in range(2):
                    b = next_bank()
                    for i in range(4):
                        k = 4 * half + i
                        pe.wait(x_tokens[k])
                        ins = on.tensor.transpose(bank[b][:, i * P:(i + 1) * P],
                                                  x[:, k * T + tt * P:k * T + (tt + 1) * P], ident)
                    done = pe.counts(ins)
                    act.wait(done)
                    t = act.counts(on.scalar.copy(nat[:, tt * D + half * 512:tt * D + (half + 1) * 512],
                                                  bank[b][:, :]))
                    free[b] = t
            act.wait(t)
            on.scalar.dma_start(out.rearrange("(s p) d -> p s d", p=P),
                                nat.rearrange("p (s d) -> p s d", s=TT)).then_inc(out_written, 16)
            act.wait((out_written, 16))

        names1 = ("ffn_w_gate", "ffn_w_up", "ffn_w_down")
        FFN_UNITS = D_FF // CHUNK

        def half_ffn(which, tokens):
            n_tok, norm = rms_norm_late(tokens, "ffn_norm", which * KT)
            done = gated_ffn(n_tok, names1, which * FFN_UNITS, FFN_UNITS, late_norm=norm)
            return add_residual(done, 0.5)

        def network():
            tokens = [x_in] * KT
            tokens = half_ffn(0, tokens)
            n_tok = rms_norm(tokens, "mix_norm", 0)
            tokens = attention(n_tok, tokens)
            tokens = half_ffn(1, tokens)
            tokens = half_ffn(2, tokens)
            n_tok = rms_norm(tokens, "mix_norm", KT, False)
            tokens = rwkv(n_tok)
            make_tap_matrices(0)
            tokens = split_x(half_ffn(3, tokens))
            for layer in range(2):
                z, z_tok = pool_conv_mixer(layer, tokens)
                tokens = norm_to_x(z, z_tok, "ln1_g_2", "ln1_b_2", layer, layer == 0)
                at = (7 + layer) * KT * T
                z = arena[:, at:at + KT * T]
                if layer == 0:
                    make_tap_matrices(1)
                    done = gated_ffn(tokens, ("dense_w1_2", "dense_w3_2", "dense_w2_2"), 0, FFN_UNITS)
                    z_tok = deep_residual(done, z)
                else:
                    z_tok = [moe(tokens, z)] * KT
                tokens = norm_to_x(z, z_tok, "ln2_g_2", "ln2_b_2", layer)
                tokens = per_layer_gate(layer, tokens)
                if layer == 0:
                    tokens = split_x(tokens)
            return tokens

        store(network())

        for n in range(max(position["unit"], halves[position["split"] - 1][0] + 1)):
            name, i, _ = stream[n]
            if n >= RAW_SLOTS:
                sp.wait(raw_read[n - RAW_SLOTS])
            elif n == 1:
                sp.wait(x_in)
            src = dram[name][i]
            rows, cols = src.shape
            at = (n % RAW_SLOTS) * UNIT
            nc.sync.dma_start(raw[0:rows, at:at + cols], src).then_inc(slot_landed[n % RAW_SLOTS], 16)


def column_units(w):
    w = np.asarray(w)
    w = w.reshape(-1, KT, P, w.shape[-1] // CHUNK, CHUNK)
    return np.ascontiguousarray(w.transpose(0, 3, 2, 1, 4)).reshape(-1, P, UNIT)


def row_units(w):
    w = np.asarray(w).reshape(-1, 2, P, D)
    return np.ascontiguousarray(w.transpose(0, 2, 1, 3)).reshape(-1, P, UNIT)


def token_T(a):
    f = a.shape[-1]
    return np.ascontiguousarray(a.reshape(T, f // P, P).transpose(2, 1, 0)).reshape(P, f // P * T)


def lay_out(inp):
    d = dict(constant_arrays())
    d["x"] = token_T(inp["x"].reshape(T, D))
    d["p_2"] = np.stack([token_T(inp["p_2"][i].reshape(T, -1)) for i in range(2)])
    cols = []
    for name, n in PARAMS:
        a = np.asarray(inp[name])
        if name in ("attn_q_norm", "attn_k_norm"):
            c = np.concatenate([a.reshape(HEAD, 1)] * 2, axis=0)
        elif name == "router_w_2":
            c = a.reshape(KT, P, N_EXPERTS).transpose(1, 0, 2).reshape(P, -1)
        else:
            c = a.reshape(n, P).T
        cols.append(c)
    d["params"] = np.ascontiguousarray(np.concatenate(cols, axis=1))
    for name in ("ffn_w_gate", "ffn_w_up", "attn_w_in", "rw_wr", "rw_wk", "rw_wv", "rw_wo", "w_in_2", "w_out_2",
                 "dense_w1_2", "dense_w3_2", "exp_w1_2", "exp_w3_2", "ple_gate_w_2"):
        d[name] = column_units(inp[name])
    for name in ("ffn_w_down", "attn_w_out", "dense_w2_2", "exp_w2_2", "ple_w_2"):
        d[name] = row_units(inp[name])
    k_tiles = lambda w: np.asarray(w).reshape(KT, P, -1).transpose(1, 0, 2).reshape(P, -1)
    d["lora_in"] = np.concatenate([k_tiles(inp["rw_w1"]), k_tiles(inp["rw_a1"])], axis=1)[None]
    d["lora_out"] = np.concatenate([inp["rw_w2"][0], inp["rw_a2"][0]], axis=1)[None]
    g1 = np.asarray(inp["rw_g1"][0])
    d["gate_in"] = column_units(np.pad(g1, ((0, 0), (0, CHUNK - g1.shape[1]))))
    g2 = np.asarray(inp["rw_g2"][0])
    d["gate_out"] = row_units(np.pad(g2, ((0, CHUNK - g2.shape[0]), (0, 0))))
    d["pool_w_2"] = np.ascontiguousarray(np.asarray(inp["pool_w_2"]).transpose(0, 2, 1, 3)).reshape(2, P, 4 * P)
    d["conv_pw_2"] = np.ascontiguousarray(
        np.asarray(inp["conv_pw_2"]).reshape(2, 4, P, 512).transpose(0, 2, 1, 3)).reshape(2, P, UNIT)
    bucket = bucket_of_distance()
    table = np.asarray(inp["rel_bias"])
    rows = []
    for j in range(GROUP_HEADS):
        for tile in range(TT):
            dist = tile * P + np.arange(P)[:, None] - np.arange(P * (tile + 1))[None, :]
            at = bucket[np.maximum(dist, 0)]
            for g in range(N_GROUPS):
                rows.append(table[:, GROUP_HEADS * g + j][at])
    d["rel_bias"] = np.concatenate(rows, axis=1)
    return {k: np.ascontiguousarray(v) for k, v in d.items()}


def kernel(**inputs):
    import concourse.bacc as bacc
    from concourse.bass_utils import run_bass_kernel_spmd

    arrays = lay_out({k: np.asarray(v) for k, v in inputs.items()})
    nc = bacc.Bacc("TRN2", target_bir_lowering=False, num_devices=1)
    dram = {name: nc.dram_tensor(f"in_{name}", a.shape, mybir.dt.from_np(a.dtype), kind="ExternalInput").ap()
            for name, a in arrays.items()}
    out = nc.dram_tensor("out", (T, D), F32, kind="ExternalOutput").ap()
    bass_macaron_attention_rwkv_conv_moe_kernel(nc, dram, out)
    result = run_bass_kernel_spmd(nc, [{f"in_{name}": a for name, a in arrays.items()}], core_ids=[0])
    return result.results[0]["out"].reshape(1, T, D)
```
